# Optimizing a Trainium2 kernel written in Bass

```python
import math
import jax, jax.numpy as jnp
from jax import lax
import numpy as np

D_MODEL = 1024
BATCH = 1
SEQ = 256
DEPTH = 2

GDN_HEADS = 8
GDN_DK = 128
GDN_DV = 128
GDN_QK = GDN_HEADS * GDN_DK
GDN_WIDTH = GDN_HEADS * GDN_DV
GDN_CONV_CH = 2 * GDN_QK + GDN_WIDTH
CONV_WIDTH = 5
CHUNK = 64
DIFF_HEADS = 8
DIFF_DH = 64
DIFF_DV = 2 * DIFF_DH
DIFF_QK = DIFF_HEADS * 2 * DIFF_DH
DIFF_WIDTH = DIFF_HEADS * DIFF_DV
Q_BLOCK = 128
ROPE_THETA = 500000.0
ROPE_DIM = DIFF_DH // 4
EPS = 1e-6

_SEG = (GDN_QK, GDN_QK, GDN_WIDTH, 4 * GDN_HEADS, GDN_WIDTH,
        DIFF_QK, DIFF_QK, DIFF_WIDTH, DIFF_WIDTH, D_MODEL, D_MODEL)
N_IN = sum(_SEG)
SPLIT_IDX = tuple(sum(_SEG[:i + 1]) for i in range(len(_SEG) - 1))


def rmsnorm(x, w):
    xf = x.astype(jnp.float32)
    y = xf * lax.rsqrt(jnp.mean(xf * xf, axis=-1, keepdims=True) + EPS)
    return y.astype(x.dtype) * w

def l2norm(x):
    return x * lax.rsqrt(jnp.sum(x * x, axis=-1, keepdims=True) + EPS)

def short_conv(x, w):
    pad = CONV_WIDTH // 2
    return lax.conv_general_dilated(
        x, w[:, None, :].astype(x.dtype), window_strides=(1,), padding=[(pad, pad)],
        dimension_numbers=("NWC", "WIO", "NWC"), feature_group_count=x.shape[-1])

def chunk_gated_delta(q, k, v, g, beta):
    f32 = jnp.float32
    q, k, v, g, beta = (t.astype(f32) for t in (q, k, v, g, beta))
    bsz, nh, seq, dk = k.shape
    dv = v.shape[-1]
    nc = seq // CHUNK
    q = q * dk ** -0.5
    kb = k * beta[..., None]
    vb = v * beta[..., None]
    rs = lambda t: t.reshape(bsz, nh, nc, CHUNK, t.shape[-1])
    q, k, kb, vb = rs(q), rs(k), rs(kb), rs(vb)
    g = jnp.cumsum(g.reshape(bsz, nh, nc, CHUNK), axis=-1)
    lower = jnp.tril(jnp.ones((CHUNK, CHUNK), dtype=bool))
    strict = jnp.tril(jnp.ones((CHUNK, CHUNK), dtype=bool), -1)
    gdiff = g[..., :, None] - g[..., None, :]
    decay = jnp.where(lower, jnp.exp(jnp.where(lower, gdiff, 0.0)), 0.0)
    L = jnp.where(strict, jnp.einsum('bhncd,bhnmd->bhncm', kb, k) * decay, 0.0)
    eye = jnp.eye(CHUNK, dtype=f32)
    T = lax.linalg.triangular_solve(eye + L, jnp.broadcast_to(eye, L.shape),
                                    left_side=True, lower=True, unit_diagonal=True)
    u = jnp.einsum('bhncm,bhnme->bhnce', T, vb)
    w = jnp.einsum('bhncm,bhnmd->bhncd', T, kb * jnp.exp(g)[..., None])
    qk = jnp.where(lower, jnp.einsum('bhncd,bhnmd->bhncm', q, k) * decay, 0.0)

    def step(state, inp):
        q_c, k_c, u_c, w_c, g_c, qk_c = inp
        v_new = u_c - jnp.einsum('bhcd,bhde->bhce', w_c, state)
        o = (jnp.einsum('bhcd,bhde->bhce', q_c * jnp.exp(g_c)[..., None], state)
             + jnp.einsum('bhcm,bhme->bhce', qk_c, v_new))
        g_last = g_c[..., -1]
        state = (state * jnp.exp(g_last)[..., None, None]
                 + jnp.einsum('bhcd,bhce->bhde', k_c * jnp.exp(g_last[..., None] - g_c)[..., None], v_new))
        return state, o

    xs = tuple(jnp.moveaxis(t, 2, 0) for t in (q, k, u, w, g, qk))
    state0 = jnp.zeros((bsz, nh, dk, dv), f32)
    _, o = lax.scan(step, state0, xs)
    return jnp.moveaxis(o, 0, 2).reshape(bsz, nh, seq, dv)

def gated_delta_branch(q, k, v, ab, z, conv_w, a_log, dt_bias, norm_w):
    bsz, seq, _ = q.shape
    f32 = jnp.float32
    qkv = jax.nn.silu(short_conv(jnp.concatenate([q, k, v], axis=-1), conv_w))
    q, k, v = jnp.split(qkv, (GDN_QK, 2 * GDN_QK), axis=-1)
    heads = lambda t, d: t.reshape(bsz, seq, GDN_HEADS, d).transpose(0, 2, 1, 3).astype(f32)
    q = l2norm(heads(q, GDN_DK))
    k = l2norm(heads(k, GDN_DK))
    v = heads(v, GDN_DV)
    ab = ab.reshape(bsz, seq, 4, GDN_HEADS).transpose(2, 0, 3, 1).astype(f32)
    beta = jax.nn.sigmoid(ab[:2])
    g = (-jnp.exp(a_log.astype(f32))[:, None, :, None]
         * jax.nn.softplus(ab[2:] + dt_bias.astype(f32)[:, None, :, None]))
    o_fwd = chunk_gated_delta(q, k, v, g[0], beta[0])
    flip = lambda t: jnp.flip(t, axis=2)
    o_bwd = flip(chunk_gated_delta(flip(q), flip(k), flip(v), flip(g[1]), flip(beta[1])))
    o = rmsnorm(o_fwd + o_bwd, norm_w.astype(f32))
    o = o.transpose(0, 2, 1, 3).reshape(bsz, seq, GDN_WIDTH).astype(z.dtype)
    return o * jax.nn.silu(z)

def partial_rope(t, cos, sin):
    half = ROPE_DIM // 2
    c = cos[:, :, None, None, :].astype(t.dtype)
    s = sin[:, :, None, None, :].astype(t.dtype)
    x1 = t[..., :half]
    x2 = t[..., half:ROPE_DIM]
    return jnp.concatenate([x1 * c - x2 * s, x2 * c + x1 * s, t[..., ROPE_DIM:]], axis=-1)

def diff_attention_branch(q, k, v, z, cos, sin, lam_params, subln_w, lambda_init):
    bsz, seq, _ = q.shape
    f32 = jnp.float32
    q = partial_rope(q.reshape(bsz, seq, DIFF_HEADS, 2, DIFF_DH), cos, sin) * (DIFF_DH ** -0.5)
    k = partial_rope(k.reshape(bsz, seq, DIFF_HEADS, 2, DIFF_DH), cos, sin)
    q = q.transpose(3, 0, 2, 1, 4)
    k = k.transpose(3, 0, 2, 1, 4)
    v = v.reshape(bsz, seq, DIFF_HEADS, DIFF_DV).transpose(0, 2, 1, 3)
    lp = lam_params.astype(f32)
    lam = jnp.exp(jnp.sum(lp[0] * lp[1])) - jnp.exp(jnp.sum(lp[2] * lp[3])) + lambda_init
    n_blk = seq // Q_BLOCK
    qb = q.reshape(2, bsz, DIFF_HEADS, n_blk, Q_BLOCK, DIFF_DH).transpose(3, 0, 1, 2, 4, 5)

    def attend(q_blk):
        s = jnp.einsum('nbhqd,nbhkd->nbhqk', q_blk, k).astype(f32)
        p = jax.nn.softmax(s, axis=-1)
        a = p[0] - lam * p[1]
        return jnp.einsum('bhqk,bhkd->bhqd', a.astype(v.dtype), v)

    o = lax.map(attend, qb)
    o = o.transpose(1, 2, 0, 3, 4).reshape(bsz, DIFF_HEADS, seq, DIFF_DV)
    o = rmsnorm(o, subln_w) * (1.0 - lambda_init)
    o = o.transpose(0, 2, 1, 3).reshape(bsz, seq, DIFF_WIDTH)
    return o * jax.nn.silu(z)

def first_inputs(seed: int = 0) -> dict:
    key = jax.random.key(seed)
    ks = jax.random.split(key, 16)
    f32 = jnp.float32
    x = jax.random.normal(ks[0], (BATCH, SEQ, D_MODEL), f32)
    positions = (jnp.arange(SEQ, dtype=jnp.int32)[None, :]
                 + jax.random.randint(ks[1], (BATCH, 1), 0, 4096, dtype=jnp.int32))
    norm_w = 1.0 + 0.02 * jax.random.normal(ks[2], (DEPTH, D_MODEL), f32)
    w_in = jax.random.normal(ks[3], (DEPTH, D_MODEL, N_IN), f32) * D_MODEL ** -0.5
    conv_w = jax.random.normal(ks[4], (DEPTH, CONV_WIDTH, GDN_CONV_CH), f32) * CONV_WIDTH ** -0.5
    a_log = jnp.log(jax.random.uniform(ks[5], (DEPTH, 2, GDN_HEADS), f32, 1.0, 16.0))
    dt = jnp.exp(jax.random.uniform(ks[6], (DEPTH, 2, GDN_HEADS), f32, math.log(1e-3), math.log(1e-1)))
    dt_bias = dt + jnp.log(-jnp.expm1(-dt))
    gdn_norm_w = 1.0 + 0.02 * jax.random.normal(ks[7], (DEPTH, GDN_DV), f32)
    diff_lambda = 0.1 * jax.random.normal(ks[8], (DEPTH, 4, DIFF_DH), f32)
    diff_subln_w = 1.0 + 0.02 * jax.random.normal(ks[9], (DEPTH, DIFF_DV), f32)
    w_pa = jax.random.normal(ks[10], (DEPTH, GDN_WIDTH, D_MODEL), f32) * GDN_WIDTH ** -0.5
    w_pb = jax.random.normal(ks[11], (DEPTH, DIFF_WIDTH, D_MODEL), f32) * DIFF_WIDTH ** -0.5
    w_out = jax.random.normal(ks[12], (DEPTH, D_MODEL, D_MODEL), f32) * D_MODEL ** -0.5
    final_norm_w = 1.0 + 0.02 * jax.random.normal(ks[13], (D_MODEL,), f32)
    return {"x": x, "positions": positions, "norm_w": norm_w, "w_in": w_in, "conv_w": conv_w,
            "a_log": a_log, "dt_bias": dt_bias, "gdn_norm_w": gdn_norm_w,
            "diff_lambda": diff_lambda, "diff_subln_w": diff_subln_w, "w_pa": w_pa,
            "w_pb": w_pb, "w_out": w_out, "final_norm_w": final_norm_w}

def first_block(x, positions, norm_w, w_in, conv_w, a_log, dt_bias, gdn_norm_w,
              diff_lambda, diff_subln_w, w_pa, w_pb, w_out, final_norm_w):
    inv_freq = ROPE_THETA ** (-(jnp.arange(0, ROPE_DIM, 2, dtype=jnp.float32) / ROPE_DIM))
    angles = positions.astype(jnp.float32)[..., None] * inv_freq
    cos, sin = jnp.cos(angles), jnp.sin(angles)
    for l in range(DEPTH):
        h = rmsnorm(x, norm_w[l])
        proj = h @ w_in[l]
        (q_a, k_a, v_a, ab_a, z_a, q_b, k_b, v_b, z_b,
         gate_a, gate_b) = jnp.split(proj, SPLIT_IDX, axis=-1)
        y_a = gated_delta_branch(q_a, k_a, v_a, ab_a, z_a, conv_w[l], a_log[l], dt_bias[l], gdn_norm_w[l])
        lambda_init = 0.8 - 0.6 * math.exp(-0.3 * l)
        y_b = diff_attention_branch(q_b, k_b, v_b, z_b, cos, sin, diff_lambda[l], diff_subln_w[l], lambda_init)
        merged = (jax.nn.sigmoid(gate_a) * (y_a @ w_pa[l])
                  + jax.nn.sigmoid(gate_b) * (y_b @ w_pb[l]))
        x = x + merged @ w_out[l]
    return rmsnorm(x, final_norm_w)


DEPTH_2 = 1

MIX_WIDTH = D_MODEL
POOL_WIDTH = MIX_WIDTH // 2
POOL_WINDOWS = (2, 4, 8, 16)
N_POOL_GROUPS = len(POOL_WINDOWS)
POOL_GROUP_DIM = POOL_WIDTH // N_POOL_GROUPS
ATTN_WIDTH = MIX_WIDTH - POOL_WIDTH
HEAD_DIM = 64
N_ATTN_HEADS = ATTN_WIDTH // HEAD_DIM
DILATED_BRANCHES = ((128, 1), (512, 4), (2048, 16))
ATTN_BLOCK = 128
IN_WIDTH = POOL_WIDTH + 3 * ATTN_WIDTH
N_REL_BUCKETS = 32
REL_MAX_EXACT = N_REL_BUCKETS // 2
REL_MAX_DISTANCE = 2048
N_EXPERTS = 32
TOP_K = 4
D_EXPERT = D_MODEL
SWIGLU_LIMIT = 7.0
SWIGLU_ALPHA = 1.702
MOE_BLOCK = 128
PLE_DIM = 256
NORM_EPS = 1e-6
NEG_INF = -1e30


def rmsnorm_2(x, g):
    xf = x.astype(jnp.float32)
    y = xf * lax.rsqrt(jnp.mean(xf * xf, axis=-1, keepdims=True) + NORM_EPS)
    return (y * g.astype(jnp.float32)).astype(x.dtype)

def pool_mixer(u, w_pool, pool_scale):
    B, S, _ = u.shape
    ug = u.reshape(B, S, N_POOL_GROUPS, POOL_GROUP_DIM)
    t = jnp.arange(S)
    outs = []
    for gi, w in enumerate(POOL_WINDOWS):
        ch = ug[:, :, gi].astype(jnp.float32)
        cs = jnp.cumsum(ch, axis=1)
        prev = jnp.pad(cs, ((0, 0), (w, 0), (0, 0)))[:, :S]
        cnt = jnp.minimum(t + 1, w).astype(jnp.float32)[None, :, None]
        outs.append(((cs - prev) / cnt - ch).astype(u.dtype))
    pooled = jnp.stack(outs, axis=2)
    mixed = jnp.einsum('bsgc,gcd->bsgd', pooled, w_pool)
    return mixed.reshape(B, S, POOL_WIDTH) * pool_scale

def t5_bucket(dist):
    n = jnp.maximum(dist, 1).astype(jnp.float32)
    large = REL_MAX_EXACT + (jnp.log(n / REL_MAX_EXACT) / math.log(REL_MAX_DISTANCE / REL_MAX_EXACT)
                             * (N_REL_BUCKETS - REL_MAX_EXACT)).astype(jnp.int32)
    large = jnp.minimum(large, N_REL_BUCKETS - 1)
    return jnp.where(dist < REL_MAX_EXACT, dist, large)

def dilated_branch(q, k, v, rel_bias, window, dil):
    B, S, H, Dh = q.shape
    w_sub = window // dil
    blk = ATTN_BLOCK
    span = dil * blk
    Sp = -(-S // span) * span
    L = Sp // dil
    nb = L // blk

    def to_sub(t):
        t = jnp.pad(t, ((0, 0), (0, Sp - S), (0, 0), (0, 0)))
        t = t.reshape(B, nb, blk, dil, H, Dh)
        return t.transpose(0, 3, 4, 1, 2, 5)

    qs, ks, vs = to_sub(q), to_sub(k), to_sub(v)
    shift = lambda t: jnp.concatenate([jnp.zeros_like(t[:, :, :, :1]), t[:, :, :, :-1]], axis=3)
    keys = jnp.concatenate([shift(ks), ks], axis=4)
    vals = jnp.concatenate([shift(vs), vs], axis=4)

    s = jnp.einsum('brhnqc,brhnkc->brhnqk', qs, keys).astype(jnp.float32) * (1.0 / math.sqrt(Dh))
    qi = jnp.arange(blk)[:, None]
    ki = jnp.arange(2 * blk)[None, :]
    rel = blk + qi - ki
    bias = rel_bias[t5_bucket(jnp.maximum(rel, 0) * dil)]
    s = s + bias.transpose(2, 0, 1)[:, None].astype(jnp.float32)
    band = (rel >= 0) & (rel <= w_sub)
    first_ok = (jnp.arange(nb)[:, None, None] > 0) | (ki[None] >= blk)
    mask = band[None] & first_ok
    s = jnp.where(mask, s, NEG_INF)
    m = jnp.max(s, axis=-1)
    e = jnp.exp(s - m[..., None])
    l = jnp.sum(e, axis=-1)
    o = jnp.einsum('brhnqk,brhnkc->brhnqc', e, vals.astype(jnp.float32)) / l[..., None]
    lse = m + jnp.log(l)
    o = o.transpose(0, 3, 4, 1, 2, 5).reshape(B, Sp, H, Dh)[:, :S]
    lse = lse.transpose(0, 3, 4, 1, 2).reshape(B, Sp, H)[:, :S]
    return o, lse

def dilated_attention(q, k, v, rel_bias):
    outs, lses = [], []
    for window, dil in DILATED_BRANCHES:
        o, lse = dilated_branch(q, k, v, rel_bias, window, dil)
        outs.append(o)
        lses.append(lse)
    w = jax.nn.softmax(jnp.stack(lses, axis=0), axis=0)
    out = jnp.sum(w[..., None] * jnp.stack(outs, axis=0), axis=0)
    return out.astype(q.dtype)

def moe(h, w_router, b_router, w_gate_up, b_gate_up, w_down, b_down):
    B, S, D = h.shape
    T = B * S
    hf = h.reshape(T, D)
    logits = (hf @ w_router + b_router).astype(jnp.float32)
    topv, topi = lax.top_k(logits, TOP_K)
    gates = jax.nn.softmax(topv, axis=-1)

    expert_ids = topi.reshape(-1)
    token_ids = jnp.repeat(jnp.arange(T), TOP_K)
    gate_flat = gates.reshape(-1)
    order = jnp.argsort(expert_ids)
    sorted_e = expert_ids[order]
    group_sizes = jnp.bincount(expert_ids, length=N_EXPERTS)
    group_starts = jnp.cumsum(group_sizes) - group_sizes
    padded_sizes = (group_sizes + MOE_BLOCK - 1) // MOE_BLOCK * MOE_BLOCK
    padded_ends = jnp.cumsum(padded_sizes)
    padded_starts = padded_ends - padded_sizes
    rank = jnp.arange(T * TOP_K) - group_starts[sorted_e]
    dest = padded_starts[sorted_e] + rank

    n_rows = T * TOP_K + N_EXPERTS * MOE_BLOCK
    n_blocks = n_rows // MOE_BLOCK
    row_token = jnp.zeros((n_rows,), jnp.int32).at[dest].set(token_ids[order])
    row_gate = jnp.zeros((n_rows,), h.dtype).at[dest].set(gate_flat[order].astype(h.dtype))
    block_expert = jnp.minimum(
        jnp.searchsorted(padded_ends, jnp.arange(n_blocks) * MOE_BLOCK, side='right'),
        N_EXPERTS - 1)
    xs = hf[row_token].reshape(n_blocks, MOE_BLOCK, D)

    def expert_block(args):
        xb, e = args
        gu = xb @ w_gate_up[e] + b_gate_up[e]
        g, u = gu[:, :D_EXPERT], gu[:, D_EXPERT:]
        g = jnp.minimum(g, SWIGLU_LIMIT)
        u = jnp.clip(u, -SWIGLU_LIMIT, SWIGLU_LIMIT)
        glu = g * jax.nn.sigmoid(SWIGLU_ALPHA * g)
        return ((u + 1.0) * glu) @ w_down[e] + b_down[e]

    ys = lax.map(expert_block, (xs, block_expert)).reshape(n_rows, D)
    out = jnp.zeros((T, D), h.dtype).at[row_token].add(ys * row_gate[:, None])
    return out.reshape(B, S, D)

def second_inputs(seed: int = 0) -> dict:
    key = jax.random.key(seed)
    ks = jax.random.split(key, 24)
    f32 = jnp.float32
    nrm = lambda k, shape, s: jax.random.normal(k, shape, f32) * s
    gain = lambda k, shape: 1.0 + 0.05 * jax.random.normal(k, shape, f32)
    return {
        "x": nrm(ks[0], (BATCH, SEQ, D_MODEL), 1.0),
        "p": nrm(ks[1], (DEPTH_2, BATCH, SEQ, PLE_DIM), 1.0),
        "g_mix": gain(ks[2], (DEPTH_2, D_MODEL)),
        "w_in": nrm(ks[3], (DEPTH_2, D_MODEL, IN_WIDTH), D_MODEL ** -0.5),
        "w_pool": nrm(ks[4], (DEPTH_2, N_POOL_GROUPS, POOL_GROUP_DIM, POOL_GROUP_DIM), POOL_GROUP_DIM ** -0.5),
        "pool_scale": gain(ks[5], (DEPTH_2, POOL_WIDTH)),
        "rel_bias": nrm(ks[6], (N_REL_BUCKETS, N_ATTN_HEADS), 0.5),
        "w_out": nrm(ks[7], (DEPTH_2, MIX_WIDTH, D_MODEL), MIX_WIDTH ** -0.5),
        "g_ffn": gain(ks[8], (DEPTH_2, D_MODEL)),
        "w_router": nrm(ks[9], (DEPTH_2, D_MODEL, N_EXPERTS), D_MODEL ** -0.5),
        "b_router": nrm(ks[10], (DEPTH_2, N_EXPERTS), 0.01),
        "w_gate_up": nrm(ks[11], (DEPTH_2, N_EXPERTS, D_MODEL, 2 * D_EXPERT), D_MODEL ** -0.5),
        "b_gate_up": nrm(ks[12], (DEPTH_2, N_EXPERTS, 2 * D_EXPERT), 0.01),
        "w_down": nrm(ks[13], (DEPTH_2, N_EXPERTS, D_EXPERT, D_MODEL), D_EXPERT ** -0.5),
        "b_down": nrm(ks[14], (DEPTH_2, N_EXPERTS, D_MODEL), 0.01),
        "g_ple": gain(ks[15], (DEPTH_2, D_MODEL)),
        "w_ple_gate": nrm(ks[16], (DEPTH_2, D_MODEL, D_MODEL), D_MODEL ** -0.5),
        "w_ple_proj": nrm(ks[17], (DEPTH_2, PLE_DIM, D_MODEL), PLE_DIM ** -0.5),
        "g_final": gain(ks[18], (D_MODEL,)),
    }

def second_block(x, p, g_mix, w_in, w_pool, pool_scale, rel_bias, w_out, g_ffn,
              w_router, b_router, w_gate_up, b_gate_up, w_down, b_down,
              g_ple, w_ple_gate, w_ple_proj, g_final):
    B, S, _ = x.shape
    for i in range(DEPTH_2):
        h = rmsnorm_2(x, g_mix[i])
        z = jnp.einsum('bsd,de->bse', h, w_in[i])
        u = z[..., :POOL_WIDTH]
        qkv = z[..., POOL_WIDTH:].reshape(B, S, 3, N_ATTN_HEADS, HEAD_DIM)
        q, k, v = qkv[:, :, 0], qkv[:, :, 1], qkv[:, :, 2]
        a_out = pool_mixer(u, w_pool[i], pool_scale[i])
        b_out = dilated_attention(q, k, v, rel_bias).reshape(B, S, ATTN_WIDTH)
        mix = jnp.concatenate([a_out, b_out], axis=-1)
        x = x + jnp.einsum('bse,ed->bsd', mix, w_out[i])
        x = x + moe(rmsnorm_2(x, g_ffn[i]), w_router[i], b_router[i], w_gate_up[i],
                    b_gate_up[i], w_down[i], b_down[i])
        gate = jax.nn.sigmoid(jnp.einsum('bsd,de->bse', rmsnorm_2(x, g_ple[i]), w_ple_gate[i]))
        x = x + jnp.einsum('bsp,pd->bsd', p[i], w_ple_proj[i]) * gate
    return rmsnorm_2(x, g_final)


def setup_inputs(seed=0):
    out = dict(first_inputs(seed))
    for name, value in second_inputs(seed + 1).items():
        if name != "x":
            out[name + "_2"] = value
    return out


def reference(
    x, positions, norm_w, w_in, conv_w, a_log, dt_bias, gdn_norm_w, diff_lambda, diff_subln_w,
    w_pa, w_pb, w_out, final_norm_w, p_2, g_mix_2, w_in_2, w_pool_2, pool_scale_2, rel_bias_2,
    w_out_2, g_ffn_2, w_router_2, b_router_2, w_gate_up_2, b_gate_up_2, w_down_2, b_down_2,
    g_ple_2, w_ple_gate_2, w_ple_proj_2, g_final_2,
):
    x = first_block(
        x, positions, norm_w, w_in, conv_w, a_log, dt_bias, gdn_norm_w, diff_lambda,
        diff_subln_w, w_pa, w_pb, w_out, final_norm_w,
    )
    return second_block(
        x, p_2, g_mix_2, w_in_2, w_pool_2, pool_scale_2, rel_bias_2, w_out_2, g_ffn_2,
        w_router_2, b_router_2, w_gate_up_2, b_gate_up_2, w_down_2, b_down_2, g_ple_2,
        w_ple_gate_2, w_ple_proj_2, g_final_2,
    )


_drawn_inputs = setup_inputs


def setup_inputs(seed=0):
    import zlib

    import numpy as np

    out = dict(_drawn_inputs(seed))
    spreads = {}
    factors = {'diff_subln_w': 3.834,
     'b_router_2': 2.678,
     'b_gate_up_2': 8.0,
     'b_down_2': 8.0,
     'g_ple_2': 7.592}
    for name, (base, spread) in spreads.items():
        noise = np.random.default_rng([zlib.crc32(name.encode()), seed]).standard_normal(out[name].shape)
        drawn = base * np.exp(spread * noise) if base else spread * noise
        out[name] = __import__('jax').numpy.asarray(drawn.astype(out[name].dtype))
    for name, factor in factors.items():
        out[name] = (out[name] * factor).astype(out[name].dtype)
    return out
```

```python
import math
from contextlib import ExitStack

import numpy as np
import concourse.bass as bass
from concourse import mybir

F32 = mybir.dt.float32
I32 = mybir.dt.int32
ALU = mybir.AluOpType
ACT = mybir.ActivationFunctionType
AXX = mybir.AxisListType.X

P = 128
S = 256
NT = S // P
D = 1024
KC = D // P
DEPTH = 2
H = 8
NB = 512
CH = 3 * D
CB = CH // P
TAPS = 5
PAD = TAPS // 2
AB = 3 * D
Z_A = AB + 4 * H
Q_B = Z_A + D
Z_B = Q_B + 3 * D
GATES = Z_B + D
LEVELS = 7
EPS = 1e-6
NE = 32
TOPK = 4
CAP = 64
ROUNDS = S // CAP
SLOTS = 6
ROPE_HALF = 8
NEG = -1e30
DIFF_SCALE = 64 ** -0.5

C_ID, C_TRI, C_STRICT, C_IOTA, C_LVL = 0, 128, 384, 512, 640
C_MISC = C_LVL + LEVELS * 2 * P
C_N = C_MISC + 12

V_NORM, V_MIX, V_FFN, V_PLE, V_POOL, V_N = 0, 16, 24, 32, 40, 44

GDN_STEPS = 16
DIFF_STEPS = 6
DIL_STEPS = 5
LAYER_STEPS = 34
MERGE_STEPS = 48


def shape_constants():
    j = np.arange(P)[:, None]
    i = np.arange(P)[None, :]
    c = np.zeros((P, C_N), np.float32)
    c[:, C_ID:C_ID + P] = j == i
    c[:, C_TRI:C_TRI + P] = j <= i
    c[:, C_TRI + P:C_TRI + 2 * P] = j >= i
    c[:, C_STRICT:C_STRICT + P] = j < i
    c[:, C_IOTA:C_IOTA + P] = i % CAP
    for n in range(LEVELS):
        s = 1 << n
        m = ((j // s) % 2 == 0) & ((i // s) % 2 == 1) & (i // (2 * s) == j // (2 * s))
        c[:, C_LVL + (2 * n) * P:C_LVL + (2 * n + 1) * P] = m
        c[:, C_LVL + (2 * n + 1) * P:C_LVL + (2 * n + 2) * P] = m.T
    inv = np.float64(500000.0) ** (-(np.arange(0, 2 * ROPE_HALF, 2) / (2.0 * ROPE_HALF)))
    c[:, C_MISC:C_MISC + ROPE_HALF] = inv.astype(np.float32)
    for l in range(DEPTH):
        lam = 0.8 - 0.6 * math.exp(-0.3 * l)
        c[:, C_MISC + 8 + l] = lam
        c[:, C_MISC + 10 + l] = 1.0 - lam
    band = np.zeros((S, 4, S), np.float32)
    for g, w in enumerate((2, 4, 8, 16)):
        for t in range(S):
            band[max(0, t - w + 1):t + 1, g, t] = np.float32(1.0) / np.float32(min(t + 1, w))
            band[t, g, t] -= 1.0
    q = np.arange(S)[:, None]
    k = np.arange(S)[None, :]
    d = q - k
    count = ((d >= 0) & (d <= 128)).astype(np.float32) + ((d >= 0) & (d % 4 == 0)) + ((d >= 0) & (d % 16 == 0))
    oh = np.zeros((33, 512), np.float32)
    for m in range(512):
        dist = 255 - m
        if dist < 0 or (dist > 128 and dist % 4):
            oh[32, m] = NEG
            continue
        b = dist if dist < 16 else min(31, 16 + int(math.log(dist / 16) / math.log(2048 / 16) * 16))
        oh[b, m] = 1.0
    return {"c_main": c, "c_band": band.reshape(S, 4 * S), "c_count": count.astype(np.float32), "c_bucket": oh}


def block_kernel(nc, a, out):
    ctx = ExitStack()
    with ctx:
        def sb(name, shape, dt=F32):
            return ctx.enter_context(nc.sbuf_tensor(name, shape, dt))

        sems = {}

        def s(name):
            if name not in sems:
                sems[name] = ctx.enter_context(nc.semaphore(name))
            return sems[name]

        ONCE = {
            "pe_once": ("vec_ps", "pool_ps", "pmix_ps", "boutT_ps", "logits_ps", "rank_ps", "gatesT_ps", "pT_ps"),
            "act_once": ("sincos", "vec_sb", "lam_exp", "pooled", "pmixed", "boutT", "gate_exp", "gatesT", "pT_sb"),
            "dve_once": ("ones_set", "angles", "lam_sums", "top_neg", "mask_sb", "gates_sb"),
        }

        def once(signal):
            return next(s(name) for name, signals in ONCE.items() if signal in signals)

        def await_once(eng, signal):
            for name, signals in ONCE.items():
                if signal in signals:
                    eng.wait_ge(s(name), signals.index(signal) + 1)

        class Steps:

            def __init__(self, eng, name):
                self.eng, self.sem, self.base, self.n = eng, s(name), 0, 0

            def start(self, base):
                self.base, self.n = base, 0

            def do(self, ins):
                self.n += 1
                ins.then_inc(self.sem, 1)

            def fence(self):
                self.eng.wait_ge(self.sem, self.base + self.n)

            def link(self, ins):
                self.do(ins)
                self.fence()

            def ended(self, n):
                assert self.n == n, (self.n, n)

        ds = bass.ds

        ring = sb("ring", [P, SLOTS, KC * NB])
        x = sb("x", [P, NT, D])
        hT = sb("hT", [P, KC, S])
        c_main = sb("c_main_sb", [P, C_N])
        ident = c_main[:, C_ID:C_ID + P]
        tri = c_main[:, C_TRI:C_TRI + 2 * P].rearrange("p (d j) -> p d j", d=2)
        strict = c_main[:, C_STRICT:C_STRICT + P]
        iota = c_main[:, C_IOTA:C_IOTA + P]
        lvl = c_main[:, C_LVL:C_MISC].rearrange("p (n d j) -> p n d j", n=LEVELS, d=2)
        inv_freq = c_main[:, C_MISC:C_MISC + 8]
        lam_init = c_main[:, C_MISC + 8:C_MISC + 10]
        one_lam = c_main[:, C_MISC + 10:C_MISC + 12]
        ones = sb("ones", [P, P])
        vec = sb("vec", [P, V_N])
        conv_wT = sb("conv_wT", [P, DEPTH * TAPS * CB])
        small = sb("small", [P, 64])
        eps, one1, ss, rstd = small[:, 0:1], small[:, 1:2], small[:, 4:6], small[:, 6:8]
        st_o, rs_o = small[:, 8:10], small[:, 10:12]
        mx, nmx, ssum, rsum = small[:, 12:16], small[:, 16:20], small[:, 20:24], small[:, 24:28]
        lam_s, neg_lam = small[:, 28:32], small[:, 32:34]
        cosb = sb("cosb", [P, NT, ROPE_HALF])
        sinb = sb("sinb", [P, NT, ROPE_HALF])
        wab = sb("wab", [P, DEPTH * KC * 4 * H])
        ab = sb("ab", [P, 4, NT, H])
        ab_t = sb("ab_t", [P, 3, 2, NT, H])
        gcum = sb("gcum", [P, 2 * NT * H])
        eg = sb("eg", [P, 2 * NT * H])
        gend = sb("gend", [P, 2 * NT * H])
        ea = sb("ea", [P, 2, H])
        R_GDN, R_SUB, R_ALOG, R_DT, R_LAM, R_N = 0, 128, 256, 272, 288, 544
        rows = sb("rows", [P, DEPTH * R_N])
        rounds_i = sb("rounds_i", [P, 1], I32)
        rel = sb("rel", [33, H])
        pos_i = sb("pos_i", [P, NT], I32)
        scratch = nc.dram_tensor("bias_scratch", (H, P, NB), F32).ap()
        region = sb("region", [P, 19552])

        def view(at, n):
            return region[:, at:at + n]

        qb, kb, vb = (view(n * NT * D, NT * D).rearrange("p (t c) -> p t c", t=NT) for n in range(3))
        XC = S + 2 * PAD
        conv_in = view(6144, CB * XC)
        conv_b = conv_in.rearrange("p (b c) -> p b c", b=CB)
        ya = conv_b[:, 0:H, PAD:PAD + S].rearrange("p h (t c) -> p h t c", t=NT)
        yaT = view(6144 + 8 * XC, KC * S).rearrange("p (k t) -> p k t", k=KC)
        ybT = view(6144 + 8 * XC + KC * S, KC * S).rearrange("p (k t) -> p k t", k=KC)
        mT = view(2048, KC * S).rearrange("p (k t) -> p k t", k=KC)
        W0 = 12384

        def wk(n, k=1):
            return view(W0 + int(n * NB), int(k * NB))

        def units(ap):
            return ap.rearrange("p (u c) -> p u c", c=P)

        c3 = wk(0, 1.5)
        qTh, kTh, vTh = c3[:, 0:S], c3[:, S:2 * S], c3[:, 2 * S:3 * S]
        e3 = wk(1.5, 1.5)
        kbg, kend = units(e3[:, 0:2 * P]), units(e3[:, 2 * P:4 * P])
        gb, bb, kv, E, qkT, Lv0, Lv1, T, U, V = (units(wk(3 + n)) for n in range(10))
        Lv = (Lv0, Lv1)
        vbeta, us = gb, Lv1
        wT, St = V[:, 0:2, :], V[:, 2:4, :]
        qs, oh = T[:, 0:2, :], T[:, 2:4, :]
        qk_h = units(wk(0))
        qkTh = wk(1)
        pm = wk(2, 2).rearrange("p (m t k) -> p m t k", m=2, t=NT)
        am = wk(4).rearrange("p (t k) -> p t k", t=NT)
        aT = units(wk(5))
        od = units(wk(6, 0.5))
        rp = [wk(7 + 0.5 * n, 0.5).rearrange("p (t g c) -> p t g c", t=NT, g=16) for n in range(4)]
        mg = [wk(n) for n in range(8)]

        z2 = view(0, 4096).rearrange("p (s t c) -> p s t c", s=4, t=NT)
        xn2 = view(4096, 2048).rearrange("p (t c) -> p t c", t=NT)
        band = view(6144, 2048).rearrange("p (t g c) -> p t g c", t=NT, g=4)
        mixT = view(8192, 2048).rearrange("p (k t) -> p k t", k=KC)
        pooledT = view(10240, 1024)
        count = view(11264, 512)
        wpool = view(11776, 512).rearrange("p (g c) -> p g c", g=4)
        bout = view(12288, 1024)
        bias2 = view(13312, 4096)
        q2h = units(view(17408, 512))
        qkT2 = view(17920, 512)
        aT2 = units(view(18432, 1024))
        p2 = view(4096, 1024)
        h2 = view(0, 2048).rearrange("p (t c) -> p t c", t=NT)
        bpad = view(2048, 2048)
        XT = view(4096, 512).rearrange("p (k c) -> p k c", k=KC)
        gm, uc, sg, ysb = (view(4608 + n * NB, NB) for n in range(4))
        actT = view(6656, 512).rearrange("p (c h t) -> p c h t", c=4, h=2)
        CT, Pg = view(7168, 256).rearrange("p (t c) -> p t c", t=NT), view(7424, 256).rearrange("p (t c) -> p t c", t=NT)
        P1 = view(7680, 128).rearrange("p (t c) -> p t c", t=NT)
        e0 = view(7808, 64)
        wr = view(7872, 256).rearrange("p (k e) -> p k e", k=KC)

        def te(at):
            return view(at, NT * NE).rearrange("p (t e) -> p t e", t=NT)

        logits, m_gt, m_eq, msk, gates, pre0, pre1, ranks = (te(8128 + 64 * n) for n in range(8))
        top8 = view(8640, 16).rearrange("p (t e) -> p t e", t=NT)
        rt = view(8656, 16)
        gatesT = view(8672, 256)
        rkx = view(8928, 320).rearrange("p (t e) -> p t e", t=NT)
        gx = view(9248, 320).rearrange("p (t e) -> p t e", t=NT)
        rkx_f, gx_f = view(8928, 320), view(9248, 320)
        brow = view(9568, 32)
        b_down = view(9600, 1024)
        grow = view(10624, 1024)
        ptok = view(11648, 512).rearrange("p (t c) -> p t c", t=NT)
        pT = view(12160, 512).rearrange("p (k t) -> p k t", k=2)
        pl = [view(12672 + n * NB, NB) for n in range(4)]
        xn3 = view(14720, 2048).rearrange("p (t c) -> p t c", t=NT)
        grow_l = view(16768, 1024)

        pb = [ctx.enter_context(nc.psum_tensor(f"bank{n}", [P, NB], F32)) for n in range(8)]
        block = ctx.enter_context(nc.Block())

        LAYER_TILES, seen = [], [0] * SLOTS
        for pos in range(26):
            slot = pos % SLOTS if pos < 24 else pos - 20
            LAYER_TILES.append((slot, seen[slot]))
            seen[slot] += 1
        PER_LAYER = seen
        LOADED = [DEPTH * n + 1 for n in PER_LAYER]

        def slot_w(slot):
            return ring[:, slot, :].rearrange("p (k n) -> p k n", k=KC)

        def tile_src(l, pos):
            if pos < 6:
                c = pos * NB
            elif pos < 12:
                c = Q_B + (pos - 6) * NB
            elif pos < 16:
                c = (Z_A if pos < 14 else Z_B) + (pos % 2) * NB
            elif pos < 24:
                g, kind = divmod(pos - 16, 4)
                if kind % 2:
                    return a["w_pa" if kind == 1 else "w_pb"][l, :, g * NB:(g + 1) * NB]
                c = GATES + kind // 2 * D + g * NB
            else:
                return a["w_out"][l, :, (pos - 24) * NB:(pos - 23) * NB]
            return a["w_in"][l, :, c:c + NB]

        def tile_read(l, pos):
            if pos < 6:
                return "qkv_ps", l * 12 + 2 * (pos + 1)
            if pos < 12:
                return "seg_ps", l * 12 + 2 * (pos - 5)
            if pos < 16:
                return "z_ps", l * 8 + 2 * (pos - 11)
            if pos < 24:
                return "merge_ps1", l * 8 + pos - 15
            return "xo_ps", l * 4 + 2 * (pos - 23)

        lay = "(k p) n -> p k n"
        NCONST = 7 + DEPTH * 7 + 3

        @block.sync
        def _(sp):
            def load(dst, src, name, **kw):
                sp.dma_start(dst, src, **kw).then_inc(s(name), 16)

            load(c_main[:, :], a["c_main"], "const_in")
            load(x[:, :, :], a["x"][0].rearrange("(t p) c -> p t c", p=P), "const_in")
            load(wk(0)[V_NORM:V_MIX, 0:P], a["norm_w"].rearrange("l (k p) -> (l k) p", p=P), "const_in")
            for row, name in ((V_MIX, "g_mix_2"), (V_FFN, "g_ffn_2"), (V_PLE, "g_ple_2")):
                load(wk(0)[row:row + 8, 0:P], a[name].rearrange("l (k p) -> (l k) p", p=P), "const_in")
            load(wk(0)[V_POOL:V_N, 0:P], a["pool_scale_2"].rearrange("l (k p) -> (l k) p", p=P), "const_in")
            for l in range(DEPTH):
                load(wk(0)[0:TAPS * CB, (1 + l) * P:(2 + l) * P], a["conv_w"][l].rearrange("w (b p) -> (w b) p", p=P), "const_in")
                load(wab[:, l * 256:(l + 1) * 256].rearrange("p (k n) -> p k n", k=KC),
                     a["w_in"][l, :, AB:AB + 4 * H].rearrange(lay, p=P), "const_in")
                for off, n, src in ((R_GDN, P, a["gdn_norm_w"][l:l + 1, :]), (R_SUB, P, a["diff_subln_w"][l:l + 1, :]),
                                    (R_ALOG, 16, a["a_log"][l:l + 1].rearrange("o d h -> o (d h)")),
                                    (R_DT, 16, a["dt_bias"][l:l + 1].rearrange("o d h -> o (d h)")),
                                    (R_LAM, 256, a["diff_lambda"][l:l + 1].rearrange("o d h -> o (d h)"))):
                    load(rows[:, l * R_N + off:l * R_N + off + n], src.broadcast_to([P, n]), "const_in")
            load(rel[0:32, :], a["rel_bias_2"], "const_in")
            load(wk(1)[0:33, :], a["c_bucket"], "const_in")
            load(pos_i[:, :], a["positions"][0].rearrange("(t p) -> p t", p=P), "const_in", allow_slow_non_contiguous=True)

            read = {}

            def load_tile(dst, src, slot, reader):
                if slot in read:
                    sp.wait_ge(s(read[slot][0]), read[slot][1])
                load(dst, src, f"w_in_slot{slot}")
                read[slot] = reader

            for l in range(DEPTH):
                for pos in range(26):
                    slot = LAYER_TILES[pos][0]
                    load_tile(slot_w(slot), tile_src(l, pos).rearrange(lay, p=P), slot, tile_read(l, pos))
                    if l == 0 and pos == 5:
                        sp.wait_ge(s("bias_rows"), H)
                        load(scratch.rearrange("h p n -> p h n"), view(0, H * NB).rearrange("p (h n) -> p h n", h=H), "bias_stored")
            for n in range(4):
                load_tile(slot_w(n), a["w_in_2"][0, :, n * NB:(n + 1) * NB].rearrange(lay, p=P), n, ("z2_ps", 2 * (n + 1)))
            for n in range(2):
                load_tile(slot_w(4 + n), a["w_out_2"][0, :, n * NB:(n + 1) * NB].rearrange(lay, p=P), 4 + n, ("xm_ps", 2 * (n + 1)))
            sp.wait_ge(s("x_added"), 4 * DEPTH)
            load(grow_l, a["final_norm_w"].rearrange("(o n) -> o n", o=1).broadcast_to([P, D]), "fnorm_in")
            load(band, a["c_band"].rearrange("(t p) (g c) -> p t g c", p=P, g=4), "mix_in")
            load(count.rearrange("p (t c) -> p t c", t=NT), a["c_count"].rearrange("(t p) c -> p t c", p=P), "mix_in")
            load(wpool, a["w_pool_2"][0].rearrange("g p c -> p g c"), "mix_in")
            sp.wait_ge(s("bias_stored"), 16)
            sp.wait_ge(s("normed"), 2 * DEPTH + 2)
            for t in range(NT):
                src = bass.AP(scratch.tensor, 255 - t * P, [[NB - 1, P], [P * NB, H], [1, S]])
                load(bias2.rearrange("p (h t k) -> p h t k", h=H, t=NT)[:, :, t, :], src, "mix_in")

            def expert(e, i):
                for j in range(6):
                    if i is None and j in read:
                        sp.wait_ge(s(read[j][0]), read[j][1])
                    if j < 4:
                        src = gate_up_src[ds(e * D + j * 256, 256), :]
                        dst = ring[:, j, :].rearrange("p (k n) -> p k n", k=2)
                    else:
                        src = down_src[ds(e * D + (j - 4) * 512, 512), :]
                        dst = ring[:, j, :].rearrange("p (k n) -> p k n", k=4)
                    src = src.rearrange(lay, p=P)
                    if i is not None:
                        sp.wait_ge(s({3: "gate_up_ps", 5: "y_ps"}.get(j, f"w_used{j}")), i)
                    load(dst, src, f"w_in_slot{j}")

            gate_up_src = a["w_gate_up_2"][0].rearrange("e d n -> (e d) n")
            down_src = a["w_down_2"][0].rearrange("e d n -> (e d) n")
            bgu = a["b_gate_up_2"][0]
            expert(0, None)
            sp.wait_ge(s("x_mixed"), 4)
            load(grow, a["g_ffn_2"].broadcast_to([P, D]), "ffn_in")
            load(wr, a["w_router_2"][0].rearrange("(k p) e -> p k e", p=P), "ffn_in")
            load(brow, a["b_router_2"].broadcast_to([P, NE]), "ffn_in")
            load(b_down[0:NE, :], a["b_down_2"][0], "ffn_in")
            load(ptok, a["p_2"][0, 0].rearrange("(t p) c -> p t c", p=P), "ffn_in")
            load(grow_l, a["g_final_2"].rearrange("(o n) -> o n", o=1).broadcast_to([P, D]), "ffn_in")
            sp.wait_ge(s("bpad_zero"), 1)
            load(bpad[0:1, :], bgu[0:1, :], "bias_in")
            sp.wait_ge(s("rounds_known"), 1)
            rounds = sp.value_load(rounds_i[0:1, 0:1], min_val=1, max_val=ROUNDS)
            n_items = sp.snap(rounds * NE)
            with sp.Fori(1, n_items) as i:
                e = sp.snap(i % NE)
                expert(e, i)
                sp.wait_ge(s("gate_up_ps"), i)
                load(bpad[0:1, :], bgu[ds(e, 1), :], "bias_in")
            for n in range(2):
                sp.wait_ge(s(f"w_used{n}"), n_items)
                load(slot_w(n), a["w_ple_gate_2"][0, :, n * NB:(n + 1) * NB].rearrange(lay, p=P), f"w_in_slot{n}")
            sp.wait_ge(s("w_used2"), n_items)
            load(ring[:, 2, 0:2048].rearrange("p (k n) -> p k n", k=2), a["w_ple_proj_2"][0].rearrange(lay, p=P), "w_in_slot2")
            sp.wait_ge(s("y_final"), 2)
            load(out[0].rearrange("(t p) c -> p t c", p=P), x[:, :, :], "stored")
            sp.wait_ge(s("stored"), 16)

        @block.tensor
        def _(pe):
            def w_wait(l, pos):
                slot, k = LAYER_TILES[pos]
                pe.wait_ge(s(f"w_in_slot{slot}"), 16 * (l * PER_LAYER[slot] + k + 1))
                return slot_w(slot)

            def transpose16(src, n):
                for kp in range(4):
                    for kk in range(2):
                        for t in range(NT):
                            last = pe.transpose(pb[kp][:, (2 * kk + t) * P:(2 * kk + t + 1) * P], src(t, 2 * kp + kk), ident)
                    last.then_inc(s("tr_ps"), 1)
                pe.wait_ge(s("tr_act"), 2 * (n + 1))
                pe.wait_ge(s("tr_dve"), 2 * (n + 1))

            def product(dst, lhs, w, n_k=KC):
                for k in range(n_k):
                    mm = pe.matmul(dst, lhs(k), w(k), start=(k == 0), stop=(k == n_k - 1))
                return mm

            def blk(ap):
                return lambda t, k: ap[:, t, k * P:(k + 1) * P]

            pe.wait_ge(s("const_in"), 16 * NCONST)
            await_once(pe, "ones_set")
            pe.transpose(pb[0][:, 0:V_N], wk(0)[0:V_N, 0:P], ident[0:V_N, 0:V_N])
            for l in range(DEPTH):
                last = pe.transpose(pb[1][:, l * P:l * P + TAPS * CB], wk(0)[0:TAPS * CB, (1 + l) * P:(2 + l) * P],
                                    ident[0:TAPS * CB, 0:TAPS * CB])
            last.then_inc(once("vec_ps"), 1)
            for h in range(H):
                if h >= 4:
                    pe.wait_ge(s("bias_rows"), h - 3)
                pe.matmul(pb[4 + h % 4][:, :], rel[:, h:h + 1].broadcast_to([33, P]), wk(1)[0:33, :],
                          start=True, stop=True).then_inc(s("bias_ps"), 1)
            pe.wait_ge(s("bias_rows"), H)
            await_once(pe, "vec_sb")

            with pe.Fori(0, DEPTH) as l:
                pe.wait_ge(s("normed"), 2 * (l + 1))
                transpose16(blk(kb), 4 * l)
                for u in range(12):
                    if u % 2 == 0:
                        w = w_wait(l, u // 2)
                    if u >= 4:
                        pe.wait_ge(s("qkv_sb_act" if u % 2 == 0 else "qkv_sb_dve"), l * 6 + (u - 4) // 2 + 1)
                    for b in range(2):
                        c = (2 * (u % 2) + b) * P
                        mm = product(pb[u % 4][:, b * S:(b + 1) * S], lambda k: w[:, k, c:c + P], lambda k: hT[:, k, :])
                    mm.then_inc(s("qkv_ps"), 1)
                for t in range(NT):
                    mm = product(pb[6][:, t * 32:(t + 1) * 32], lambda k: hT[:, k, t * P:(t + 1) * P],
                                 lambda k: wab[:, ds(l * 256 + k * 32, 32)])
                mm.then_inc(s("ab_ps"), 1)
                for u in range(12):
                    t = u % 2
                    if t == 0:
                        w = w_wait(l, 6 + u // 2)
                    if u >= 4:
                        pe.wait_ge(s("seg_sb_act" if t == 0 else "seg_sb_dve"), l * 6 + (u - 4) // 2 + 1)
                    else:
                        pe.wait_ge(s("qkv_sb_act" if t == 0 else "qkv_sb_dve"), l * 6 + 5 + u // 2)
                    mm = product(pb[u % 4][:, :], lambda k: hT[:, k, t * P:(t + 1) * P], lambda k: w[:, k, :])
                    mm.then_inc(s("seg_ps"), 1)
                pe.wait_ge(s("g_sb"), l + 1)
                for d in range(2):
                    g_d = ab[:, 2 + d, :, :].rearrange("p t h -> p (t h)")
                    pe.matmul(pb[5][:, d * 16:(d + 1) * 16], tri[:, d, :], g_d, start=True, stop=True)
                    mm = pe.matmul(pb[5][:, 32 + d * 16:32 + (d + 1) * 16], ones[:, :], g_d, start=True, stop=True)
                mm.then_inc(s("gcum_ps"), 1)
                with pe.Fori(0, H) as h:
                    n = l * H + h
                    pe.wait_ge(s("seg_sb_act"), (l + 1) * 6)
                    pe.wait_ge(s("seg_sb_dve"), (l + 1) * 6)
                    pe.wait_ge(s("gd_gb"), 2 * (n + 1))
                    for u in range(4):
                        pe.matmul(pb[3][:, u * P:(u + 1) * P], gb[:, u, :], tri[:, u // 2, :], start=True, stop=True)
                    for u in range(4):
                        mm = pe.matmul(pb[4][:, u * P:(u + 1) * P], bb[:, u, :], ident, start=True, stop=True)
                    mm.then_inc(s("gd_rows_ps"), 1)
                    pe.wait_ge(s("gd_sq"), n + 1)
                    pe.matmul(pb[0][:, :], ones[:, :], e3[:, 0:2 * S], start=True, stop=True).then_inc(s("gd_norm_ps"), 1)
                    pe.wait_ge(s("gd_qkn"), 2 * (n + 1))
                    for t in range(NT):
                        pe.transpose(pb[1][:, t * P:(t + 1) * P], kTh[:, t * P:(t + 1) * P], ident)
                        mm = pe.transpose(pb[1][:, (2 + t) * P:(3 + t) * P], vTh[:, t * P:(t + 1) * P], ident)
                    mm.then_inc(s("gd_kv_ps"), 1)
                    for t in range(NT):
                        kt = kTh[:, t * P:(t + 1) * P]
                        pe.matmul(pb[2][:, t * P:(t + 1) * P], kt, kt, start=True, stop=True)
                        mm = pe.matmul(pb[2][:, (2 + t) * P:(3 + t) * P], kt, qTh[:, t * P:(t + 1) * P], start=True, stop=True)
                    mm.then_inc(s("gd_kk_ps"), 1)
                    pe.wait_ge(s("gd_u"), n * LEVELS + 1)
                    for u in range(4):
                        mm = pe.transpose(pb[5][:, u * P:(u + 1) * P], U[:, u, :], ident)
                    mm.then_inc(s("gd_v_ps"), 1)
                    for v in range(1, LEVELS):
                        pe.wait_ge(s("gd_lvl"), n * LEVELS + v + 1)
                        if v == 1:
                            pe.wait_ge(s("gd_vcopy"), n * LEVELS + 1)
                        else:
                            pe.wait_ge(s("gd_t"), n * (LEVELS - 2) + v - 1)
                        for u in range(4):
                            mm = pe.matmul(pb[5][:, u * P:(u + 1) * P], Lv[v % 2][:, u, :], T[:, u, :], start=True, stop=True)
                        mm.then_inc(s("gd_v_ps"), 1)
                        pe.wait_ge(s("gd_vcopy"), n * LEVELS + v + 1)
                        pe.wait_ge(s("gd_u"), n * LEVELS + v)
                        if v < LEVELS - 1:
                            for u in range(4):
                                mm = pe.matmul(pb[6][:, u * P:(u + 1) * P], U[:, u, :], V[:, u, :], start=True, stop=True)
                            mm.then_inc(s("gd_tv_ps"), 1)
                        for u in range(4):
                            mm = pe.matmul(pb[7][:, u * P:(u + 1) * P], V[:, u, :], U[:, u, :], start=True, stop=True)
                        mm.then_inc(s("gd_vu_ps"), 1)
                    pe.wait_ge(s("gd_u"), (n + 1) * LEVELS)
                    pe.wait_ge(s("gd_vb"), 5 * (n + 1))
                    for u in range(4):
                        pe.matmul(pb[0][:, u * P:(u + 1) * P], U[:, u, :], vbeta[:, u, :], start=True, stop=True)
                    for d in range(2):
                        mm = pe.matmul(pb[1][:, d * P:(d + 1) * P], kbg[:, d, :], U[:, 1 + d, :], start=True, stop=True)
                    mm.then_inc(s("gd_uw_ps"), 1)
                    pe.wait_ge(s("gd_uw_sb"), 2 * (n + 1))
                    for d in range(2):
                        mm = pe.matmul(pb[2][:, d * P:(d + 1) * P], kend[:, d, :], us[:, 3 * d, :], start=True, stop=True)
                    mm.then_inc(s("gd_s_ps"), 1)
                    pe.wait_ge(s("gd_s_sb"), n + 1)
                    for d in range(2):
                        pe.matmul(pb[3][:, d * P:(d + 1) * P], wT[:, d, :], St[:, d, :], start=True, stop=True)
                        mm = pe.matmul(pb[5][:, d * P:(d + 1) * P], qTh[:, (1 - d) * P:(2 - d) * P], St[:, d, :],
                                       start=True, stop=True)
                    mm.then_inc(s("gd_ws_ps"), 1)
                    pe.wait_ge(s("gd_vnew"), n + 1)
                    for t in range(NT):
                        for d in range(2):
                            mm = pe.matmul(pb[4][:, t * P:(t + 1) * P], qkT[:, 2 * d + t, :], us[:, 2 * d + t, :],
                                           start=(d == 0), stop=(d == 1))
                    mm.then_inc(s("gd_o_ps"), 1)
                    pe.wait_ge(s("gd_y"), n + 1)

                with pe.Fori(0, H) as h:
                    n = l * H + h
                    pe.wait_ge(s("at_qk"), 2 * (n + 1))
                    for j in range(4):
                        mm = pe.transpose(pb[0][:, j * P:(j + 1) * P], qk_h[:, j, :], ident)
                    mm.then_inc(s("at_qkT_ps"), 1)
                    pe.wait_ge(s("at_qkT"), n + 1)
                    for m in range(2):
                        for t in range(NT):
                            mm = pe.matmul(pb[1 + m][:, t * S:(t + 1) * S], qkTh[m * 64:(m + 1) * 64, t * P:(t + 1) * P],
                                           qkTh[m * 64:(m + 1) * 64, S:2 * S], start=True, stop=True)
                        mm.then_inc(s("at_s_ps"), 1)
                    pe.wait_ge(s("at_p"), n + 1)
                    for kt in range(NT):
                        for t in range(NT):
                            mm = pe.transpose(pb[3][:, (kt * 2 + t) * P:(kt * 2 + t + 1) * P], am[:, t, kt * P:(kt + 1) * P], ident)
                    mm.then_inc(s("at_pT_ps"), 1)
                    pe.wait_ge(s("at_pT"), n + 1)
                    for t in range(NT):
                        for kt in range(NT):
                            mm = pe.matmul(pb[4][:, t * P:(t + 1) * P], aT[:, kt * 2 + t, :], vb[:, kt, ds(h * P, P)],
                                           start=(kt == 0), stop=(kt == 1))
                    mm.then_inc(s("at_o_ps"), 1)
                    pe.wait_ge(s("at_y"), n + 1)

                for u in range(8):
                    t = u % 2
                    if t == 0:
                        w = w_wait(l, 12 + u // 2)
                    if u >= 4:
                        pe.wait_ge(s("z_gated"), l * 8 + u - 3)
                    product(pb[4 + u % 4][:, :], lambda k: hT[:, k, t * P:(t + 1) * P], lambda k: w[:, k, :]).then_inc(s("z_ps"), 1)
                pe.wait_ge(s("z_gated"), l * 8 + 4)
                transpose16(lambda t, k: ya[:, k, t, :], 4 * l + 1)
                pe.wait_ge(s("z_gated"), l * 8 + 8)
                transpose16(blk(qb), 4 * l + 2)
                for g in range(2):
                    if g == 1:
                        pe.wait_ge(s("merged"), 4 * l + 2)
                    for kind in range(4):
                        w = w_wait(l, 16 + 4 * g + kind)
                        src = (hT, yaT, hT, ybT)[kind]
                        for t in range(NT):
                            product(pb[4 * t + kind][:, :], lambda k: src[:, k, t * P:(t + 1) * P],
                                    lambda k: w[:, k, :]).then_inc(s(f"merge_ps{t}"), 1)
                pe.wait_ge(s("merged"), 4 * (l + 1))
                transpose16(blk(qb), 4 * l + 3)
                for u in range(4):
                    t = u % 2
                    if t == 0:
                        w = w_wait(l, 24 + u // 2)
                    product(pb[4 + u][:, :], lambda k: mT[:, k, t * P:(t + 1) * P], lambda k: w[:, k, :]).then_inc(s("xo_ps"), 1)
                pe.wait_ge(s("x_added"), 4 * (l + 1))

            pe.wait_ge(s("normed"), 2 * DEPTH + 4)
            transpose16(blk(xn2), 8)
            for u in range(8):
                t = u % 2
                if t == 0:
                    slot = u // 2
                    pe.wait_ge(s(f"w_in_slot{slot}"), 16 * LOADED[slot])
                if u >= 4:
                    pe.wait_ge(s("z2_sb_act" if t == 0 else "z2_sb_dve"), (u - 4) // 2 + 1)
                product(pb[4 + u % 4][:, :], lambda k: hT[:, k, t * P:(t + 1) * P], lambda k: slot_w(slot)[:, k, :]).then_inc(s("z2_ps"), 1)
            pe.wait_ge(s("z2_sb_act"), 4)
            pe.wait_ge(s("z2_sb_dve"), 4)
            pe.wait_ge(s("mix_in"), 16 * 5)
            for g in range(4):
                mm = product(pb[g // 2][:, (g % 2) * S:(g % 2 + 1) * S], lambda t: z2[:, 0, t, g * P:(g + 1) * P],
                             lambda t: band[:, t, g, :], NT)
            mm.then_inc(once("pool_ps"), 1)
            await_once(pe, "pooled")
            for g in range(4):
                mm = pe.matmul(pb[2 + g // 2][:, (g % 2) * S:(g % 2 + 1) * S], wpool[:, g, :], pooledT[:, g * S:(g + 1) * S],
                               start=True, stop=True)
            mm.then_inc(once("pmix_ps"), 1)
            await_once(pe, "pmixed")
            with pe.Fori(DEPTH * H, DEPTH * H + H // 2) as n:
                pe.wait_ge(s("at_qk"), 2 * (n + 1))
                for j in range(4):
                    mm = pe.transpose(pb[0][:, j * P:(j + 1) * P], q2h[:, j, :], ident)
                mm.then_inc(s("at_qkT_ps"), 1)
                pe.wait_ge(s("at_qkT"), n + 1)
                for m in range(2):
                    for t in range(NT):
                        mm = pe.matmul(pb[1 + m][:, t * S:(t + 1) * S], qkT2[m * 64:(m + 1) * 64, t * P:(t + 1) * P],
                                       qkT2[m * 64:(m + 1) * 64, S:2 * S], start=True, stop=True)
                    mm.then_inc(s("at_s_ps"), 1)
                pe.wait_ge(s("at_p"), n + 1)
                for m in range(2):
                    for kt in range(NT):
                        for t in range(NT):
                            c = (kt * 2 + t) * P
                            mm = pe.transpose(pb[3 + m][:, c:c + P], p2[:, m * 512 + t * S + kt * P:m * 512 + t * S + (kt + 1) * P], ident)
                mm.then_inc(s("at_pT_ps"), 1)
                pe.wait_ge(s("at_pT"), n + 1)
                for t in range(NT):
                    for m in range(2):
                        mm = product(pb[5][:, t * P + m * 64:t * P + (m + 1) * 64], lambda kt: aT2[:, m * 4 + kt * 2 + t, :],
                                     lambda kt: z2[:, 3, kt, ds(n * P + (m * 64 - DEPTH * H * P), 64)], NT)
                mm.then_inc(s("at_o_ps"), 1)
                pe.wait_ge(s("at_y"), n + 1)
            for t in range(NT):
                for c in range(4):
                    mm = pe.transpose(pb[c // 2][:, (c % 2) * S + t * P:(c % 2) * S + (t + 1) * P],
                                      bout[:, t * 512 + c * P:t * 512 + (c + 1) * P], ident)
            mm.then_inc(once("boutT_ps"), 1)
            await_once(pe, "boutT")
            for u in range(4):
                t, slot = u % 2, 4 + u // 2
                if t == 0:
                    pe.wait_ge(s(f"w_in_slot{slot}"), 16 * LOADED[slot])
                product(pb[4 + u][:, :], lambda k: mixT[:, k, t * P:(t + 1) * P], lambda k: slot_w(slot)[:, k, :]).then_inc(s("xm_ps"), 1)

            pe.wait_ge(s("normed"), 2 * DEPTH + 6)
            transpose16(blk(h2), 9)
            pe.wait_ge(s("ffn_in"), 16 * 6)
            for t in range(NT):
                mm = product(pb[0][:, t * NE:(t + 1) * NE], lambda k: hT[:, k, t * P:(t + 1) * P], lambda k: wr[:, k, :])
            mm.then_inc(once("logits_ps"), 1)
            await_once(pe, "mask_sb")
            pe.matmul(pb[1][:, 0:NE], strict, msk[:, 0, :], start=True, stop=True)
            pe.matmul(pb[1][:, NE:2 * NE], strict, msk[:, 1, :], start=True, stop=False)
            pe.matmul(pb[1][:, NE:2 * NE], ones[:, :], msk[:, 0, :], start=False, stop=True)
            pe.matmul(pb[1][:, 2 * NE:3 * NE], ones[:, :], msk[:, 0, :], start=True, stop=False)
            pe.matmul(pb[1][:, 2 * NE:3 * NE], ones[:, :], msk[:, 1, :], start=False, stop=True).then_inc(once("rank_ps"), 1)
            await_once(pe, "gates_sb")
            for t in range(NT):
                mm = pe.transpose(pb[2][0:NE, t * P:(t + 1) * P], gates[:, t, :], ident)
            mm.then_inc(once("gatesT_ps"), 1)
            await_once(pe, "gatesT")
            for t in range(NT):
                for g in range(2):
                    pe.matmul(pb[4 + 2 * t + g][:, :], gatesT[0:NE, t * P:(t + 1) * P], b_down[0:NE, g * NB:(g + 1) * NB],
                              start=True, stop=False, skip_group_check=True)

            def gather():
                for k in range(KC):
                    for t in range(NT):
                        mm = pe.matmul(pb[3][:, k * CAP:(k + 1) * CAP], h2[:, t, k * P:(k + 1) * P], P1[:, t, :],
                                       start=(t == 0), stop=(t == 1))
                mm.then_inc(s("gather_ps"), 1)

            pe.wait_ge(s("onehot"), 1)
            gather()
            rounds = pe.value_load(rounds_i[0:1, 0:1], min_val=1, max_val=ROUNDS) if False else None
            pe.wait_ge(s("rounds_known"), 1)
            rounds = pe.value_load(rounds_i[0:1, 0:1], min_val=1, max_val=ROUNDS)
            n_items = pe.snap(rounds * NE)
            with pe.Fori(0, n_items) as i:
                pe.wait_ge(s("XT_sb"), i + 1)
                pe.wait_ge(s("bias_in"), 16 * (i + 1))
                for g in range(2):
                    for hf in range(2):
                        pe.matmul(pb[g][hf * 64:(hf + 1) * 64, :], e0, bpad[:, g * D + hf * NB:g * D + (hf + 1) * NB],
                                  start=True, stop=False)
                for j in range(4):
                    pe.wait_ge(s(f"w_in_slot{j}"), 16 * (LOADED[j] + 1 + i))
                    wj = ring[:, j, :].rearrange("p (k n) -> p k n", k=2)
                    for kk in range(2):
                        for g in range(2):
                            for hf in range(2):
                                c = g * D + hf * NB
                                mm = pe.matmul(pb[g][hf * 64:(hf + 1) * 64, :], XT[:, 2 * j + kk, :], wj[:, kk, c:c + NB],
                                               start=False, stop=(j == 3 and kk == 1))
                    mm.then_inc(s("gate_up_ps" if j == 3 else f"w_used{j}"), 1)
                pe.wait_ge(s("onehot"), i + 2)
                gather()
                pe.wait_ge(s("onehot_g"), i + 1)
                for t in range(NT):
                    mm = pe.transpose(pb[2][:, t * P:(t + 1) * P], Pg[:, t, :], ident)
                mm.then_inc(s("CT_ps"), 1)
                pe.wait_ge(s("act"), i + 1)
                pe.wait_ge(s("XT_sb"), i + 2)
                for c in range(4):
                    mm = pe.transpose(pb[3][:, c * P:(c + 1) * P], gm[:, c * P:(c + 1) * P], ident)
                mm.then_inc(s("actT_ps"), 1)
                pe.wait_ge(s("CT_sb"), i + 1)
                pe.wait_ge(s("actT_sb"), i + 1)
                for j in range(2):
                    pe.wait_ge(s(f"w_in_slot{4 + j}"), 16 * (LOADED[4 + j] + 1 + i))
                    wj = ring[:, 4 + j, :].rearrange("p (k n) -> p k n", k=4)
                    for c in range(4):
                        for hf in range(2):
                            mm = pe.matmul(pb[2][hf * 64:(hf + 1) * 64, :], actT[:, c, j, :], wj[:, c, hf * NB:(hf + 1) * NB],
                                           start=(j == 0 and c == 0), stop=(j == 1 and c == 3))
                    mm.then_inc(s("y_ps" if j == 1 else "w_used4"), 1)
                pe.wait_ge(s("y_sb"), i + 1)
                for hf in range(2):
                    for t in range(NT):
                        mm = pe.matmul(pb[4 + 2 * t + hf][:, :], CT[hf * 64:(hf + 1) * 64, t, :], ysb[hf * 64:(hf + 1) * 64, :],
                                       start=False, stop=False, skip_group_check=True)
                mm.then_inc(s("combined"), 1)

            pe.wait_ge(s("x_moe"), 4)
            for t in range(NT):
                for k in range(2):
                    mm = pe.transpose(pb[4][:, k * S + t * P:k * S + (t + 1) * P], ptok[:, t, k * P:(k + 1) * P], ident)
            mm.then_inc(once("pT_ps"), 1)
            pe.wait_ge(s("normed"), 2 * DEPTH + 8)
            transpose16(blk(xn3), 10)
            await_once(pe, "pT_sb")
            pe.wait_ge(s("w_in_slot2"), 16 * (LOADED[2] + 1 + n_items))
            wp = ring[:, 2, 0:2048].rearrange("p (k n) -> p k n", k=2)
            for g in range(2):
                pe.wait_ge(s(f"w_in_slot{g}"), 16 * (LOADED[g] + 1 + n_items))
                for t in range(NT):
                    product(pb[2 * g + t][:, :], lambda k: hT[:, k, t * P:(t + 1) * P], lambda k: slot_w(g)[:, k, :]).then_inc(s("ple_ps"), 1)
                    product(pb[4 + 2 * g + t][:, :], lambda k: pT[:, k, t * P:(t + 1) * P],
                            lambda k: wp[:, k, g * NB:(g + 1) * NB], 2).then_inc(s("ple_ps"), 1)

        @block.scalar
        def _(act):
            me = Steps(act, "act_steps")
            in_layer = Steps(act, "act_layer_steps")
            in_gdn = Steps(act, "act_gdn_steps")

            def copies16(n, scale):
                for j, kp in enumerate((0, 2)):
                    act.wait_ge(s("tr_ps"), 4 * n + kp + 1)
                    for kk in range(2):
                        k = 2 * kp + kk
                        dst, sc = scale(k)
                        last = act.activation(dst, pb[kp][:, kk * S:(kk + 1) * S], ACT.Copy, scale=sc)
                    last.then_inc(s("tr_act"), 1)

            def row_rstd(steps, junk, n):
                for t in range(NT):
                    steps.do(act.activation(junk[:, t, :], x[:, t, :], ACT.Square, accum_out=ss[:, t:t + 1]))
                steps.fence()
                steps.link(act.activation(rstd, ss, ACT.Ln, bias=eps, scale=1.0 / D))
                act.activation(rstd, rstd, ACT.Exp, scale=-0.5).then_inc(s("rstd"), 1)

            def hT_with(at):
                return lambda k: (hT[:, k, :], vec[:, at(k)])

            await_once(act, "angles")
            act.activation(cosb[:, :, :], cosb[:, :, :], ACT.Sin)
            act.activation(sinb[:, :, :], sinb[:, :, :], ACT.Sin).then_inc(once("sincos"), 1)
            await_once(act, "vec_ps")
            act.activation(vec[:, :], pb[0][:, 0:V_N], ACT.Copy)
            act.activation(conv_wT[:, 0:TAPS * CB], pb[1][:, 0:TAPS * CB], ACT.Copy)
            act.activation(conv_wT[:, TAPS * CB:2 * TAPS * CB], pb[1][:, P:P + TAPS * CB], ACT.Copy).then_inc(once("vec_sb"), 1)
            for h in range(H):
                act.wait_ge(s("bias_ps"), h + 1)
                act.activation(view(h * NB, NB), pb[4 + h % 4][:, :], ACT.Copy).then_inc(s("bias_rows"), 1)
            await_once(act, "lam_sums")
            act.activation(lam_s, lam_s, ACT.Exp).then_inc(once("lam_exp"), 1)
            await_once(act, "vec_sb")
            act.wait_ge(s("bias_stored"), 16)

            with act.Fori(0, DEPTH) as l:
                in_layer.start(l * 6)
                row_rstd(in_layer, kb, l)
                copies16(4 * l, lambda k: (hT[:, k, :], vec[:, ds(l * KC + V_NORM + k, 1)]))
                for u in range(0, 12, 2):
                    act.wait_ge(s("qkv_ps"), l * 12 + u + 1)
                    act.activation(conv_b[:, 2 * u:2 * u + 2, PAD:PAD + S], pb[u % 4][:, :].rearrange("p (b c) -> p b c", b=2),
                                   ACT.Copy).then_inc(s("qkv_sb_act"), 1)
                act.wait_ge(s("ab_ps"), l + 1)
                for t in range(NT):
                    last = act.activation(ab[:, :, t, :], pb[6][:, t * 32:(t + 1) * 32].rearrange("p (c h) -> p c h", c=4), ACT.Copy)
                last.then_inc(s("ab_sb"), 1)
                act.wait_ge(s("ab_neg"), l + 1)
                in_layer.link(act.activation(ab_t[:, 1], ab_t[:, 1], ACT.Exp))
                in_layer.do(act.activation(ab_t[:, 1], ab_t[:, 1], ACT.Ln, bias=one1))
                in_layer.do(act.activation(ab[:, 0:2], ab[:, 0:2], ACT.Exp, scale=-1.0))
                act.activation(ea[:, :, :], rows[:, ds(l * R_N + R_ALOG, 16)].rearrange("p (d h) -> p d h", d=2), ACT.Exp).then_inc(s("ab_exp"), 1)
                for u in range(0, 12, 2):
                    act.wait_ge(s("seg_ps"), l * 12 + u + 1)
                    dst = (qb, kb, vb)[u // 4]
                    act.activation(dst[:, 0, (u // 2 % 2) * NB:(u // 2 % 2 + 1) * NB], pb[u % 4][:, :], ACT.Copy).then_inc(s("seg_sb_act"), 1)
                act.wait_ge(s("gcum_cp"), l + 1)
                act.activation(eg[:, :], gcum[:, :], ACT.Exp)
                act.activation(gend[:, :], gend[:, :], ACT.Exp).then_inc(s("gcum_sb"), 1)
                in_layer.ended(6)

                with act.Fori(0, H) as h:
                    n = l * H + h
                    in_gdn.start(n * 4)
                    act.wait_ge(s("gd_conv"), n + 1)
                    act.activation(e3, c3, ACT.Exp, scale=-1.0).then_inc(s("gd_e"), 1)
                    act.wait_ge(s("gd_silu"), n + 1)
                    act.activation(e3[:, 0:2 * S], c3[:, 0:2 * S], ACT.Square).then_inc(s("gd_sq"), 1)
                    act.wait_ge(s("gd_norm_ps"), n + 1)
                    in_gdn.link(act.activation(e3[:, 0:2 * S], pb[0][:, :], ACT.Ln, bias=eps))
                    act.activation(e3[:, 0:2 * S], e3[:, 0:2 * S], ACT.Exp, scale=-0.5).then_inc(s("gd_rn"), 1)
                    act.wait_ge(s("gd_diff"), n + 1)
                    act.activation(E, E, ACT.Exp).then_inc(s("gd_ex"), 1)
                    act.wait_ge(s("gd_kv_ps"), n + 1)
                    act.activation(kv, units(pb[1][:, :]), ACT.Copy).then_inc(s("gd_kv"), 1)
                    for v in range(LEVELS):
                        act.wait_ge(s("gd_v_ps"), n * LEVELS + v + 1)
                        act.activation(T if v == 0 else V, units(pb[5][:, :]), ACT.Copy).then_inc(s("gd_vcopy"), 1)
                    act.wait_ge(s("gd_uw_ps"), n + 1)
                    act.activation(us, units(pb[0][:, :]), ACT.Copy).then_inc(s("gd_uw_sb"), 1)
                    act.activation(wT, units(pb[1][:, 0:2 * P]), ACT.Copy).then_inc(s("gd_uw_sb"), 1)
                    act.wait_ge(s("gd_s_ps"), n + 1)
                    act.activation(St, units(pb[2][:, 0:2 * P]), ACT.Copy).then_inc(s("gd_s_sb"), 1)
                    act.wait_ge(s("gd_ws_ps"), n + 1)
                    for d in range(2):
                        last = act.activation(qs[:, d, :], pb[5][:, d * P:(d + 1) * P], ACT.Copy,
                                              scale=eg[:, ds(h + (1 + d) * H, 1)])
                    last.then_inc(s("gd_qs"), 1)
                    act.wait_ge(s("gd_osum"), n + 1)
                    for t in range(NT):
                        in_gdn.do(act.activation(E[:, t, :], oh[:, t, :], ACT.Square, accum_out=st_o[:, t:t + 1]))
                    in_gdn.fence()
                    in_gdn.link(act.activation(rs_o, st_o, ACT.Ln, bias=eps, scale=1.0 / P))
                    act.activation(rs_o, rs_o, ACT.Exp, scale=-0.5).then_inc(s("gd_rs"), 1)
                    in_gdn.ended(4)
                    act.wait_ge(s("gd_y"), n + 1)

                with act.Fori(0, H) as h:
                    n = l * H + h
                    act.wait_ge(s("at_qkT_ps"), n + 1)
                    act.activation(qkTh, pb[0][:, :], ACT.Copy).then_inc(s("at_qkT"), 1)
                    act.wait_ge(s("at_max"), n + 1)
                    for m in range(2):
                        for t in range(NT):
                            j = 2 * m + t
                            last = act.activation(pm[:, m, t, :], pb[1 + m][:, t * S:(t + 1) * S], ACT.Exp, bias=nmx[:, j:j + 1],
                                                  scale=DIFF_SCALE, accum_out=ssum[:, j:j + 1])
                    last.then_inc(s("at_exp"), 1)
                    act.wait_ge(s("at_pT_ps"), n + 1)
                    act.activation(aT, units(pb[3][:, :]), ACT.Copy).then_inc(s("at_pT"), 1)
                    act.wait_ge(s("at_o_ps"), n + 1)
                    for t in range(NT):
                        last = act.activation(od[:, t, :], pb[4][:, t * P:(t + 1) * P], ACT.Square, accum_out=st_o[:, t:t + 1])
                    last.then_inc(s("at_ss"), 1)
                    act.wait_ge(s("at_ss"), n + 1)
                    act.activation(rs_o, st_o, ACT.Ln, bias=eps, scale=1.0 / P).then_inc(s("at_ln"), 1)
                    act.wait_ge(s("at_ln"), n + 1)
                    act.activation(rs_o, rs_o, ACT.Exp, scale=-0.5).then_inc(s("at_rs"), 1)
                    act.wait_ge(s("at_y"), n + 1)

                for u in range(8):
                    act.wait_ge(s("z_ps"), l * 8 + u + 1)
                    if u >= 4:
                        act.wait_ge(s("z_gated"), l * 8 + u - 3)
                    act.activation(mg[u % 4], pb[4 + u % 4][:, :], ACT.Exp, scale=-1.0).then_inc(s("z_exp"), 1)
                    if u == 3:
                        act.wait_ge(s("z_gated"), l * 8 + 4)
                        copies16(4 * l + 1, lambda k: (yaT[:, k, :], 1.0))
                copies16(4 * l + 2, lambda k: (ybT[:, k, :], 1.0))
                for g in range(2):
                    for t in range(NT):
                        act.wait_ge(s(f"merge_ps{t}"), l * 8 + 4 * g + 3)
                        if g == 1:
                            act.wait_ge(s("merged"), 4 * l + t + 1)
                        act.activation(mg[4 * t], pb[4 * t][:, :], ACT.Exp, scale=-1.0)
                        act.activation(mg[4 * t + 1], pb[4 * t + 2][:, :], ACT.Exp, scale=-1.0).then_inc(s("merge_exp"), 1)
                copies16(4 * l + 3, lambda k: (mT[:, k, :], 1.0))
                act.wait_ge(s("x_added"), 4 * (l + 1))

            me.start(0)
            row_rstd(me, xn2, 2)
            act.wait_ge(s("normed"), 2 * DEPTH + 2)
            row_rstd(me, xn2, 3)
            copies16(8, lambda k: (hT[:, k, :], vec[:, V_MIX + k:V_MIX + k + 1]))
            for u in range(0, 8, 2):
                act.wait_ge(s("z2_ps"), u + 1)
                act.activation(z2[:, u // 2, 0, :], pb[4 + u % 4][:, :], ACT.Copy).then_inc(s("z2_sb_act"), 1)
            await_once(act, "pool_ps")
            act.activation(pooledT[:, 0:NB], pb[0][:, :], ACT.Copy)
            act.activation(pooledT[:, NB:2 * NB], pb[1][:, :], ACT.Copy).then_inc(once("pooled"), 1)
            await_once(act, "pmix_ps")
            for g in range(4):
                last = act.activation(mixT[:, g, :], pb[2 + g // 2][:, (g % 2) * S:(g % 2 + 1) * S], ACT.Copy,
                                      scale=vec[:, V_POOL + g:V_POOL + g + 1])
            last.then_inc(once("pmixed"), 1)
            with act.Fori(DEPTH * H, DEPTH * H + H // 2) as n:
                act.wait_ge(s("at_qkT_ps"), n + 1)
                act.activation(qkT2, pb[0][:, :], ACT.Copy).then_inc(s("at_qkT"), 1)
                act.wait_ge(s("at_max"), n + 1)
                for j in range(4):
                    last = act.activation(p2[:, j * S:(j + 1) * S], p2[:, j * S:(j + 1) * S], ACT.Exp, bias=nmx[:, j:j + 1])
                last.then_inc(s("at_exp"), 1)
                act.wait_ge(s("at_pT_ps"), n + 1)
                for m in range(2):
                    last = act.activation(aT2[:, 4 * m:4 * m + 4, :], units(pb[3 + m][:, :]), ACT.Copy)
                last.then_inc(s("at_pT"), 1)
                act.wait_ge(s("at_y"), n + 1)
            await_once(act, "boutT_ps")
            act.activation(mixT[:, 4:6, :], pb[0][:, :].rearrange("p (k t) -> p k t", k=2), ACT.Copy)
            act.activation(mixT[:, 6:8, :], pb[1][:, :].rearrange("p (k t) -> p k t", k=2), ACT.Copy).then_inc(once("boutT"), 1)
            act.wait_ge(s("x_mixed"), 4)
            row_rstd(me, h2, 4)
            copies16(9, lambda k: (hT[:, k, :], 1.0))
            await_once(act, "top_neg")
            for t in range(NT):
                last = act.activation(gates[:, t, :], logits[:, t, :], ACT.Exp, bias=rt[:, t:t + 1])
            last.then_inc(once("gate_exp"), 1)
            await_once(act, "gatesT_ps")
            act.activation(gatesT[0:NE, :], pb[2][0:NE, 0:2 * P], ACT.Copy).then_inc(once("gatesT"), 1)
            act.wait_ge(s("gather_ps"), 1)
            act.activation(XT, pb[3][:, :].rearrange("p (k c) -> p k c", k=KC), ACT.Copy).then_inc(s("XT_sb"), 1)
            act.wait_ge(s("rounds_known"), 1)
            rounds = act.value_load(rounds_i[0:1, 0:1], min_val=1, max_val=ROUNDS)
            n_items = act.snap(rounds * NE)
            with act.Fori(0, n_items) as i:
                act.wait_ge(s("g_clamped"), i + 1)
                act.activation(sg, gm, ACT.Sigmoid, scale=1.702).then_inc(s("sig"), 1)
                act.wait_ge(s("gather_ps"), i + 2)
                act.activation(XT, pb[3][:, :].rearrange("p (k c) -> p k c", k=KC), ACT.Copy).then_inc(s("XT_sb"), 1)
                act.wait_ge(s("y_ps"), i + 1)
                act.activation(ysb, pb[2][:, :], ACT.Copy).then_inc(s("y_sb"), 1)
            act.wait_ge(s("x_moe"), 4)
            row_rstd(me, xn3, 5)
            await_once(act, "pT_ps")
            act.activation(pT, pb[4][:, :].rearrange("p (k t) -> p k t", k=2), ACT.Copy).then_inc(once("pT_sb"), 1)
            copies16(10, lambda k: (hT[:, k, :], vec[:, V_PLE + k:V_PLE + k + 1]))
            for u in range(4):
                act.wait_ge(s("ple_ps"), 2 * u + 1)
                act.activation(pl[u], pb[u][:, :], ACT.Exp, scale=-1.0).then_inc(s("ple_exp"), 1)
            act.wait_ge(s("x_ple"), 4)
            row_rstd(me, xn3, 6)

        @block.vector
        def _(dve):
            me = Steps(dve, "dve_steps")
            in_layer = Steps(dve, "dve_layer_steps")
            in_gdn = Steps(dve, "dve_gdn_steps")
            in_diff = Steps(dve, "dve_diff_steps")
            in_dil = Steps(dve, "dve_dil_steps")
            in_moe = Steps(dve, "dve_moe_steps")

            def copies16(n, scale):
                for kp in (1, 3):
                    dve.wait_ge(s("tr_ps"), 4 * n + kp + 1)
                    for kk in range(2):
                        dst, sc = scale(2 * kp + kk)
                        src = pb[kp][:, kk * S:(kk + 1) * S]
                        last = dve.tensor_copy(dst, src) if sc is None else dve.tensor_scalar(dst, src, sc, None, ALU.mult)
                    last.then_inc(s("tr_dve"), 1)

            def normed(dst, n, row=None):
                dve.wait_ge(s("rstd"), n + 1)
                for t in range(NT):
                    if row is None:
                        ins = dve.tensor_scalar(dst[:, t, :], x[:, t, :], rstd[:, t:t + 1], None, ALU.mult)
                    else:
                        ins = dve.scalar_tensor_tensor(dst[:, t, :], x[:, t, :], rstd[:, t:t + 1], row, ALU.mult, ALU.mult)
                    ins.then_inc(s("normed"), 1)

            me.do(dve.memset(small[:, :], EPS))
            me.do(dve.memset(ones[:, :], 1.0))
            me.do(dve.memset(rel[32:33, :], 1.0))
            me.fence()
            me.link(dve.memset(one1, 1.0))
            dve.wait_ge(s("const_in"), 16 * NCONST)
            me.link(dve.tensor_copy(cosb[:, :, 0:1], pos_i[:, :].unsqueeze(2)))
            dve.tensor_scalar(ones[:, 0:1], ones[:, 0:1], 1.0, None, ALU.mult).then_inc(once("ones_set"), 1)
            ang, turn = wk(5)[:, 0:16].rearrange("p (t c) -> p t c", t=NT), wk(5)[:, 16:32].rearrange("p (t c) -> p t c", t=NT)
            me.link(dve.tensor_tensor(ang, cosb[:, :, 0:1].broadcast_to([P, NT, ROPE_HALF]),
                                      inv_freq.unsqueeze(1).broadcast_to([P, NT, ROPE_HALF]), ALU.mult))
            MAGIC = 1.5 * 2.0 ** 23
            TWO_PI = (6.28125, 0.00193500518798828125, 2 * math.pi - 6.28125 - 0.00193500518798828125)
            for dst, quarter in ((sinb, 0.0), (cosb, 0.25)):
                me.link(dve.tensor_scalar(turn, ang, 1.0 / (2 * math.pi), quarter, ALU.mult, ALU.add))
                me.link(dve.tensor_scalar(turn, turn, MAGIC, None, ALU.add))
                me.link(dve.tensor_scalar(turn, turn, MAGIC, None, ALU.subtract))
                me.link(dve.scalar_tensor_tensor(dst[:, :, :], turn, -TWO_PI[0], ang, ALU.mult, ALU.add))
                me.link(dve.scalar_tensor_tensor(dst[:, :, :], turn, -TWO_PI[1], dst[:, :, :], ALU.mult, ALU.add))
                me.link(dve.scalar_tensor_tensor(dst[:, :, :], turn, -TWO_PI[2], dst[:, :, :], ALU.mult, ALU.add))
                if quarter:
                    me.link(dve.tensor_scalar(dst[:, :, :], dst[:, :, :], math.pi / 2, None, ALU.add))
                me.link(dve.tensor_scalar(dst[:, :, :], dst[:, :, :], 3.141592, -3.141592, ALU.min, ALU.max))
            dve.tensor_scalar(sinb[:, :, :], sinb[:, :, :], 1.0, None, ALU.mult).then_inc(once("angles"), 1)
            lam_p = wk(6)
            for l in range(DEPTH):
                lp = rows[:, l * R_N + R_LAM:l * R_N + R_LAM + 256].rearrange("p (a b c) -> p a b c", a=2, b=2)
                me.link(dve.tensor_tensor(lam_p[:, 0:128].rearrange("p (a c) -> p a c", a=2), lp[:, :, 0, :], lp[:, :, 1, :], ALU.mult))
                me.link(dve.tensor_reduce(lam_s[:, 2 * l:2 * l + 2], lam_p[:, 0:128].rearrange("p (a c) -> p a c", a=2), AXX, ALU.add))
                sub = rows[:, l * R_N + R_SUB:l * R_N + R_SUB + P]
                me.link(dve.tensor_scalar(sub, sub, one_lam[:, l:l + 1], None, ALU.mult))
            dve.tensor_scalar(lam_s, lam_s, 1.0, None, ALU.mult).then_inc(once("lam_sums"), 1)
            await_once(dve, "lam_exp")
            lam2 = lam_s.rearrange("p (l a) -> p l a", a=2)
            me.link(dve.tensor_tensor(neg_lam.unsqueeze(2), lam2[:, :, 1:2], lam2[:, :, 0:1], ALU.subtract))
            me.link(dve.tensor_tensor(neg_lam, neg_lam, lam_init, ALU.subtract))
            await_once(dve, "sincos")
            await_once(dve, "vec_sb")
            dve.wait_ge(s("bias_stored"), 16)
            me.link(dve.memset(conv_b[:, :, 0:PAD], 0.0))
            me.link(dve.memset(conv_b[:, :, PAD + S:XC], 0.0))

            with dve.Fori(0, DEPTH) as l:
                in_layer.start(l * (LAYER_STEPS + MERGE_STEPS))
                normed(kb, l)
                copies16(4 * l, lambda k: (hT[:, k, :], vec[:, ds(l * KC + V_NORM + k, 1)]))
                in_layer.do(dve.memset(conv_b[:, 8:CB, 0:PAD], 0.0))
                in_layer.do(dve.memset(conv_b[:, 8:CB, PAD + S:XC], 0.0))
                for u in range(1, 12, 2):
                    dve.wait_ge(s("qkv_ps"), l * 12 + u + 1)
                    dve.tensor_copy(conv_b[:, 2 * u:2 * u + 2, PAD:PAD + S],
                                    pb[u % 4][:, :].rearrange("p (b c) -> p b c", b=2)).then_inc(s("qkv_sb_dve"), 1)
                dve.wait_ge(s("ab_sb"), l + 1)
                z = ab[:, 2:4]
                dt_row = rows[:, ds(l * R_N + R_DT, 16)].rearrange("p (d h) -> p d h", d=2).unsqueeze(2).broadcast_to([P, 2, NT, H])
                in_layer.link(dve.tensor_tensor(z, z, dt_row, ALU.add))
                in_layer.do(dve.tensor_scalar(ab_t[:, 0], z, 0.0, None, ALU.max))
                in_layer.link(dve.tensor_scalar(ab_t[:, 2], z, -1.0, None, ALU.mult))
                dve.tensor_tensor(ab_t[:, 1], z, ab_t[:, 2], ALU.min).then_inc(s("ab_neg"), 1)
                dve.wait_ge(s("ab_exp"), l + 1)
                in_layer.do(dve.tensor_scalar(ab[:, 0:2], ab[:, 0:2], 1.0, None, ALU.add))
                in_layer.link(dve.tensor_tensor(ab_t[:, 0], ab_t[:, 0], ab_t[:, 1], ALU.add))
                in_layer.do(dve.reciprocal(ab[:, 0:2], ab[:, 0:2]))
                in_layer.link(dve.tensor_scalar(ab_t[:, 0], ab_t[:, 0], -1.0, None, ALU.mult))
                dve.tensor_tensor(z, ab_t[:, 0], ea[:, :, :].unsqueeze(2).broadcast_to([P, 2, NT, H]), ALU.mult).then_inc(s("g_sb"), 1)
                for u in range(1, 12, 2):
                    dve.wait_ge(s("seg_ps"), l * 12 + u + 1)
                    dst = (qb, kb, vb)[u // 4]
                    dve.tensor_copy(dst[:, 1, (u // 2 % 2) * NB:(u // 2 % 2 + 1) * NB], pb[u % 4][:, :]).then_inc(s("seg_sb_dve"), 1)
                dve.wait_ge(s("gcum_ps"), l + 1)
                in_layer.link(dve.tensor_copy(gcum[:, :], pb[5][:, 0:32]))
                dve.tensor_tensor(gend[:, :], pb[5][:, 32:64], gcum[:, :], ALU.subtract).then_inc(s("gcum_cp"), 1)
                dve.wait_ge(s("seg_sb_act"), (l + 1) * 6)
                dve.wait_ge(s("seg_sb_dve"), (l + 1) * 6)
                for t4 in (qb, kb):
                    v4 = t4.rearrange("p t (g c) -> p t g c", g=16)
                    x1, x2 = v4[:, :, :, 0:ROPE_HALF], v4[:, :, :, ROPE_HALF:2 * ROPE_HALF]
                    for t in range(NT):
                        cs = cosb[:, t:t + 1, :].broadcast_to([P, 16, ROPE_HALF])
                        sn = sinb[:, t:t + 1, :].broadcast_to([P, 16, ROPE_HALF])
                        in_layer.do(dve.tensor_tensor(rp[0][:, t], x1[:, t], cs, ALU.mult))
                        in_layer.do(dve.tensor_tensor(rp[1][:, t], x2[:, t], sn, ALU.mult))
                        in_layer.do(dve.tensor_tensor(rp[2][:, t], x2[:, t], cs, ALU.mult))
                        in_layer.link(dve.tensor_tensor(rp[3][:, t], x1[:, t], sn, ALU.mult))
                        in_layer.do(dve.tensor_tensor(x1[:, t], rp[0][:, t], rp[1][:, t], ALU.subtract))
                        in_layer.do(dve.tensor_tensor(x2[:, t], rp[2][:, t], rp[3][:, t], ALU.add))
                in_layer.fence()
                dve.nop().then_inc(s("roped"), 1)
                in_layer.ended(LAYER_STEPS)

                with dve.Fori(0, H) as h:
                    n = l * H + h
                    in_gdn.start(n * GDN_STEPS)
                    dve.wait_ge(s("gcum_sb"), l + 1)
                    dve.wait_ge(s("qkv_sb_act"), (l + 1) * 6)
                    dve.wait_ge(s("qkv_sb_dve"), (l + 1) * 6)
                    for j in range(TAPS):
                        for m in range(3):
                            src = conv_in[:, ds(h * XC + (m * H * XC + j), S)]
                            w = conv_wT[:, ds(l * (TAPS * CB) + h + (j * CB + m * H), 1)]
                            dst = c3[:, m * S:(m + 1) * S]
                            if j == 0:
                                ins = dve.tensor_scalar(dst, src, w, None, ALU.mult)
                            else:
                                ins = dve.scalar_tensor_tensor(dst, src, w, dst, ALU.mult, ALU.add)
                            if j < TAPS - 1:
                                in_gdn.do(ins)
                        if j < TAPS - 1:
                            in_gdn.fence()
                    ins.then_inc(s("gd_conv"), 1)
                    dve.wait_ge(s("gd_rows_ps"), n + 1)
                    for u in range(4):
                        ins = dve.tensor_scalar(E[:, u, :], pb[3][:, u * P:(u + 1) * P], gcum[:, ds(h + u * H, 1)], 0.0,
                                                ALU.subtract, ALU.min)
                    ins.then_inc(s("gd_diff"), 1)
                    dve.wait_ge(s("gd_e"), n + 1)
                    in_gdn.link(dve.tensor_scalar(e3, e3, 1.0, None, ALU.add))
                    in_gdn.link(dve.reciprocal(e3, e3))
                    dve.tensor_tensor(c3, c3, e3, ALU.mult).then_inc(s("gd_silu"), 1)
                    dve.wait_ge(s("gd_rn"), n + 1)
                    dve.wait_ge(s("gd_silu"), n + 1)
                    dve.scalar_tensor_tensor(qTh, qTh, P ** -0.5, e3[:, 0:S], ALU.mult, ALU.mult).then_inc(s("gd_qkn"), 1)
                    dve.tensor_tensor(kTh, kTh, e3[:, S:2 * S], ALU.mult).then_inc(s("gd_qkn"), 1)
                    dve.wait_ge(s("gd_kk_ps"), n + 1)
                    dve.wait_ge(s("gd_em"), n + 1)
                    E4 = E.rearrange("p (d t) c -> p d t c", d=2)
                    kk4 = pb[2][:, :].rearrange("p (s t c) -> p s t c", s=2, t=NT)
                    in_gdn.do(dve.tensor_tensor(qkT.rearrange("p (d t) c -> p d t c", d=2), E4,
                                                kk4[:, 1:2].broadcast_to([P, 2, NT, P]), ALU.mult))
                    in_gdn.link(dve.tensor_tensor(E4, E4, kk4[:, 0:1].broadcast_to([P, 2, NT, P]), ALU.mult))
                    dve.tensor_tensor(E, E, units(pb[4][:, :]), ALU.mult).then_inc(s("gd_lt"), 1)
                    dve.wait_ge(s("gd_kv"), n + 1)
                    dve.wait_ge(s("gd_qkn"), 2 * (n + 1))
                    kv4 = kv.rearrange("p (s t) c -> p s t c", s=2)
                    dve.tensor_tensor(vbeta.rearrange("p (d t) c -> p d t c", d=2), kv4[:, 1:2].broadcast_to([P, 2, NT, P]),
                                      bb.rearrange("p (d t) c -> p d t c", d=2), ALU.mult).then_inc(s("gd_vb"), 1)
                    ab_f = ab[:, :, :, :].rearrange("p c t h -> p (c t h)")
                    for d in range(2):
                        second = 1 + d
                        dve.tensor_scalar(kbg[:, d, :], kv[:, 1 - d, :], ab_f[:, ds(h + second * H, 1)],
                                          eg[:, ds(h + second * H, 1)], ALU.mult, ALU.mult).then_inc(s("gd_vb"), 1)
                        dve.tensor_scalar(kend[:, d, :], kv[:, d, :], gend[:, ds(h + 3 * d * H, 1)], None,
                                          ALU.mult).then_inc(s("gd_vb"), 1)
                    dve.wait_ge(s("gd_lvl"), n * LEVELS + 1)
                    dve.tensor_tensor(U, ident.unsqueeze(1).broadcast_to([P, 4, P]), Lv[0], ALU.subtract).then_inc(s("gd_u"), 1)
                    for v in range(1, LEVELS):
                        if v < LEVELS - 1:
                            dve.wait_ge(s("gd_tv_ps"), n * (LEVELS - 2) + v)
                            dve.tensor_tensor(T, T, units(pb[6][:, :]), ALU.subtract).then_inc(s("gd_t"), 1)
                        dve.wait_ge(s("gd_vu_ps"), n * (LEVELS - 1) + v)
                        dve.tensor_tensor(U, U, units(pb[7][:, :]), ALU.subtract).then_inc(s("gd_u"), 1)
                    dve.wait_ge(s("gd_ws_ps"), n + 1)
                    dve.tensor_tensor(us[:, 1:3, :], us[:, 1:3, :], units(pb[3][:, 0:2 * P]), ALU.subtract).then_inc(s("gd_vnew"), 1)
                    dve.wait_ge(s("gd_o_ps"), n + 1)
                    dve.wait_ge(s("gd_qs"), n + 1)
                    for t in range(NT):
                        ins = dve.tensor_tensor(oh[:, t, :], pb[4][:, t * P:(t + 1) * P], qs[:, 1 - t, :], ALU.add)
                    ins.then_inc(s("gd_osum"), 1)
                    dve.wait_ge(s("gd_rs"), n + 1)
                    for t in range(NT):
                        ins = dve.scalar_tensor_tensor(conv_in[:, ds(h * XC + (PAD + t * P), P)], oh[:, t, :], rs_o[:, t:t + 1],
                                                       rows[:, ds(l * R_N + R_GDN, P)], ALU.mult, ALU.mult)
                    ins.then_inc(s("gd_y"), 1)
                    in_gdn.ended(GDN_STEPS)

                with dve.Fori(0, H) as h:
                    n = l * H + h
                    in_diff.start(n * DIFF_STEPS)
                    for m in range(2):
                        dve.wait_ge(s("at_s_ps"), 2 * n + m + 1)
                        in_diff.do(dve.tensor_reduce(mx[:, 2 * m:2 * m + 2], pb[1 + m][:, :].rearrange("p (t k) -> p t k", t=NT), AXX, ALU.max))
                    in_diff.fence()
                    dve.tensor_scalar(nmx, mx, -DIFF_SCALE, None, ALU.mult).then_inc(s("at_max"), 1)
                    dve.wait_ge(s("at_exp"), n + 1)
                    in_diff.link(dve.reciprocal(rsum, ssum))
                    in_diff.link(dve.tensor_scalar(rsum[:, 2:4], rsum[:, 2:4], neg_lam[:, ds(l, 1)], None, ALU.mult))
                    for t in range(NT):
                        in_diff.do(dve.tensor_scalar(am[:, t, :], pm[:, 0, t, :], rsum[:, t:t + 1], None, ALU.mult))
                    in_diff.fence()
                    for t in range(NT):
                        ins = dve.scalar_tensor_tensor(am[:, t, :], pm[:, 1, t, :], rsum[:, 2 + t:3 + t], am[:, t, :], ALU.mult, ALU.add)
                    ins.then_inc(s("at_p"), 1)
                    dve.wait_ge(s("at_rs"), n + 1)
                    for t in range(NT):
                        ins = dve.scalar_tensor_tensor(qb[:, t, ds(h * P, P)], pb[4][:, t * P:(t + 1) * P], rs_o[:, t:t + 1],
                                                       rows[:, ds(l * R_N + R_SUB, P)], ALU.mult, ALU.mult)
                    ins.then_inc(s("at_y"), 1)
                    in_diff.ended(DIFF_STEPS)

                in_layer.start(l * (LAYER_STEPS + MERGE_STEPS) + LAYER_STEPS)
                for u in range(8):
                    g, t, e = u // 2 % 2, u % 2, mg[u % 4]
                    dve.wait_ge(s("z_exp"), l * 8 + u + 1)
                    in_layer.link(dve.tensor_scalar(e, e, 1.0, None, ALU.add))
                    in_layer.link(dve.reciprocal(e, e))
                    in_layer.link(dve.tensor_tensor(e, e, pb[4 + u % 4][:, :], ALU.mult))
                    if u < 4:
                        y = ya[:, 4 * g:4 * g + 4, t, :]
                        dve.tensor_tensor(y, y, units(e), ALU.mult).then_inc(s("z_gated"), 1)
                    else:
                        y = qb[:, t, g * NB:(g + 1) * NB]
                        dve.tensor_tensor(y, y, e, ALU.mult).then_inc(s("z_gated"), 1)
                    if u == 3:
                        copies16(4 * l + 1, lambda k: (yaT[:, k, :], None))
                copies16(4 * l + 2, lambda k: (ybT[:, k, :], None))
                for g in range(2):
                    for t in range(NT):
                        dve.wait_ge(s("merge_exp"), 4 * l + 2 * g + t + 1)
                        dve.wait_ge(s(f"merge_ps{t}"), l * 8 + 4 * g + 4)
                        for j in range(2):
                            in_layer.do(dve.tensor_scalar(mg[4 * t + j], mg[4 * t + j], 1.0, None, ALU.add))
                        in_layer.fence()
                        for j in range(2):
                            in_layer.do(dve.reciprocal(mg[4 * t + j], mg[4 * t + j]))
                        in_layer.fence()
                        for j in range(2):
                            in_layer.do(dve.tensor_tensor(mg[4 * t + j], mg[4 * t + j], pb[4 * t + 1 + 2 * j][:, :], ALU.mult))
                        in_layer.fence()
                        dve.tensor_tensor(qb[:, t, g * NB:(g + 1) * NB], mg[4 * t], mg[4 * t + 1], ALU.add).then_inc(s("merged"), 1)
                copies16(4 * l + 3, lambda k: (mT[:, k, :], None))
                for u in range(4):
                    dve.wait_ge(s("xo_ps"), 4 * l + u + 1)
                    xs = x[:, u % 2, (u // 2) * NB:(u // 2 + 1) * NB]
                    dve.tensor_tensor(xs, xs, pb[4 + u][:, :], ALU.add).then_inc(s("x_added"), 1)
                dve.wait_ge(s("x_added"), 4 * (l + 1))
                in_layer.ended(MERGE_STEPS)

            dve.wait_ge(s("fnorm_in"), 16)
            normed(x, 2, grow_l)
            dve.wait_ge(s("normed"), 2 * DEPTH + 2)
            normed(xn2, 3)
            copies16(8, lambda k: (hT[:, k, :], vec[:, V_MIX + k:V_MIX + k + 1]))
            for u in range(1, 8, 2):
                dve.wait_ge(s("z2_ps"), u + 1)
                dve.tensor_copy(z2[:, u // 2, 1, :], pb[4 + u % 4][:, :]).then_inc(s("z2_sb_dve"), 1)
            with dve.Fori(DEPTH * H, DEPTH * H + H // 2) as n:
                in_dil.start((n - DEPTH * H) * DIL_STEPS)
                for m in range(2):
                    dve.wait_ge(s("at_s_ps"), 2 * n + m + 1)
                    in_dil.do(dve.scalar_tensor_tensor(p2[:, m * NB:(m + 1) * NB], pb[1 + m][:, :], 0.125,
                                                       bias2[:, ds(n * (2 * NB) + (m - 2 * DEPTH * H) * NB, NB)], ALU.mult, ALU.add))
                in_dil.fence()
                in_dil.link(dve.tensor_reduce(mx, p2.rearrange("p (j k) -> p j k", j=4), AXX, ALU.max))
                dve.tensor_scalar(nmx, mx, -1.0, None, ALU.mult).then_inc(s("at_max"), 1)
                dve.wait_ge(s("at_exp"), n + 1)
                for m in range(2):
                    ins = dve.tensor_tensor(p2[:, m * NB:(m + 1) * NB], p2[:, m * NB:(m + 1) * NB], count, ALU.mult)
                ins.then_inc(s("at_p"), 1)
                dve.wait_ge(s("at_p"), n + 1)
                in_dil.link(dve.tensor_reduce(ssum, p2.rearrange("p (j k) -> p j k", j=4), AXX, ALU.add))
                in_dil.link(dve.reciprocal(rsum, ssum))
                dve.wait_ge(s("at_o_ps"), n + 1)
                for t in range(NT):
                    for m in range(2):
                        ins = dve.tensor_scalar(bout[:, ds(n * P + (t * 512 + m * 64 - DEPTH * H * P), 64)], pb[5][:, t * P + m * 64:t * P + (m + 1) * 64],
                                                rsum[:, 2 * m + t:2 * m + t + 1], None, ALU.mult)
                ins.then_inc(s("at_y"), 1)
                in_dil.ended(DIL_STEPS)
            for u in range(4):
                dve.wait_ge(s("xm_ps"), u + 1)
                xs = x[:, u % 2, (u // 2) * NB:(u // 2 + 1) * NB]
                dve.tensor_tensor(xs, xs, pb[4 + u][:, :], ALU.add).then_inc(s("x_mixed"), 1)
            dve.memset(bpad, 0.0).then_inc(s("bpad_zero"), 1)
            dve.memset(e0, 0.0).then_inc(s("bpad_zero"), 1)
            dve.wait_ge(s("bpad_zero"), 2)
            dve.memset(e0[0:1, :], 1.0).then_inc(s("bpad_zero"), 1)
            dve.wait_ge(s("x_mixed"), 4)
            dve.wait_ge(s("ffn_in"), 16 * 6)
            normed(h2, 4, grow)
            copies16(9, lambda k: (hT[:, k, :], None))
            r2 = Steps(dve, "dve_router_steps")
            await_once(dve, "logits_ps")
            r2.link(dve.tensor_tensor(logits, pb[0][:, 0:2 * NE].rearrange("p (t e) -> p t e", t=NT),
                                      brow.unsqueeze(1).broadcast_to([P, NT, NE]), ALU.add))
            for t in range(NT):
                r2.do(dve.max(top8[:, t, :], logits[:, t, :]))
            r2.fence()
            dve.tensor_scalar(rt[:, 0:2].unsqueeze(2), top8[:, :, 0:1], -1.0, None, ALU.mult).then_inc(once("top_neg"), 1)
            for t in range(NT):
                r2.do(dve.tensor_scalar(m_gt[:, t, :], logits[:, t, :], top8[:, t, 3:4], None, ALU.is_gt))
                r2.do(dve.tensor_scalar(m_eq[:, t, :], logits[:, t, :], top8[:, t, 3:4], None, ALU.is_equal))
            r2.fence()
            r2.link(dve.tensor_reduce(rt[:, 2:4], m_gt, AXX, ALU.add))
            r2.link(dve.tensor_scalar(rt[:, 4:6], rt[:, 2:4], -1.0, float(TOPK), ALU.mult, ALU.add))
            src, dst = m_eq, pre0
            for sh in (1, 2, 4, 8, 16):
                r2.do(dve.tensor_copy(dst[:, :, 0:sh], src[:, :, 0:sh]))
                r2.link(dve.tensor_tensor(dst[:, :, sh:NE], src[:, :, sh:NE], src[:, :, 0:NE - sh], ALU.add))
                src, dst = dst, (pre1 if dst is pre0 else pre0)
            for t in range(NT):
                r2.do(dve.scalar_tensor_tensor(msk[:, t, :], src[:, t, :], rt[:, 4 + t:5 + t], m_eq[:, t, :], ALU.is_le, ALU.mult))
            r2.fence()
            dve.tensor_tensor(msk, msk, m_gt, ALU.add).then_inc(once("mask_sb"), 1)
            await_once(dve, "mask_sb")
            await_once(dve, "gate_exp")
            r2.link(dve.tensor_tensor(gates, gates, msk, ALU.mult))
            r2.link(dve.tensor_reduce(rt[:, 6:8], gates, AXX, ALU.add))
            r2.link(dve.reciprocal(rt[:, 8:10], rt[:, 6:8]))
            for t in range(NT):
                ins = dve.tensor_scalar(gates[:, t, :], gates[:, t, :], rt[:, 8 + t:9 + t], None, ALU.mult)
            ins.then_inc(once("gates_sb"), 1)
            await_once(dve, "rank_ps")
            r2.link(dve.scalar_tensor_tensor(ranks, pb[1][:, 0:2 * NE].rearrange("p (t e) -> p t e", t=NT), 1.0, msk, ALU.add, ALU.mult))
            await_once(dve, "gates_sb")
            for r in range(ROUNDS + 1):
                r2.do(dve.tensor_scalar(rkx[:, :, r * NE:(r + 1) * NE], ranks, -1.0 - CAP * r, None, ALU.add))
                r2.do(dve.tensor_copy(gx[:, :, r * NE:(r + 1) * NE], gates))
            r2.link(dve.tensor_reduce(rt[:, 10:11], pb[1][:, 2 * NE:3 * NE], AXX, ALU.max))
            r2.link(dve.tensor_scalar(rt[:, 11:12], rt[:, 10:11], float(CAP), 1.0, ALU.is_gt, ALU.add))
            for r in range(2, ROUNDS):
                r2.link(dve.scalar_tensor_tensor(rt[:, 11:12], rt[:, 10:11], float(CAP * r), rt[:, 11:12], ALU.is_gt, ALU.add))
            for t in range(NT):
                ins = dve.tensor_scalar(P1[:, t, :], iota[:, 0:CAP], rkx[:, t, 0:1], None, ALU.is_equal)
            ins.then_inc(s("onehot"), 1)
            dve.tensor_copy(rounds_i[:, :], rt[:, 11:12]).then_inc(s("rounds_known"), 1)
            dve.wait_ge(s("rounds_known"), 1)
            rounds = dve.value_load(rounds_i[0:1, 0:1], min_val=1, max_val=ROUNDS)
            n_items = dve.snap(rounds * NE)
            NX = (ROUNDS + 1) * NE
            with dve.Fori(0, n_items) as i:
                in_moe.start(i * 2)
                dve.wait_ge(s("gather_ps"), i + 1)
                for t in range(NT):
                    ins = dve.tensor_scalar(Pg[:, t, :], iota, rkx_f[:, ds(i + t * NX, 1)], gx_f[:, ds(i + t * NX, 1)], ALU.is_equal, ALU.mult)
                ins.then_inc(s("onehot_g"), 1)
                for t in range(NT):
                    ins = dve.tensor_scalar(P1[:, t, :], iota[:, 0:CAP], rkx_f[:, ds(i + (t * NX + 1), 1)], None, ALU.is_equal)
                ins.then_inc(s("onehot"), 1)
                dve.wait_ge(s("gate_up_ps"), i + 1)
                dve.tensor_scalar(gm, pb[0][:, :], 7.0, None, ALU.min).then_inc(s("g_clamped"), 1)
                in_moe.link(dve.tensor_scalar(uc, pb[1][:, :], 7.0, -7.0, ALU.min, ALU.max))
                dve.wait_ge(s("g_clamped"), i + 1)
                in_moe.link(dve.scalar_tensor_tensor(uc, uc, 1.0, gm, ALU.add, ALU.mult))
                dve.wait_ge(s("sig"), i + 1)
                dve.tensor_tensor(gm, uc, sg, ALU.mult).then_inc(s("act"), 1)
                dve.wait_ge(s("CT_ps"), i + 1)
                dve.tensor_copy(CT, pb[2][:, 0:2 * P].rearrange("p (t c) -> p t c", t=NT)).then_inc(s("CT_sb"), 1)
                dve.wait_ge(s("actT_ps"), i + 1)
                dve.tensor_copy(actT, pb[3][:, :].rearrange("p (c h t) -> p c h t", c=4, h=2)).then_inc(s("actT_sb"), 1)
                in_moe.ended(2)
                dve.wait_ge(s("combined"), i + 1)
            for u in range(4):
                xs = x[:, u // 2, (u % 2) * NB:(u % 2 + 1) * NB]
                dve.tensor_tensor(xs, xs, pb[4 + u][:, :], ALU.add).then_inc(s("x_moe"), 1)
            dve.wait_ge(s("x_moe"), 4)
            normed(xn3, 5)
            copies16(10, lambda k: (hT[:, k, :], vec[:, V_PLE + k:V_PLE + k + 1]))
            r3 = Steps(dve, "dve_ple_steps")
            for u in range(4):
                dve.wait_ge(s("ple_exp"), u + 1)
                dve.wait_ge(s("ple_ps"), 2 * u + 2)
                r3.link(dve.tensor_scalar(pl[u], pl[u], 1.0, None, ALU.add))
                r3.link(dve.reciprocal(pl[u], pl[u]))
                r3.link(dve.tensor_tensor(pl[u], pl[u], pb[4 + u][:, :], ALU.mult))
                xs = x[:, u % 2, (u // 2) * NB:(u // 2 + 1) * NB]
                dve.tensor_tensor(xs, xs, pl[u], ALU.add).then_inc(s("x_ple"), 1)
            dve.wait_ge(s("x_ple"), 4)
            dve.wait_ge(s("rstd"), 7)
            for t in range(NT):
                dve.scalar_tensor_tensor(x[:, t, :], x[:, t, :], rstd[:, t:t + 1], grow_l, ALU.mult, ALU.mult).then_inc(s("y_final"), 1)

        @block.gpsimd
        def _(pool):
            with pool.Fori(0, DEPTH) as l:
                with pool.Fori(0, H) as h:
                    n = l * H + h
                    pool.wait_ge(s("gcum_sb"), l + 1)
                    ab_u = ab[:, :, :, :].rearrange("p c t h -> p (c t) h")
                    pool.tensor_copy(gb, ab_u[:, 4:8, ds(h, 1)].broadcast_to([P, 4, P])).then_inc(s("gd_gb"), 1)
                    pool.tensor_copy(bb, ab_u[:, 0:4, ds(h, 1)].broadcast_to([P, 4, P])).then_inc(s("gd_gb"), 1)
                    pool.wait_ge(s("gd_ex"), n + 1)
                    E4 = E.rearrange("p (d t) c -> p d t c", d=2)
                    pool.tensor_tensor(E4, E4, tri.unsqueeze(2).broadcast_to([P, 2, NT, P]), ALU.mult).then_inc(s("gd_em"), 1)
                    pool.wait_ge(s("gd_lt"), n + 1)
                    for v in range(LEVELS):
                        if v == 2:
                            pool.wait_ge(s("gd_u"), n * LEVELS + 1)
                        elif v > 2:
                            pool.wait_ge(s("gd_v_ps"), n * LEVELS + v - 1)
                        pool.tensor_tensor(Lv[v % 2].rearrange("p (d t) c -> p d t c", d=2), E4,
                                           lvl[:, v].unsqueeze(2).broadcast_to([P, 2, NT, P]), ALU.mult).then_inc(s("gd_lvl"), 1)
                    pool.wait_ge(s("gd_y"), n + 1)
                with pool.Fori(0, H) as h:
                    n = l * H + h
                    pool.wait_ge(s("roped"), l + 1)
                    pool.tensor_copy(qk_h[:, 0:2, :], qb[:, :, ds(h * P, P)]).then_inc(s("at_qk"), 1)
                    pool.tensor_copy(qk_h[:, 2:4, :], kb[:, :, ds(h * P, P)]).then_inc(s("at_qk"), 1)
                    pool.wait_ge(s("at_y"), n + 1)
            pool.wait_ge(s("z2_sb_act"), 4)
            pool.wait_ge(s("z2_sb_dve"), 4)
            with pool.Fori(DEPTH * H, DEPTH * H + H // 2) as n:
                pool.tensor_copy(q2h[:, 0:2, :], z2[:, 1, :, ds(n * P - DEPTH * H * P, P)]).then_inc(s("at_qk"), 1)
                pool.tensor_copy(q2h[:, 2:4, :], z2[:, 2, :, ds(n * P - DEPTH * H * P, P)]).then_inc(s("at_qk"), 1)
                pool.wait_ge(s("at_y"), n + 1)


_INS = ["x", "positions", "norm_w", "w_in", "conv_w", "a_log", "dt_bias", "gdn_norm_w", "diff_lambda", "diff_subln_w",
        "w_pa", "w_pb", "w_out", "final_norm_w", "p_2", "g_mix_2", "w_in_2", "w_pool_2", "pool_scale_2", "rel_bias_2",
        "w_out_2", "g_ffn_2", "w_router_2", "b_router_2", "w_gate_up_2", "b_gate_up_2", "w_down_2", "b_down_2",
        "g_ple_2", "w_ple_gate_2", "w_ple_proj_2", "g_final_2"]


def kernel(**inputs):
    import concourse.bacc as bacc
    from concourse.bass_utils import run_bass_kernel_spmd

    nc = bacc.Bacc("TRN2", target_bir_lowering=False, num_devices=1)
    arrays = {name: np.ascontiguousarray(inputs[name]) for name in _INS}
    arrays.update(shape_constants())
    aps = {name: nc.dram_tensor(name + "_dram", v.shape, mybir.dt.from_np(v.dtype), kind="ExternalInput").ap()
           for name, v in arrays.items()}
    out = nc.dram_tensor("out_dram", (1, S, D), F32, kind="ExternalOutput").ap()
    block_kernel(nc, aps, out)
    r = run_bass_kernel_spmd(nc, [{name + "_dram": v for name, v in arrays.items()}], core_ids=[0])
    return np.asarray(r.results[0]["out_dram"])
```

```python
import math
from contextlib import ExitStack

import numpy as np
import concourse.bass as bass
from concourse import mybir

F32 = mybir.dt.float32
I32 = mybir.dt.int32
ALU = mybir.AluOpType
ACT = mybir.ActivationFunctionType
AXX = mybir.AxisListType.X

P = 128
S = 256
NT = S // P
D = 1024
KC = D // P
DEPTH = 2
H = 8
NB = 512
CH = 3 * D
CB = CH // P
TAPS = 5
PAD = TAPS // 2
AB = 3 * D
Z_A = AB + 4 * H
Q_B = Z_A + D
Z_B = Q_B + 3 * D
GATES = Z_B + D
LEVELS = 7
EPS = 1e-6
NE = 32
TOPK = 4
CAP = 64
ROUNDS = S // CAP
SLOTS = 6
RING = 5
ROPE_HALF = 8
NEG = -1e30
DIFF_SCALE = 64 ** -0.5

C_ID, C_TRI, C_STRICT, C_IOTA, C_LVL = 0, 128, 384, 512, 640
C_MISC = C_LVL + LEVELS * 2 * P
C_N = C_MISC + 12

V_NORM, V_MIX, V_FFN, V_PLE, V_POOL, V_N = 0, 16, 24, 32, 40, 44

GDN_STEPS = 15
DIFF_STEPS = 6
DIL_STEPS = 5
LAYER_STEPS = 34
MERGE_STEPS = 8


def shape_constants():
    j = np.arange(P)[:, None]
    i = np.arange(P)[None, :]
    c = np.zeros((P, C_N), np.float32)
    c[:, C_ID:C_ID + P] = j == i
    c[:, C_TRI:C_TRI + P] = j <= i
    c[:, C_TRI + P:C_TRI + 2 * P] = j >= i
    c[:, C_STRICT:C_STRICT + P] = j < i
    c[:, C_IOTA:C_IOTA + P] = i % CAP
    for n in range(LEVELS):
        s = 1 << n
        m = ((j // s) % 2 == 0) & ((i // s) % 2 == 1) & (i // (2 * s) == j // (2 * s))
        c[:, C_LVL + (2 * n) * P:C_LVL + (2 * n + 1) * P] = m
        c[:, C_LVL + (2 * n + 1) * P:C_LVL + (2 * n + 2) * P] = m.T
    inv = np.float64(500000.0) ** (-(np.arange(0, 2 * ROPE_HALF, 2) / (2.0 * ROPE_HALF)))
    c[:, C_MISC:C_MISC + ROPE_HALF] = inv.astype(np.float32)
    for l in range(DEPTH):
        lam = 0.8 - 0.6 * math.exp(-0.3 * l)
        c[:, C_MISC + 8 + l] = lam
        c[:, C_MISC + 10 + l] = 1.0 - lam
    band = np.zeros((S, 4, S), np.float32)
    for g, w in enumerate((2, 4, 8, 16)):
        for t in range(S):
            band[max(0, t - w + 1):t + 1, g, t] = np.float32(1.0) / np.float32(min(t + 1, w))
            band[t, g, t] -= 1.0
    q = np.arange(S)[:, None]
    k = np.arange(S)[None, :]
    d = q - k
    count = ((d >= 0) & (d <= 128)).astype(np.float32) + ((d >= 0) & (d % 4 == 0)) + ((d >= 0) & (d % 16 == 0))
    oh = np.zeros((33, 512), np.float32)
    for m in range(512):
        dist = 255 - m
        if dist < 0 or (dist > 128 and dist % 4):
            oh[32, m] = NEG
            continue
        b = dist if dist < 16 else min(31, 16 + int(math.log(dist / 16) / math.log(2048 / 16) * 16))
        oh[b, m] = 1.0
    return {"c_main": c, "c_band": band.reshape(S, 4 * S), "c_count": count.astype(np.float32), "c_bucket": oh}


def block_kernel(nc, a, out):
    ctx = ExitStack()
    with ctx:
        def sb(name, shape, dt=F32):
            return ctx.enter_context(nc.sbuf_tensor(name, shape, dt))

        sems = {}

        def s(name):
            if name not in sems:
                sems[name] = ctx.enter_context(nc.semaphore(name))
            return sems[name]

        ONCE = {
            "pe_once": ("vec_ps", "pool_ps", "pmix_ps", "boutT_ps", "logits_ps", "rank_ps", "gatesT_ps", "pT_ps"),
            "act_once": ("sincos", "vec_sb", "lam_exp", "pooled", "pmixed", "boutT", "gate_exp", "gatesT", "pT_sb"),
            "dve_once": ("ones_set", "angles", "lam_sums", "top_neg", "mask_sb", "gates_sb"),
        }

        def once(signal):
            return next(s(name) for name, signals in ONCE.items() if signal in signals)

        def await_once(eng, signal):
            for name, signals in ONCE.items():
                if signal in signals:
                    eng.wait_ge(s(name), signals.index(signal) + 1)

        class Steps:

            def __init__(self, eng, name):
                self.eng, self.sem, self.base, self.n = eng, s(name), 0, 0

            def start(self, base):
                self.base, self.n = base, 0

            def do(self, ins):
                self.n += 1
                ins.then_inc(self.sem, 1)

            def fence(self):
                self.eng.wait_ge(self.sem, self.base + self.n)

            def link(self, ins):
                self.do(ins)
                self.fence()

            def ended(self, n):
                assert self.n == n, (self.n, n)

        ds = bass.ds

        ring = sb("ring", [P, RING * KC * NB])
        x = sb("x", [P, NT, D])
        hT = sb("hT", [P, KC, S])
        c_main = sb("c_main_sb", [P, C_N])
        ident = c_main[:, C_ID:C_ID + P]
        tri = c_main[:, C_TRI:C_TRI + 2 * P].rearrange("p (d j) -> p d j", d=2)
        strict = c_main[:, C_STRICT:C_STRICT + P]
        iota = c_main[:, C_IOTA:C_IOTA + P]
        lvl = c_main[:, C_LVL:C_MISC].rearrange("p (n d j) -> p n d j", n=LEVELS, d=2)
        inv_freq = c_main[:, C_MISC:C_MISC + 8]
        lam_init = c_main[:, C_MISC + 8:C_MISC + 10]
        one_lam = c_main[:, C_MISC + 10:C_MISC + 12]
        ones = sb("ones", [P, P])
        vec = sb("vec", [P, V_N])
        conv_wT = sb("conv_wT", [P, DEPTH * TAPS * CB])
        small = sb("small", [P, 64])
        eps, one1, ss, rstd = small[:, 0:1], small[:, 1:2], small[:, 4:6], small[:, 6:8]
        st_o, rs_o = small[:, 8:10], small[:, 10:12]
        mx, nmx, ssum, rsum = small[:, 12:16], small[:, 16:20], small[:, 20:24], small[:, 24:28]
        lam_s, neg_lam = small[:, 28:32], small[:, 32:34]
        st_d, rs_d = small[:, 34:36], small[:, 36:38]
        cosb = sb("cosb", [P, NT, ROPE_HALF])
        sinb = sb("sinb", [P, NT, ROPE_HALF])
        wab = sb("wab", [P, DEPTH * KC * 4 * H])
        ab = sb("ab", [P, 4, NT, H])
        ab_t = sb("ab_t", [P, 3, 2, NT, H])
        gcum = sb("gcum", [P, 2 * NT * H])
        eg = sb("eg", [P, 2 * NT * H])
        gend = sb("gend", [P, 2 * NT * H])
        ea = sb("ea", [P, 2, H])
        R_GDN, R_SUB, R_ALOG, R_DT, R_LAM, R_N = 0, 128, 256, 272, 288, 544
        rows = sb("rows", [P, DEPTH * R_N])
        rounds_i = sb("rounds_i", [P, 1], I32)
        rel = sb("rel", [33, H])
        pos_i = sb("pos_i", [P, NT], I32)
        scratch = nc.dram_tensor("bias_scratch", (H, P, NB), F32).ap()
        region = sb("region", [P, 19552 + KC * NB])

        def view(at, n):
            return region[:, at:at + n]

        qb, kb, vb = (view(n * NT * D, NT * D).rearrange("p (t c) -> p t c", t=NT) for n in range(3))
        XC = S + 2 * PAD
        conv_in = view(6144, CB * XC)
        conv_b = conv_in.rearrange("p (b c) -> p b c", b=CB)
        ya = conv_b[:, 0:H, PAD:PAD + S].rearrange("p h (t c) -> p h t c", t=NT)
        sz = conv_b[:, H:CB, PAD:PAD + S].rearrange("p (s h) (a c) -> p h s a c", s=2, a=2)
        yaT = view(NT * D, KC * S).rearrange("p (k t) -> p k t", k=KC)
        ybT = view(2 * NT * D, KC * S).rearrange("p (k t) -> p k t", k=KC)
        mT = view(6144, KC * S).rearrange("p (k t) -> p k t", k=KC)
        W0 = 12384

        def wk(n, k=1):
            return view(W0 + int(n * NB), int(k * NB))

        def units(ap):
            return ap.rearrange("p (u c) -> p u c", c=P)

        c3 = wk(0, 1.5)
        kTh, vTh = c3[:, S:2 * S], c3[:, 2 * S:3 * S]
        q2 = [wk(1.5 + 0.5 * n, 0.5) for n in range(2)]
        e3 = wk(2.5, 1.5)
        gb, bb, vbeta, kk2, Lv0, Lv1, T, U, V = (units(wk(4 + n)) for n in range(9))
        kv = gb
        kbg, kend = kk2[:, 0:2, :], kk2[:, 2:4, :]
        Es = [units(wk(13 + n)) for n in range(2)]
        LTs = [units(wk(15 + n)) for n in range(2)]
        Lv = (Lv0, Lv1)
        us = Lv1
        wT, St = V[:, 0:2, :], V[:, 2:4, :]
        qs, oh = units(e3)[:, 0:2, :], units(e3)[:, 2:4, :]
        qk_h = units(wk(17))
        aT = qk_h
        qkTh = wk(18)
        pm = wk(19, 2).rearrange("p (m t k) -> p m t k", m=2, t=NT)
        mz = wk(21)
        rp = [wk(0.5 * n, 0.5).rearrange("p (t g c) -> p t g c", t=NT, g=16) for n in range(4)]
        mg = [wk(n) for n in range(8)]

        z2 = view(0, 4096).rearrange("p (s t c) -> p s t c", s=4, t=NT)
        xn2 = view(4096, 2048).rearrange("p (t c) -> p t c", t=NT)
        band = view(6144, 2048).rearrange("p (t g c) -> p t g c", t=NT, g=4)
        mixT = view(8192, 2048).rearrange("p (k t) -> p k t", k=KC)
        pooledT = view(10240, 1024)
        count = view(11264, 512)
        wpool = view(11776, 512).rearrange("p (g c) -> p g c", g=4)
        bout = view(12288, 1024)
        bias2 = view(13312, 4096)
        q2h = units(view(17408, 512))
        qkT2 = view(17920, 512)
        aT2 = units(view(18432, 1024))
        p2 = view(4096, 1024)
        h2 = view(0, 2048).rearrange("p (t c) -> p t c", t=NT)
        bpad = view(2048, 2048)
        XT = view(4096, 512).rearrange("p (k c) -> p k c", k=KC)
        gm, uc, sg, ysb = (view(4608 + n * NB, NB) for n in range(4))
        actT = view(6656, 512).rearrange("p (c h t) -> p c h t", c=4, h=2)
        CT, Pg = view(7168, 256).rearrange("p (t c) -> p t c", t=NT), view(7424, 256).rearrange("p (t c) -> p t c", t=NT)
        P1 = view(7680, 128).rearrange("p (t c) -> p t c", t=NT)
        e0 = view(7808, 64)
        wr = view(7872, 256).rearrange("p (k e) -> p k e", k=KC)

        def te(at):
            return view(at, NT * NE).rearrange("p (t e) -> p t e", t=NT)

        logits, m_gt, m_eq, msk, gates, pre0, pre1, ranks = (te(8128 + 64 * n) for n in range(8))
        top8 = view(8640, 16).rearrange("p (t e) -> p t e", t=NT)
        rt = view(8656, 16)
        gatesT = view(8672, 256)
        rkx = view(8928, 320).rearrange("p (t e) -> p t e", t=NT)
        gx = view(9248, 320).rearrange("p (t e) -> p t e", t=NT)
        rkx_f, gx_f = view(8928, 320), view(9248, 320)
        brow = view(9568, 32)
        b_down = view(9600, 1024)
        grow = view(10624, 1024)
        ptok = view(11648, 512).rearrange("p (t c) -> p t c", t=NT)
        pT = view(12160, 512).rearrange("p (k t) -> p k t", k=2)
        pl = [view(12672 + n * NB, NB) for n in range(4)]
        xn3 = view(14720, 2048).rearrange("p (t c) -> p t c", t=NT)
        grow_l = view(16768, 1024)

        pb = [ctx.enter_context(nc.psum_tensor(f"bank{n}", [P, NB], F32)) for n in range(8)]
        block = ctx.enter_context(nc.Block())

        LAYER_TILES, seen = [], [0] * SLOTS
        for pos in range(26):
            slot = -pos % RING
            LAYER_TILES.append((slot, seen[slot]))
            seen[slot] += 1
        PER_LAYER = seen
        MIX_SLOTS = (4, 3, 2, 1, 0, 5)
        LOADED = [DEPTH * n + 1 for n in PER_LAYER]

        def slot_mem(slot):
            return ring[:, slot * KC * NB:(slot + 1) * KC * NB] if slot < RING else view(19552, KC * NB)

        def slot_w(slot):
            return slot_mem(slot).rearrange("p (k n) -> p k n", k=KC)

        def tile_src(l, pos):
            if pos < 6:
                c = pos * NB
            elif pos < 12:
                c = Q_B + (pos - 6) * NB
            elif pos < 16:
                c = (Z_A if pos < 14 else Z_B) + (pos % 2) * NB
            elif pos < 24:
                g, kind = divmod(pos - 16, 4)
                if kind % 2:
                    return a["w_pa" if kind == 1 else "w_pb"][l, :, g * NB:(g + 1) * NB]
                c = GATES + kind // 2 * D + g * NB
            else:
                return a["w_out"][l, :, (pos - 24) * NB:(pos - 23) * NB]
            return a["w_in"][l, :, c:c + NB]

        def tile_read(l, pos):
            if pos < 6:
                return "qkv_ps", l * 12 + 2 * (pos + 1)
            if pos < 12:
                return "seg_ps", l * 12 + 2 * (pos - 5)
            if pos < 16:
                return "z_ps", l * 8 + 2 * (pos - 11)
            if pos < 24:
                return "merge_ps1", l * 8 + pos - 15
            return "xo_ps", l * 4 + 2 * (pos - 23)

        lay = "(k p) n -> p k n"
        NCONST = 7 + DEPTH * 7 + 3

        @block.sync
        def _(sp):
            def load(dst, src, name, **kw):
                sp.dma_start(dst, src, **kw).then_inc(s(name), 16)

            load(c_main[:, :], a["c_main"], "const_in")
            load(x[:, :, :], a["x"][0].rearrange("(t p) c -> p t c", p=P), "const_in")
            load(wk(0)[V_NORM:V_MIX, 0:P], a["norm_w"].rearrange("l (k p) -> (l k) p", p=P), "const_in")
            for row, name in ((V_MIX, "g_mix_2"), (V_FFN, "g_ffn_2"), (V_PLE, "g_ple_2")):
                load(wk(0)[row:row + 8, 0:P], a[name].rearrange("l (k p) -> (l k) p", p=P), "const_in")
            load(wk(0)[V_POOL:V_N, 0:P], a["pool_scale_2"].rearrange("l (k p) -> (l k) p", p=P), "const_in")
            for l in range(DEPTH):
                load(wk(0)[0:TAPS * CB, (1 + l) * P:(2 + l) * P], a["conv_w"][l].rearrange("w (b p) -> (w b) p", p=P), "const_in")
                load(wab[:, l * 256:(l + 1) * 256].rearrange("p (k n) -> p k n", k=KC),
                     a["w_in"][l, :, AB:AB + 4 * H].rearrange(lay, p=P), "const_in")
                for off, n, src in ((R_GDN, P, a["gdn_norm_w"][l:l + 1, :]), (R_SUB, P, a["diff_subln_w"][l:l + 1, :]),
                                    (R_ALOG, 16, a["a_log"][l:l + 1].rearrange("o d h -> o (d h)")),
                                    (R_DT, 16, a["dt_bias"][l:l + 1].rearrange("o d h -> o (d h)")),
                                    (R_LAM, 256, a["diff_lambda"][l:l + 1].rearrange("o d h -> o (d h)"))):
                    load(rows[:, l * R_N + off:l * R_N + off + n], src.broadcast_to([P, n]), "const_in")
            load(rel[0:32, :], a["rel_bias_2"], "const_in")
            load(wk(1)[0:33, :], a["c_bucket"], "const_in")
            load(pos_i[:, :], a["positions"][0].rearrange("(t p) -> p t", p=P), "const_in", allow_slow_non_contiguous=True)

            read = {}

            def load_tile(dst, src, slot, reader):
                if slot in read:
                    sp.wait_ge(s(read[slot][0]), read[slot][1])
                load(dst, src, f"w_in_slot{slot}")
                read[slot] = reader

            for l in range(DEPTH):
                for pos in list(range(26)) if l == 0 else [1, 2, 3, 4, 0] + list(range(5, 26)):
                    slot = LAYER_TILES[pos][0]
                    load_tile(slot_w(slot), tile_src(l, pos).rearrange(lay, p=P), slot, tile_read(l, pos))
                    if l == 0 and pos == 4:
                        sp.wait_ge(s("bias_rows"), H)
                        load(scratch.rearrange("h p n -> p h n"), view(0, H * NB).rearrange("p (h n) -> p h n", h=H), "bias_stored")
            for n in range(4):
                load_tile(slot_w(MIX_SLOTS[n]), a["w_in_2"][0, :, n * NB:(n + 1) * NB].rearrange(lay, p=P), MIX_SLOTS[n],
                          ("z2_ps", 2 * (n + 1)))
            read[5] = ("x_added", 4 * DEPTH)
            for n in range(2):
                load_tile(slot_w(MIX_SLOTS[4 + n]), a["w_out_2"][0, :, n * NB:(n + 1) * NB].rearrange(lay, p=P),
                          MIX_SLOTS[4 + n], ("xm_ps", 2 * (n + 1)))
            sp.wait_ge(s("x_added"), 4 * DEPTH)
            load(grow_l, a["final_norm_w"].rearrange("(o n) -> o n", o=1).broadcast_to([P, D]), "fnorm_in")
            load(band, a["c_band"].rearrange("(t p) (g c) -> p t g c", p=P, g=4), "mix_in")
            load(count.rearrange("p (t c) -> p t c", t=NT), a["c_count"].rearrange("(t p) c -> p t c", p=P), "mix_in")
            load(wpool, a["w_pool_2"][0].rearrange("g p c -> p g c"), "mix_in")
            sp.wait_ge(s("bias_stored"), 16)
            sp.wait_ge(s("normed"), 2 * DEPTH + 2)
            for t in range(NT):
                src = bass.AP(scratch.tensor, 255 - t * P, [[NB - 1, P], [P * NB, H], [1, S]])
                load(bias2.rearrange("p (h t k) -> p h t k", h=H, t=NT)[:, :, t, :], src, "mix_in")

            def expert(e, i):
                for j in range(6):
                    if i is None and j in read:
                        sp.wait_ge(s(read[j][0]), read[j][1])
                    if j < 4:
                        src = gate_up_src[ds(e * D + j * 256, 256), :]
                        dst = slot_mem(j).rearrange("p (k n) -> p k n", k=2)
                    else:
                        src = down_src[ds(e * D + (j - 4) * 512, 512), :]
                        dst = slot_mem(j).rearrange("p (k n) -> p k n", k=4)
                    src = src.rearrange(lay, p=P)
                    if i is not None:
                        sp.wait_ge(s({3: "gate_up_ps", 5: "y_ps"}.get(j, f"w_used{j}")), i)
                    load(dst, src, f"w_in_slot{j}")

            gate_up_src = a["w_gate_up_2"][0].rearrange("e d n -> (e d) n")
            down_src = a["w_down_2"][0].rearrange("e d n -> (e d) n")
            bgu = a["b_gate_up_2"][0]
            expert(0, None)
            sp.wait_ge(s("x_mixed"), 4)
            load(grow, a["g_ffn_2"].broadcast_to([P, D]), "ffn_in")
            load(wr, a["w_router_2"][0].rearrange("(k p) e -> p k e", p=P), "ffn_in")
            load(brow, a["b_router_2"].broadcast_to([P, NE]), "ffn_in")
            load(b_down[0:NE, :], a["b_down_2"][0], "ffn_in")
            load(ptok, a["p_2"][0, 0].rearrange("(t p) c -> p t c", p=P), "ffn_in")
            load(grow_l, a["g_final_2"].rearrange("(o n) -> o n", o=1).broadcast_to([P, D]), "ffn_in")
            sp.wait_ge(s("bpad_zero"), 1)
            load(bpad[0:1, :], bgu[0:1, :], "bias_in")
            sp.wait_ge(s("rounds_known"), 1)
            rounds = sp.value_load(rounds_i[0:1, 0:1], min_val=1, max_val=ROUNDS)
            n_items = sp.snap(rounds * NE)
            with sp.Fori(1, n_items) as i:
                e = sp.snap(i % NE)
                expert(e, i)
                sp.wait_ge(s("gate_up_ps"), i)
                load(bpad[0:1, :], bgu[ds(e, 1), :], "bias_in")
            for n in range(2):
                sp.wait_ge(s(f"w_used{n}"), n_items)
                load(slot_w(n), a["w_ple_gate_2"][0, :, n * NB:(n + 1) * NB].rearrange(lay, p=P), f"w_in_slot{n}")
            sp.wait_ge(s("w_used2"), n_items)
            load(slot_mem(2)[:, 0:2048].rearrange("p (k n) -> p k n", k=2), a["w_ple_proj_2"][0].rearrange(lay, p=P), "w_in_slot2")
            sp.wait_ge(s("y_final"), 2)
            load(out[0].rearrange("(t p) c -> p t c", p=P), x[:, :, :], "stored")
            sp.wait_ge(s("stored"), 16)

        @block.tensor
        def _(pe):
            def w_wait(l, pos):
                slot, k = LAYER_TILES[pos]
                pe.wait_ge(s(f"w_in_slot{slot}"), 16 * (l * PER_LAYER[slot] + k + 1))
                return slot_w(slot)

            def transpose16(src, n):
                for kp in range(4):
                    for kk in range(2):
                        for t in range(NT):
                            last = pe.transpose(pb[kp][:, (2 * kk + t) * P:(2 * kk + t + 1) * P], src(t, 2 * kp + kk), ident)
                    last.then_inc(s("tr_ps"), 1)
                pe.wait_ge(s("tr_act"), 2 * (n + 1))
                pe.wait_ge(s("tr_dve"), 2 * (n + 1))

            def product(dst, lhs, w, n_k=KC):
                for k in range(n_k):
                    mm = pe.matmul(dst, lhs(k), w(k), start=(k == 0), stop=(k == n_k - 1))
                return mm

            def blk(ap):
                return lambda t, k: ap[:, t, k * P:(k + 1) * P]

            pe.wait_ge(s("const_in"), 16 * NCONST)
            await_once(pe, "ones_set")
            pe.transpose(pb[0][:, 0:V_N], wk(0)[0:V_N, 0:P], ident[0:V_N, 0:V_N])
            for l in range(DEPTH):
                last = pe.transpose(pb[1][:, l * P:l * P + TAPS * CB], wk(0)[0:TAPS * CB, (1 + l) * P:(2 + l) * P],
                                    ident[0:TAPS * CB, 0:TAPS * CB])
            last.then_inc(once("vec_ps"), 1)
            for h in range(H):
                if h >= 4:
                    pe.wait_ge(s("bias_rows"), h - 3)
                pe.matmul(pb[4 + h % 4][:, :], rel[:, h:h + 1].broadcast_to([33, P]), wk(1)[0:33, :],
                          start=True, stop=True).then_inc(s("bias_ps"), 1)
            pe.wait_ge(s("bias_rows"), H)
            await_once(pe, "vec_sb")

            with pe.Fori(0, DEPTH) as l:
                pe.wait_ge(s("normed"), 2 * (l + 1))
                transpose16(blk(kb), 4 * l)
                for u in range(12):
                    if u % 2 == 0:
                        w = w_wait(l, u // 2)
                    if u >= 4:
                        pe.wait_ge(s("qkv_sb_act" if u % 2 == 0 else "qkv_sb_dve"), l * 6 + (u - 4) // 2 + 1)
                    for b in range(2):
                        c = (2 * (u % 2) + b) * P
                        mm = product(pb[u % 4][:, b * S:(b + 1) * S], lambda k: w[:, k, c:c + P], lambda k: hT[:, k, :])
                    mm.then_inc(s("qkv_ps"), 1)
                for t in range(NT):
                    mm = product(pb[6][:, t * 32:(t + 1) * 32], lambda k: hT[:, k, t * P:(t + 1) * P],
                                 lambda k: wab[:, ds(l * 256 + k * 32, 32)])
                mm.then_inc(s("ab_ps"), 1)
                for u in range(12):
                    t = u % 2
                    if t == 0:
                        w = w_wait(l, 6 + u // 2)
                    if u >= 4:
                        pe.wait_ge(s("seg_sb_act" if t == 0 else "seg_sb_dve"), l * 6 + (u - 4) // 2 + 1)
                    else:
                        pe.wait_ge(s("qkv_sb_act" if t == 0 else "qkv_sb_dve"), l * 6 + 5 + u // 2)
                    mm = product(pb[u % 4][:, :], lambda k: hT[:, k, t * P:(t + 1) * P], lambda k: w[:, k, :])
                    mm.then_inc(s("seg_ps"), 1)
                pe.wait_ge(s("g_sb"), l + 1)
                for d in range(2):
                    g_d = ab[:, 2 + d, :, :].rearrange("p t h -> p (t h)")
                    pe.matmul(pb[5][:, d * 16:(d + 1) * 16], tri[:, d, :], g_d, start=True, stop=True)
                    mm = pe.matmul(pb[5][:, 32 + d * 16:32 + (d + 1) * 16], ones[:, :], g_d, start=True, stop=True)
                mm.then_inc(s("gcum_ps"), 1)
                def decay_rows(n):
                    pe.wait_ge(s("gd_gb"), 2 * n + 1)
                    for u in range(4):
                        mm = pe.matmul(pb[7][:, u * P:(u + 1) * P], gb[:, u, :], tri[:, u // 2, :], start=True, stop=True)
                    mm.then_inc(s("gd_rows_ps"), 1)

                def beta_rows(n):
                    pe.wait_ge(s("gd_gb"), 2 * n + 2)
                    pe.wait_ge(s("gd_diff"), n + 1)
                    for u in range(4):
                        mm = pe.matmul(pb[7][:, u * P:(u + 1) * P], bb[:, u, :], ident, start=True, stop=True)
                    mm.then_inc(s("gd_brow_ps"), 1)

                def norms(n):
                    pe.wait_ge(s("gd_sq"), n + 1)
                    pe.wait_ge(s("gd_bm"), n + 1)
                    pe.matmul(pb[7][:, :], ones[:, :], e3[:, 0:2 * S], start=True, stop=True).then_inc(s("gd_norm_ps"), 1)

                def kv_rows(n):
                    pe.wait_ge(s("gd_qkn"), 2 * (n + 1))
                    for t in range(NT):
                        pe.transpose(pb[7][:, t * P:(t + 1) * P], kTh[:, t * P:(t + 1) * P], ident)
                        mm = pe.transpose(pb[7][:, (2 + t) * P:(3 + t) * P], vTh[:, t * P:(t + 1) * P], ident)
                    mm.then_inc(s("gd_kv_ps"), 1)

                def gram(n, par):
                    pe.wait_ge(s("gd_kv"), n + 1)
                    for t in range(NT):
                        kt = kTh[:, t * P:(t + 1) * P]
                        pe.matmul(pb[7][:, t * P:(t + 1) * P], kt, kt, start=True, stop=True)
                        mm = pe.matmul(pb[7][:, (2 + t) * P:(3 + t) * P], kt, q2[par][:, t * P:(t + 1) * P], start=True, stop=True)
                    mm.then_inc(s("gd_kk_ps"), 1)

                def z_part(j, t, parts):
                    for k in parts:
                        mm = pe.matmul(pb[3][:, :], hT[:, k, t * P:(t + 1) * P], ring[:, ds(j * (-KC * NB) + (3 * KC + k) * NB, NB)],
                                       start=(k == 0), stop=(k == KC - 1))
                    if parts[-1] == KC - 1:
                        mm.then_inc(s("z_ps"), 1)

                def scores(n):
                    pe.wait_ge(s("at_qkT"), n + 1)
                    for m in range(2):
                        for t in range(NT):
                            mm = pe.matmul(pb[5 + m][:, t * S:(t + 1) * S], qkTh[m * 64:(m + 1) * 64, t * P:(t + 1) * P],
                                           qkTh[m * 64:(m + 1) * 64, S:2 * S], start=True, stop=True)
                        mm.then_inc(s("at_s_ps"), 1)

                def head_step(h, j, par, n, prep=True):
                    pe.wait_ge(s("gd_u"), n * LEVELS + 1)
                    for u in range(4):
                        mm = pe.transpose(pb[0][:, u * P:(u + 1) * P], U[:, u, :], ident)
                    mm.then_inc(s("gd_v_ps"), 1)
                    pe.wait_ge(s("at_qk"), 2 * (n + 1))
                    for i in range(4):
                        mm = pe.transpose(pb[4][:, i * P:(i + 1) * P], qk_h[:, i, :], ident)
                    mm.then_inc(s("at_qkT_ps"), 1)
                    for v in range(1, LEVELS):
                        pe.wait_ge(s("gd_lvl"), n * LEVELS + v + 1)
                        if v == 1:
                            pe.wait_ge(s("gd_vcopy"), n * LEVELS + 1)
                        else:
                            pe.wait_ge(s("gd_t"), n * (LEVELS - 2) + v - 1)
                        for u in range(4):
                            mm = pe.matmul(pb[0][:, u * P:(u + 1) * P], Lv[v % 2][:, u, :], T[:, u, :], start=True, stop=True)
                        mm.then_inc(s("gd_v_ps"), 1)
                        z_part(j, par, [v - 1])
                        pe.wait_ge(s("gd_vcopy"), n * LEVELS + v + 1)
                        pe.wait_ge(s("gd_u"), n * LEVELS + v)
                        if v < LEVELS - 1:
                            for u in range(4):
                                mm = pe.matmul(pb[1][:, u * P:(u + 1) * P], U[:, u, :], V[:, u, :], start=True, stop=True)
                            mm.then_inc(s("gd_tv_ps"), 1)
                        for u in range(4):
                            mm = pe.matmul(pb[2][:, u * P:(u + 1) * P], V[:, u, :], U[:, u, :], start=True, stop=True)
                        mm.then_inc(s("gd_vu_ps"), 1)
                        if v == 2:
                            scores(n)
                        if prep:
                            if v == 1:
                                decay_rows(n + 1)
                            elif v == 3:
                                beta_rows(n + 1)
                            elif v == 5:
                                norms(n + 1)
                            elif v == 6:
                                kv_rows(n + 1)
                    pe.wait_ge(s("gd_u"), (n + 1) * LEVELS)
                    pe.wait_ge(s("gd_vb"), 5 * (n + 1))
                    for u in range(4):
                        pe.matmul(pb[1][:, u * P:(u + 1) * P], U[:, u, :], vbeta[:, u, :], start=True, stop=True)
                    for d in range(2):
                        mm = pe.matmul(pb[2][:, d * P:(d + 1) * P], kbg[:, d, :], U[:, 1 + d, :], start=True, stop=True)
                    mm.then_inc(s("gd_uw_ps"), 1)
                    z_part(j, par, [6])
                    pe.wait_ge(s("gd_uw_sb"), 2 * (n + 1))
                    for d in range(2):
                        mm = pe.matmul(pb[0][:, d * P:(d + 1) * P], kend[:, d, :], us[:, 3 * d, :], start=True, stop=True)
                    mm.then_inc(s("gd_s_ps"), 1)
                    if prep:
                        gram(n + 1, 1 - par)
                    z_part(j, par, [7])
                    pe.wait_ge(s("gd_s_sb"), n + 1)
                    for d in range(2):
                        pe.matmul(pb[1][:, d * P:(d + 1) * P], wT[:, d, :], St[:, d, :], start=True, stop=True)
                        mm = pe.matmul(pb[2][:, d * P:(d + 1) * P], q2[par][:, (1 - d) * P:(2 - d) * P], St[:, d, :],
                                       start=True, stop=True)
                    mm.then_inc(s("gd_ws_ps"), 1)
                    pe.wait_ge(s("at_p"), n + 1)
                    for kt in range(NT):
                        for t in range(NT):
                            mm = pe.transpose(pb[4][:, (kt * 2 + t) * P:(kt * 2 + t + 1) * P], pm[:, 0, t, kt * P:(kt + 1) * P], ident)
                    mm.then_inc(s("at_pT_ps"), 1)
                    pe.wait_ge(s("gd_vnew"), n + 1)
                    for t in range(NT):
                        for d in range(2):
                            mm = pe.matmul(pb[0][:, t * P:(t + 1) * P], Es[par][:, 2 * d + t, :], us[:, 2 * d + t, :],
                                           start=(d == 0), stop=(d == 1))
                    mm.then_inc(s("gd_o_ps"), 1)
                    pe.wait_ge(s("at_pT"), n + 1)
                    for t in range(NT):
                        for kt in range(NT):
                            mm = pe.matmul(pb[5][:, t * P:(t + 1) * P], aT[:, kt * 2 + t, :], vb[:, kt, ds(h * P, P)],
                                           start=(kt == 0), stop=(kt == 1))
                    mm.then_inc(s("at_o_ps"), 1)

                pe.wait_ge(s("seg_sb_act"), (l + 1) * 6)
                pe.wait_ge(s("seg_sb_dve"), (l + 1) * 6)
                for j in range(4):
                    w_wait(l, 12 + j)
                decay_rows(l * H)
                beta_rows(l * H)
                norms(l * H)
                kv_rows(l * H)
                gram(l * H, 0)
                with pe.Fori(0, H // 2 - 1) as j:
                    for par in range(2):
                        head_step(2 * j + par, j, par, l * H + 2 * j + par)
                for par in range(2):
                    head_step(H - 2 + par, H // 2 - 1, par, l * H + H - 2 + par, prep=(par == 0))

                pe.wait_ge(s("z_gated"), l * 8 + 4)
                transpose16(lambda t, k: ya[:, k, t, :], 4 * l + 1)
                pe.wait_ge(s("z_gated"), l * 8 + 8)
                transpose16(blk(qb), 4 * l + 2)
                for g in range(2):
                    if g == 1:
                        pe.wait_ge(s("merged"), 4 * l + 2)
                    for kind in range(4):
                        w = w_wait(l, 16 + 4 * g + kind)
                        src = (hT, yaT, hT, ybT)[kind]
                        for t in range(NT):
                            product(pb[4 * t + kind][:, :], lambda k: src[:, k, t * P:(t + 1) * P],
                                    lambda k: w[:, k, :]).then_inc(s(f"merge_ps{t}"), 1)
                pe.wait_ge(s("merged"), 4 * (l + 1))
                transpose16(blk(qb), 4 * l + 3)
                for u in range(4):
                    t = u % 2
                    if t == 0:
                        w = w_wait(l, 24 + u // 2)
                    product(pb[4 + u][:, :], lambda k: mT[:, k, t * P:(t + 1) * P], lambda k: w[:, k, :]).then_inc(s("xo_ps"), 1)
                pe.wait_ge(s("x_added"), 4 * (l + 1))

            pe.wait_ge(s("normed"), 2 * DEPTH + 4)
            transpose16(blk(xn2), 8)
            for u in range(8):
                t = u % 2
                if t == 0:
                    slot = MIX_SLOTS[u // 2]
                    pe.wait_ge(s(f"w_in_slot{slot}"), 16 * LOADED[slot])
                if u >= 4:
                    pe.wait_ge(s("z2_sb_act" if t == 0 else "z2_sb_dve"), (u - 4) // 2 + 1)
                product(pb[4 + u % 4][:, :], lambda k: hT[:, k, t * P:(t + 1) * P], lambda k: slot_w(slot)[:, k, :]).then_inc(s("z2_ps"), 1)
            pe.wait_ge(s("z2_sb_act"), 4)
            pe.wait_ge(s("z2_sb_dve"), 4)
            pe.wait_ge(s("mix_in"), 16 * 5)
            for g in range(4):
                mm = product(pb[g // 2][:, (g % 2) * S:(g % 2 + 1) * S], lambda t: z2[:, 0, t, g * P:(g + 1) * P],
                             lambda t: band[:, t, g, :], NT)
            mm.then_inc(once("pool_ps"), 1)
            await_once(pe, "pooled")
            for g in range(4):
                mm = pe.matmul(pb[2 + g // 2][:, (g % 2) * S:(g % 2 + 1) * S], wpool[:, g, :], pooledT[:, g * S:(g + 1) * S],
                               start=True, stop=True)
            mm.then_inc(once("pmix_ps"), 1)
            await_once(pe, "pmixed")
            with pe.Fori(DEPTH * H, DEPTH * H + H // 2) as n:
                pe.wait_ge(s("at_qk"), 2 * (n + 1))
                for j in range(4):
                    mm = pe.transpose(pb[0][:, j * P:(j + 1) * P], q2h[:, j, :], ident)
                mm.then_inc(s("at_qkT_ps"), 1)
                pe.wait_ge(s("at_qkT"), n + 1)
                for m in range(2):
                    for t in range(NT):
                        mm = pe.matmul(pb[1 + m][:, t * S:(t + 1) * S], qkT2[m * 64:(m + 1) * 64, t * P:(t + 1) * P],
                                       qkT2[m * 64:(m + 1) * 64, S:2 * S], start=True, stop=True)
                    mm.then_inc(s("at_s_ps"), 1)
                pe.wait_ge(s("at_p"), n + 1)
                for m in range(2):
                    for kt in range(NT):
                        for t in range(NT):
                            c = (kt * 2 + t) * P
                            mm = pe.transpose(pb[3 + m][:, c:c + P], p2[:, m * 512 + t * S + kt * P:m * 512 + t * S + (kt + 1) * P], ident)
                mm.then_inc(s("at_pT_ps"), 1)
                pe.wait_ge(s("at_pT"), n + 1)
                for t in range(NT):
                    for m in range(2):
                        mm = product(pb[5][:, t * P + m * 64:t * P + (m + 1) * 64], lambda kt: aT2[:, m * 4 + kt * 2 + t, :],
                                     lambda kt: z2[:, 3, kt, ds(n * P + (m * 64 - DEPTH * H * P), 64)], NT)
                mm.then_inc(s("at_o_ps"), 1)
                pe.wait_ge(s("at_y"), n + 1)
            for t in range(NT):
                for c in range(4):
                    mm = pe.transpose(pb[c // 2][:, (c % 2) * S + t * P:(c % 2) * S + (t + 1) * P],
                                      bout[:, t * 512 + c * P:t * 512 + (c + 1) * P], ident)
            mm.then_inc(once("boutT_ps"), 1)
            await_once(pe, "boutT")
            for u in range(4):
                t, slot = u % 2, MIX_SLOTS[4 + u // 2]
                if t == 0:
                    pe.wait_ge(s(f"w_in_slot{slot}"), 16 * LOADED[slot])
                product(pb[4 + u][:, :], lambda k: mixT[:, k, t * P:(t + 1) * P], lambda k: slot_w(slot)[:, k, :]).then_inc(s("xm_ps"), 1)

            pe.wait_ge(s("normed"), 2 * DEPTH + 6)
            transpose16(blk(h2), 9)
            pe.wait_ge(s("ffn_in"), 16 * 6)
            for t in range(NT):
                mm = product(pb[0][:, t * NE:(t + 1) * NE], lambda k: hT[:, k, t * P:(t + 1) * P], lambda k: wr[:, k, :])
            mm.then_inc(once("logits_ps"), 1)
            await_once(pe, "mask_sb")
            pe.matmul(pb[1][:, 0:NE], strict, msk[:, 0, :], start=True, stop=True)
            pe.matmul(pb[1][:, NE:2 * NE], strict, msk[:, 1, :], start=True, stop=False)
            pe.matmul(pb[1][:, NE:2 * NE], ones[:, :], msk[:, 0, :], start=False, stop=True)
            pe.matmul(pb[1][:, 2 * NE:3 * NE], ones[:, :], msk[:, 0, :], start=True, stop=False)
            pe.matmul(pb[1][:, 2 * NE:3 * NE], ones[:, :], msk[:, 1, :], start=False, stop=True).then_inc(once("rank_ps"), 1)
            await_once(pe, "gates_sb")
            for t in range(NT):
                mm = pe.transpose(pb[2][0:NE, t * P:(t + 1) * P], gates[:, t, :], ident)
            mm.then_inc(once("gatesT_ps"), 1)
            await_once(pe, "gatesT")
            for t in range(NT):
                for g in range(2):
                    pe.matmul(pb[4 + 2 * t + g][:, :], gatesT[0:NE, t * P:(t + 1) * P], b_down[0:NE, g * NB:(g + 1) * NB],
                              start=True, stop=False, skip_group_check=True)

            def gather():
                for k in range(KC):
                    for t in range(NT):
                        mm = pe.matmul(pb[3][:, k * CAP:(k + 1) * CAP], h2[:, t, k * P:(k + 1) * P], P1[:, t, :],
                                       start=(t == 0), stop=(t == 1))
                mm.then_inc(s("gather_ps"), 1)

            def combine():
                for hf in range(2):
                    for t in range(NT):
                        mm = pe.matmul(pb[4 + 2 * t + hf][:, :], CT[hf * 64:(hf + 1) * 64, t, :], ysb[hf * 64:(hf + 1) * 64, :],
                                       start=False, stop=False, skip_group_check=True)
                mm.then_inc(s("combined"), 1)

            pe.wait_ge(s("onehot"), 1)
            gather()
            pe.wait_ge(s("rounds_known"), 1)
            rounds = pe.value_load(rounds_i[0:1, 0:1], min_val=1, max_val=ROUNDS)
            n_items = pe.snap(rounds * NE)
            with pe.Fori(0, n_items) as i:
                pe.wait_ge(s("XT_sb"), i + 1)
                pe.wait_ge(s("y_sb"), i + 1)
                pe.wait_ge(s("bias_in"), 16 * (i + 1))
                for g in range(2):
                    for hf in range(2):
                        pe.matmul(pb[g][hf * 64:(hf + 1) * 64, :], e0, bpad[:, g * D + hf * NB:g * D + (hf + 1) * NB],
                                  start=True, stop=False)
                for j in range(4):
                    pe.wait_ge(s(f"w_in_slot{j}"), 16 * (LOADED[j] + 1 + i))
                    wj = slot_mem(j).rearrange("p (k n) -> p k n", k=2)
                    for kk in range(2):
                        for g in range(2):
                            for hf in range(2):
                                c = g * D + hf * NB
                                mm = pe.matmul(pb[g][hf * 64:(hf + 1) * 64, :], XT[:, 2 * j + kk, :], wj[:, kk, c:c + NB],
                                               start=False, stop=(j == 3 and kk == 1))
                    mm.then_inc(s("gate_up_ps" if j == 3 else f"w_used{j}"), 1)
                combine()
                pe.wait_ge(s("onehot"), i + 2)
                gather()
                pe.wait_ge(s("onehot_g"), i + 1)
                for t in range(NT):
                    mm = pe.transpose(pb[2][:, t * P:(t + 1) * P], Pg[:, t, :], ident)
                mm.then_inc(s("CT_ps"), 1)
                pe.wait_ge(s("act"), i + 1)
                pe.wait_ge(s("XT_sb"), i + 2)
                for c in range(4):
                    mm = pe.transpose(pb[3][:, c * P:(c + 1) * P], gm[:, c * P:(c + 1) * P], ident)
                mm.then_inc(s("actT_ps"), 1)
                pe.wait_ge(s("CT_sb"), i + 1)
                pe.wait_ge(s("actT_sb"), i + 1)
                for j in range(2):
                    pe.wait_ge(s(f"w_in_slot{4 + j}"), 16 * (LOADED[4 + j] + 1 + i))
                    wj = slot_mem(4 + j).rearrange("p (k n) -> p k n", k=4)
                    for c in range(4):
                        for hf in range(2):
                            mm = pe.matmul(pb[2][hf * 64:(hf + 1) * 64, :], actT[:, c, j, :], wj[:, c, hf * NB:(hf + 1) * NB],
                                           start=(j == 0 and c == 0), stop=(j == 1 and c == 3))
                    mm.then_inc(s("y_ps" if j == 1 else "w_used4"), 1)
            pe.wait_ge(s("y_sb"), n_items + 1)
            combine()

            pe.wait_ge(s("x_moe"), 4)
            for t in range(NT):
                for k in range(2):
                    mm = pe.transpose(pb[4][:, k * S + t * P:k * S + (t + 1) * P], ptok[:, t, k * P:(k + 1) * P], ident)
            mm.then_inc(once("pT_ps"), 1)
            pe.wait_ge(s("normed"), 2 * DEPTH + 8)
            transpose16(blk(xn3), 10)
            await_once(pe, "pT_sb")
            pe.wait_ge(s("w_in_slot2"), 16 * (LOADED[2] + 1 + n_items))
            wp = slot_mem(2)[:, 0:2048].rearrange("p (k n) -> p k n", k=2)
            for g in range(2):
                pe.wait_ge(s(f"w_in_slot{g}"), 16 * (LOADED[g] + 1 + n_items))
                for t in range(NT):
                    product(pb[2 * g + t][:, :], lambda k: hT[:, k, t * P:(t + 1) * P], lambda k: slot_w(g)[:, k, :]).then_inc(s("ple_ps"), 1)
                    product(pb[4 + 2 * g + t][:, :], lambda k: pT[:, k, t * P:(t + 1) * P],
                            lambda k: wp[:, k, g * NB:(g + 1) * NB], 2).then_inc(s("ple_ps"), 1)

        @block.scalar
        def _(act):
            me = Steps(act, "act_steps")
            in_layer = Steps(act, "act_layer_steps")
            in_gdn = Steps(act, "act_prep_steps")
            in_head = Steps(act, "act_head_steps")

            def copies16(n, scale):
                for j, kp in enumerate((0, 2)):
                    act.wait_ge(s("tr_ps"), 4 * n + kp + 1)
                    for kk in range(2):
                        k = 2 * kp + kk
                        dst, sc = scale(k)
                        last = act.activation(dst, pb[kp][:, kk * S:(kk + 1) * S], ACT.Copy, scale=sc)
                    last.then_inc(s("tr_act"), 1)

            def row_rstd(steps, junk, n):
                for t in range(NT):
                    steps.do(act.activation(junk[:, t, :], x[:, t, :], ACT.Square, accum_out=ss[:, t:t + 1]))
                steps.fence()
                steps.link(act.activation(rstd, ss, ACT.Ln, bias=eps, scale=1.0 / D))
                act.activation(rstd, rstd, ACT.Exp, scale=-0.5).then_inc(s("rstd"), 1)

            def hT_with(at):
                return lambda k: (hT[:, k, :], vec[:, at(k)])

            await_once(act, "angles")
            act.activation(cosb[:, :, :], cosb[:, :, :], ACT.Sin)
            act.activation(sinb[:, :, :], sinb[:, :, :], ACT.Sin).then_inc(once("sincos"), 1)
            await_once(act, "vec_ps")
            act.activation(vec[:, :], pb[0][:, 0:V_N], ACT.Copy)
            act.activation(conv_wT[:, 0:TAPS * CB], pb[1][:, 0:TAPS * CB], ACT.Copy)
            act.activation(conv_wT[:, TAPS * CB:2 * TAPS * CB], pb[1][:, P:P + TAPS * CB], ACT.Copy).then_inc(once("vec_sb"), 1)
            for h in range(H):
                act.wait_ge(s("bias_ps"), h + 1)
                act.activation(view(h * NB, NB), pb[4 + h % 4][:, :], ACT.Copy).then_inc(s("bias_rows"), 1)
            await_once(act, "lam_sums")
            act.activation(lam_s, lam_s, ACT.Exp).then_inc(once("lam_exp"), 1)
            await_once(act, "vec_sb")
            act.wait_ge(s("bias_stored"), 16)

            with act.Fori(0, DEPTH) as l:
                in_layer.start(l * 6)
                row_rstd(in_layer, kb, l)
                copies16(4 * l, lambda k: (hT[:, k, :], vec[:, ds(l * KC + V_NORM + k, 1)]))
                for u in range(0, 12, 2):
                    act.wait_ge(s("qkv_ps"), l * 12 + u + 1)
                    act.activation(conv_b[:, 2 * u:2 * u + 2, PAD:PAD + S], pb[u % 4][:, :].rearrange("p (b c) -> p b c", b=2),
                                   ACT.Copy).then_inc(s("qkv_sb_act"), 1)
                act.wait_ge(s("ab_ps"), l + 1)
                for t in range(NT):
                    last = act.activation(ab[:, :, t, :], pb[6][:, t * 32:(t + 1) * 32].rearrange("p (c h) -> p c h", c=4), ACT.Copy)
                last.then_inc(s("ab_sb"), 1)
                act.wait_ge(s("ab_neg"), l + 1)
                in_layer.link(act.activation(ab_t[:, 1], ab_t[:, 1], ACT.Exp))
                in_layer.do(act.activation(ab_t[:, 1], ab_t[:, 1], ACT.Ln, bias=one1))
                in_layer.do(act.activation(ab[:, 0:2], ab[:, 0:2], ACT.Exp, scale=-1.0))
                act.activation(ea[:, :, :], rows[:, ds(l * R_N + R_ALOG, 16)].rearrange("p (d h) -> p d h", d=2), ACT.Exp).then_inc(s("ab_exp"), 1)
                for u in range(0, 12, 2):
                    act.wait_ge(s("seg_ps"), l * 12 + u + 1)
                    dst = (qb, kb, vb)[u // 4]
                    act.activation(dst[:, 0, (u // 2 % 2) * NB:(u // 2 % 2 + 1) * NB], pb[u % 4][:, :], ACT.Copy).then_inc(s("seg_sb_act"), 1)
                act.wait_ge(s("gcum_cp"), l + 1)
                act.activation(eg[:, :], gcum[:, :], ACT.Exp)
                act.activation(gend[:, :], gend[:, :], ACT.Exp).then_inc(s("gcum_sb"), 1)
                in_layer.ended(6)

                def silu_exps(n):
                    act.wait_ge(s("gd_conv"), n + 1)
                    in_gdn.link(act.activation(e3, e3, ACT.Exp, scale=-1.0))
                    in_gdn.link(act.activation(e3, e3, ACT.Ln, bias=one1))
                    act.activation(e3, e3, ACT.Exp, scale=-1.0).then_inc(s("gd_e"), 1)

                def decay_exp(n, par):
                    act.wait_ge(s("gd_diff"), n + 1)
                    act.activation(Es[par], Es[par], ACT.Exp).then_inc(s("gd_ex"), 1)

                def squares(n):
                    act.wait_ge(s("gd_silu"), n + 1)
                    act.activation(e3[:, 0:2 * S], c3[:, 0:2 * S], ACT.Square).then_inc(s("gd_sq"), 1)

                def inverse_norms(n):
                    act.wait_ge(s("gd_norm_ps"), n + 1)
                    in_gdn.link(act.activation(e3[:, 0:2 * S], pb[7][:, :], ACT.Ln, bias=eps))
                    act.activation(e3[:, 0:2 * S], e3[:, 0:2 * S], ACT.Exp, scale=-0.5).then_inc(s("gd_rn"), 1)

                def kv_copy(n):
                    act.wait_ge(s("gd_kv_ps"), n + 1)
                    act.activation(kv, units(pb[7][:, :]), ACT.Copy).then_inc(s("gd_kv"), 1)

                def head_step(h, par, n, prep=True):
                    in_head.start(n * 6)
                    for v in range(LEVELS):
                        act.wait_ge(s("gd_v_ps"), n * LEVELS + v + 1)
                        act.activation(T if v == 0 else V, units(pb[0][:, :]), ACT.Copy).then_inc(s("gd_vcopy"), 1)
                        if v == 0:
                            act.wait_ge(s("at_qkT_ps"), n + 1)
                            act.activation(qkTh, pb[4][:, :], ACT.Copy).then_inc(s("at_qkT"), 1)
                        if prep:
                            if v == 0:
                                in_gdn.start((n + 1) * 3)
                            elif v == 2:
                                decay_exp(n + 1, 1 - par)
                            elif v == 3:
                                silu_exps(n + 1)
                            elif v == 4:
                                squares(n + 1)
                            elif v == 6:
                                inverse_norms(n + 1)
                        if v == 5:
                            act.wait_ge(s("at_max"), n + 1)
                            for m in range(2):
                                for t in range(NT):
                                    i = 2 * m + t
                                    last = act.activation(pm[:, m, t, :], pb[5 + m][:, t * S:(t + 1) * S], ACT.Exp,
                                                          bias=nmx[:, i:i + 1], scale=DIFF_SCALE, accum_out=ssum[:, i:i + 1])
                            last.then_inc(s("at_exp"), 1)
                    if prep:
                        kv_copy(n + 1)
                    act.wait_ge(s("gd_uw_ps"), n + 1)
                    act.activation(us, units(pb[1][:, :]), ACT.Copy).then_inc(s("gd_uw_sb"), 1)
                    act.activation(wT, units(pb[2][:, 0:2 * P]), ACT.Copy).then_inc(s("gd_uw_sb"), 1)
                    act.wait_ge(s("gd_s_ps"), n + 1)
                    act.activation(St, units(pb[0][:, 0:2 * P]), ACT.Copy).then_inc(s("gd_s_sb"), 1)
                    act.wait_ge(s("gd_ws_ps"), n + 1)
                    for d in range(2):
                        last = act.activation(qs[:, d, :], pb[2][:, d * P:(d + 1) * P], ACT.Copy, scale=eg[:, ds(h + (1 + d) * H, 1)])
                    last.then_inc(s("gd_qs"), 1)
                    act.wait_ge(s("at_pT_ps"), n + 1)
                    act.activation(aT, units(pb[4][:, :]), ACT.Copy).then_inc(s("at_pT"), 1)
                    act.wait_ge(s("gd_osum"), n + 1)
                    for t in range(NT):
                        in_head.do(act.activation(qs[:, t, :], oh[:, t, :], ACT.Square, accum_out=st_o[:, t:t + 1]))
                    in_head.fence()
                    in_head.link(act.activation(rs_o, st_o, ACT.Ln, bias=eps, scale=1.0 / P))
                    act.activation(rs_o, rs_o, ACT.Exp, scale=-0.5).then_inc(s("gd_rs"), 1)
                    act.wait_ge(s("z_low"), n + 1)
                    in_head.link(act.activation(mz, mz, ACT.Exp, scale=-1.0))
                    in_head.link(act.activation(mz, mz, ACT.Ln, bias=one1))
                    act.activation(mz, mz, ACT.Exp, scale=-1.0).then_inc(s("z_exp"), 1)
                    act.wait_ge(s("at_o_ps"), n + 1)
                    for t in range(NT):
                        last = act.activation(pm[:, 1, t, 0:P], pb[5][:, t * P:(t + 1) * P], ACT.Square, accum_out=st_d[:, t:t + 1])
                    last.then_inc(s("at_ss"), 1)
                    act.wait_ge(s("at_ss"), n + 1)
                    in_head.link(act.activation(rs_d, st_d, ACT.Ln, bias=eps, scale=1.0 / P))
                    act.activation(rs_d, rs_d, ACT.Exp, scale=-0.5).then_inc(s("at_rs"), 1)
                    in_head.ended(6)

                in_gdn.start(l * H * 3)
                decay_exp(l * H, 0)
                silu_exps(l * H)
                squares(l * H)
                inverse_norms(l * H)
                kv_copy(l * H)
                in_gdn.ended(3)
                with act.Fori(0, H // 2 - 1) as j:
                    for par in range(2):
                        head_step(2 * j + par, par, l * H + 2 * j + par)
                for par in range(2):
                    head_step(H - 2 + par, par, l * H + H - 2 + par, prep=(par == 0))

                copies16(4 * l + 1, lambda k: (yaT[:, k, :], 1.0))
                copies16(4 * l + 2, lambda k: (ybT[:, k, :], 1.0))
                in_merge = Steps(act, "act_merge_steps")
                in_merge.start(l * 16)
                for g in range(2):
                    for t in range(NT):
                        act.wait_ge(s("gates_low"), 4 * l + 2 * g + t + 1)
                        for m in range(2):
                            in_merge.do(act.activation(mg[4 * t + m], mg[4 * t + m], ACT.Exp, scale=-1.0))
                        in_merge.fence()
                        for m in range(2):
                            in_merge.do(act.activation(mg[4 * t + m], mg[4 * t + m], ACT.Ln, bias=one1))
                        in_merge.fence()
                        for m in range(2):
                            last = act.activation(mg[4 * t + m], mg[4 * t + m], ACT.Exp, scale=-1.0)
                        last.then_inc(s("merge_exp"), 1)
                in_merge.ended(16)
                copies16(4 * l + 3, lambda k: (mT[:, k, :], 1.0))
                act.wait_ge(s("x_added"), 4 * (l + 1))

            me.start(0)
            row_rstd(me, xn2, 2)
            act.wait_ge(s("normed"), 2 * DEPTH + 2)
            row_rstd(me, xn2, 3)
            copies16(8, lambda k: (hT[:, k, :], vec[:, V_MIX + k:V_MIX + k + 1]))
            for u in range(0, 8, 2):
                act.wait_ge(s("z2_ps"), u + 1)
                act.activation(z2[:, u // 2, 0, :], pb[4 + u % 4][:, :], ACT.Copy).then_inc(s("z2_sb_act"), 1)
            await_once(act, "pool_ps")
            act.activation(pooledT[:, 0:NB], pb[0][:, :], ACT.Copy)
            act.activation(pooledT[:, NB:2 * NB], pb[1][:, :], ACT.Copy).then_inc(once("pooled"), 1)
            await_once(act, "pmix_ps")
            for g in range(4):
                last = act.activation(mixT[:, g, :], pb[2 + g // 2][:, (g % 2) * S:(g % 2 + 1) * S], ACT.Copy,
                                      scale=vec[:, V_POOL + g:V_POOL + g + 1])
            last.then_inc(once("pmixed"), 1)
            with act.Fori(DEPTH * H, DEPTH * H + H // 2) as n:
                act.wait_ge(s("at_qkT_ps"), n + 1)
                act.activation(qkT2, pb[0][:, :], ACT.Copy).then_inc(s("at_qkT"), 1)
                act.wait_ge(s("at_max"), n + 1)
                for j in range(4):
                    last = act.activation(p2[:, j * S:(j + 1) * S], p2[:, j * S:(j + 1) * S], ACT.Exp, bias=nmx[:, j:j + 1])
                last.then_inc(s("at_exp"), 1)
                act.wait_ge(s("at_pT_ps"), n + 1)
                for m in range(2):
                    last = act.activation(aT2[:, 4 * m:4 * m + 4, :], units(pb[3 + m][:, :]), ACT.Copy)
                last.then_inc(s("at_pT"), 1)
                act.wait_ge(s("at_y"), n + 1)
            await_once(act, "boutT_ps")
            act.activation(mixT[:, 4:6, :], pb[0][:, :].rearrange("p (k t) -> p k t", k=2), ACT.Copy)
            act.activation(mixT[:, 6:8, :], pb[1][:, :].rearrange("p (k t) -> p k t", k=2), ACT.Copy).then_inc(once("boutT"), 1)
            act.wait_ge(s("x_mixed"), 4)
            row_rstd(me, h2, 4)
            copies16(9, lambda k: (hT[:, k, :], 1.0))
            await_once(act, "top_neg")
            for t in range(NT):
                last = act.activation(gates[:, t, :], logits[:, t, :], ACT.Exp, bias=rt[:, t:t + 1])
            last.then_inc(once("gate_exp"), 1)
            await_once(act, "gatesT_ps")
            act.activation(gatesT[0:NE, :], pb[2][0:NE, 0:2 * P], ACT.Copy).then_inc(once("gatesT"), 1)
            act.wait_ge(s("gather_ps"), 1)
            act.activation(XT, pb[3][:, :].rearrange("p (k c) -> p k c", k=KC), ACT.Copy).then_inc(s("XT_sb"), 1)
            act.wait_ge(s("rounds_known"), 1)
            rounds = act.value_load(rounds_i[0:1, 0:1], min_val=1, max_val=ROUNDS)
            n_items = act.snap(rounds * NE)
            with act.Fori(0, n_items) as i:
                act.wait_ge(s("g_clamped"), i + 1)
                act.activation(sg, gm, ACT.Sigmoid, scale=1.702).then_inc(s("sig"), 1)
                act.wait_ge(s("gather_ps"), i + 2)
                act.activation(XT, pb[3][:, :].rearrange("p (k c) -> p k c", k=KC), ACT.Copy).then_inc(s("XT_sb"), 1)
                act.wait_ge(s("y_ps"), i + 1)
                act.activation(ysb, pb[2][:, :], ACT.Copy).then_inc(s("y_sb"), 1)
            act.wait_ge(s("x_moe"), 4)
            row_rstd(me, xn3, 5)
            await_once(act, "pT_ps")
            act.activation(pT, pb[4][:, :].rearrange("p (k t) -> p k t", k=2), ACT.Copy).then_inc(once("pT_sb"), 1)
            copies16(10, lambda k: (hT[:, k, :], vec[:, V_PLE + k:V_PLE + k + 1]))
            for u in range(4):
                act.wait_ge(s("ple_ps"), 2 * u + 1)
                act.activation(pl[u], pb[u][:, :], ACT.Exp, scale=-1.0).then_inc(s("ple_exp"), 1)
            act.wait_ge(s("x_ple"), 4)
            row_rstd(me, xn3, 6)

        @block.vector
        def _(dve):
            me = Steps(dve, "dve_steps")
            in_layer = Steps(dve, "dve_layer_steps")
            in_gdn = Steps(dve, "dve_gdn_steps")
            in_diff = Steps(dve, "dve_diff_steps")
            in_dil = Steps(dve, "dve_dil_steps")
            in_moe = Steps(dve, "dve_moe_steps")

            def copies16(n, scale):
                for kp in (1, 3):
                    dve.wait_ge(s("tr_ps"), 4 * n + kp + 1)
                    for kk in range(2):
                        dst, sc = scale(2 * kp + kk)
                        src = pb[kp][:, kk * S:(kk + 1) * S]
                        last = dve.tensor_copy(dst, src) if sc is None else dve.tensor_scalar(dst, src, sc, None, ALU.mult)
                    last.then_inc(s("tr_dve"), 1)

            def normed(dst, n, row=None):
                dve.wait_ge(s("rstd"), n + 1)
                for t in range(NT):
                    if row is None:
                        ins = dve.tensor_scalar(dst[:, t, :], x[:, t, :], rstd[:, t:t + 1], None, ALU.mult)
                    else:
                        ins = dve.scalar_tensor_tensor(dst[:, t, :], x[:, t, :], rstd[:, t:t + 1], row, ALU.mult, ALU.mult)
                    ins.then_inc(s("normed"), 1)

            me.do(dve.memset(small[:, :], EPS))
            me.do(dve.memset(ones[:, :], 1.0))
            me.do(dve.memset(rel[32:33, :], 1.0))
            me.fence()
            me.link(dve.memset(one1, 1.0))
            dve.wait_ge(s("const_in"), 16 * NCONST)
            me.link(dve.tensor_copy(cosb[:, :, 0:1], pos_i[:, :].unsqueeze(2)))
            dve.tensor_scalar(ones[:, 0:1], ones[:, 0:1], 1.0, None, ALU.mult).then_inc(once("ones_set"), 1)
            ang, turn = wk(5)[:, 0:16].rearrange("p (t c) -> p t c", t=NT), wk(5)[:, 16:32].rearrange("p (t c) -> p t c", t=NT)
            me.link(dve.tensor_tensor(ang, cosb[:, :, 0:1].broadcast_to([P, NT, ROPE_HALF]),
                                      inv_freq.unsqueeze(1).broadcast_to([P, NT, ROPE_HALF]), ALU.mult))
            MAGIC = 1.5 * 2.0 ** 23
            TWO_PI = (6.28125, 0.00193500518798828125, 2 * math.pi - 6.28125 - 0.00193500518798828125)
            for dst, quarter in ((sinb, 0.0), (cosb, 0.25)):
                me.link(dve.tensor_scalar(turn, ang, 1.0 / (2 * math.pi), quarter, ALU.mult, ALU.add))
                me.link(dve.tensor_scalar(turn, turn, MAGIC, None, ALU.add))
                me.link(dve.tensor_scalar(turn, turn, MAGIC, None, ALU.subtract))
                me.link(dve.scalar_tensor_tensor(dst[:, :, :], turn, -TWO_PI[0], ang, ALU.mult, ALU.add))
                me.link(dve.scalar_tensor_tensor(dst[:, :, :], turn, -TWO_PI[1], dst[:, :, :], ALU.mult, ALU.add))
                me.link(dve.scalar_tensor_tensor(dst[:, :, :], turn, -TWO_PI[2], dst[:, :, :], ALU.mult, ALU.add))
                if quarter:
                    me.link(dve.tensor_scalar(dst[:, :, :], dst[:, :, :], math.pi / 2, None, ALU.add))
                me.link(dve.tensor_scalar(dst[:, :, :], dst[:, :, :], 3.141592, -3.141592, ALU.min, ALU.max))
            dve.tensor_scalar(sinb[:, :, :], sinb[:, :, :], 1.0, None, ALU.mult).then_inc(once("angles"), 1)
            lam_p = wk(6)
            for l in range(DEPTH):
                lp = rows[:, l * R_N + R_LAM:l * R_N + R_LAM + 256].rearrange("p (a b c) -> p a b c", a=2, b=2)
                me.link(dve.tensor_tensor(lam_p[:, 0:128].rearrange("p (a c) -> p a c", a=2), lp[:, :, 0, :], lp[:, :, 1, :], ALU.mult))
                me.link(dve.tensor_reduce(lam_s[:, 2 * l:2 * l + 2], lam_p[:, 0:128].rearrange("p (a c) -> p a c", a=2), AXX, ALU.add))
                sub = rows[:, l * R_N + R_SUB:l * R_N + R_SUB + P]
                me.link(dve.tensor_scalar(sub, sub, one_lam[:, l:l + 1], None, ALU.mult))
            dve.tensor_scalar(lam_s, lam_s, 1.0, None, ALU.mult).then_inc(once("lam_sums"), 1)
            await_once(dve, "lam_exp")
            lam2 = lam_s.rearrange("p (l a) -> p l a", a=2)
            me.link(dve.tensor_tensor(neg_lam.unsqueeze(2), lam2[:, :, 1:2], lam2[:, :, 0:1], ALU.subtract))
            me.link(dve.tensor_tensor(neg_lam, neg_lam, lam_init, ALU.subtract))
            await_once(dve, "sincos")
            await_once(dve, "vec_sb")
            dve.wait_ge(s("bias_stored"), 16)
            me.link(dve.memset(conv_b[:, :, 0:PAD], 0.0))
            me.link(dve.memset(conv_b[:, :, PAD + S:XC], 0.0))

            with dve.Fori(0, DEPTH) as l:
                in_layer.start(l * (LAYER_STEPS + MERGE_STEPS))
                normed(kb, l)
                copies16(4 * l, lambda k: (hT[:, k, :], vec[:, ds(l * KC + V_NORM + k, 1)]))
                in_layer.do(dve.memset(conv_b[:, 0:H, 0:PAD], 0.0))
                in_layer.do(dve.memset(conv_b[:, 0:H, PAD + S:XC], 0.0))
                for u in range(1, 12, 2):
                    dve.wait_ge(s("qkv_ps"), l * 12 + u + 1)
                    dve.tensor_copy(conv_b[:, 2 * u:2 * u + 2, PAD:PAD + S],
                                    pb[u % 4][:, :].rearrange("p (b c) -> p b c", b=2)).then_inc(s("qkv_sb_dve"), 1)
                dve.wait_ge(s("ab_sb"), l + 1)
                z = ab[:, 2:4]
                dt_row = rows[:, ds(l * R_N + R_DT, 16)].rearrange("p (d h) -> p d h", d=2).unsqueeze(2).broadcast_to([P, 2, NT, H])
                in_layer.link(dve.tensor_tensor(z, z, dt_row, ALU.add))
                in_layer.do(dve.tensor_scalar(ab_t[:, 0], z, 0.0, None, ALU.max))
                in_layer.link(dve.tensor_scalar(ab_t[:, 2], z, -1.0, None, ALU.mult))
                dve.tensor_tensor(ab_t[:, 1], z, ab_t[:, 2], ALU.min).then_inc(s("ab_neg"), 1)
                dve.wait_ge(s("ab_exp"), l + 1)
                in_layer.do(dve.tensor_scalar(ab[:, 0:2], ab[:, 0:2], 1.0, None, ALU.add))
                in_layer.link(dve.tensor_tensor(ab_t[:, 0], ab_t[:, 0], ab_t[:, 1], ALU.add))
                in_layer.do(dve.reciprocal(ab[:, 0:2], ab[:, 0:2]))
                in_layer.link(dve.tensor_scalar(ab_t[:, 0], ab_t[:, 0], -1.0, None, ALU.mult))
                dve.tensor_tensor(z, ab_t[:, 0], ea[:, :, :].unsqueeze(2).broadcast_to([P, 2, NT, H]), ALU.mult).then_inc(s("g_sb"), 1)
                for u in range(1, 12, 2):
                    dve.wait_ge(s("seg_ps"), l * 12 + u + 1)
                    dst = (qb, kb, vb)[u // 4]
                    dve.tensor_copy(dst[:, 1, (u // 2 % 2) * NB:(u // 2 % 2 + 1) * NB], pb[u % 4][:, :]).then_inc(s("seg_sb_dve"), 1)
                dve.wait_ge(s("gcum_ps"), l + 1)
                in_layer.link(dve.tensor_copy(gcum[:, :], pb[5][:, 0:32]))
                dve.tensor_tensor(gend[:, :], pb[5][:, 32:64], gcum[:, :], ALU.subtract).then_inc(s("gcum_cp"), 1)
                dve.wait_ge(s("seg_sb_act"), (l + 1) * 6)
                dve.wait_ge(s("seg_sb_dve"), (l + 1) * 6)
                for t4 in (qb, kb):
                    v4 = t4.rearrange("p t (g c) -> p t g c", g=16)
                    x1, x2 = v4[:, :, :, 0:ROPE_HALF], v4[:, :, :, ROPE_HALF:2 * ROPE_HALF]
                    for t in range(NT):
                        cs = cosb[:, t:t + 1, :].broadcast_to([P, 16, ROPE_HALF])
                        sn = sinb[:, t:t + 1, :].broadcast_to([P, 16, ROPE_HALF])
                        in_layer.do(dve.tensor_tensor(rp[0][:, t], x1[:, t], cs, ALU.mult))
                        in_layer.do(dve.tensor_tensor(rp[1][:, t], x2[:, t], sn, ALU.mult))
                        in_layer.do(dve.tensor_tensor(rp[2][:, t], x2[:, t], cs, ALU.mult))
                        in_layer.link(dve.tensor_tensor(rp[3][:, t], x1[:, t], sn, ALU.mult))
                        in_layer.do(dve.tensor_tensor(x1[:, t], rp[0][:, t], rp[1][:, t], ALU.subtract))
                        in_layer.do(dve.tensor_tensor(x2[:, t], rp[2][:, t], rp[3][:, t], ALU.add))
                in_layer.fence()
                dve.nop().then_inc(s("roped"), 1)
                in_layer.ended(LAYER_STEPS)

                def conv_taps(h, js):
                    for j in js:
                        for m in range(3):
                            src = conv_in[:, ds(h * XC + (m * H * XC + j), S)]
                            w = conv_wT[:, ds(l * (TAPS * CB) + h + (j * CB + m * H), 1)]
                            dst = c3[:, m * S:(m + 1) * S]
                            if j == 0:
                                in_gdn.do(dve.tensor_scalar(dst, src, w, None, ALU.mult))
                            else:
                                in_gdn.do(dve.scalar_tensor_tensor(dst, src, w, dst, ALU.mult, ALU.add))
                        in_gdn.fence()

                def conv_end(n):
                    dve.tensor_scalar(e3, c3, -40.0, None, ALU.max).then_inc(s("gd_conv"), 1)

                def decay_diff(h, n, par):
                    dve.wait_ge(s("gd_rows_ps"), n + 1)
                    for u in range(4):
                        ins = dve.tensor_scalar(Es[par][:, u, :], pb[7][:, u * P:(u + 1) * P], gcum[:, ds(h + u * H, 1)], 0.0,
                                                ALU.subtract, ALU.min)
                    ins.then_inc(s("gd_diff"), 1)

                def beta_decay(n, par):
                    dve.wait_ge(s("gd_em"), n + 1)
                    dve.wait_ge(s("gd_brow_ps"), n + 1)
                    dve.tensor_tensor(LTs[par], Es[par], units(pb[7][:, :]), ALU.mult).then_inc(s("gd_bm"), 1)

                def silu_end(n):
                    dve.wait_ge(s("gd_e"), n + 1)
                    dve.tensor_tensor(c3, c3, e3, ALU.mult).then_inc(s("gd_silu"), 1)

                def unit_qk(n, par):
                    dve.wait_ge(s("gd_rn"), n + 1)
                    dve.scalar_tensor_tensor(q2[par], c3[:, 0:S], P ** -0.5, e3[:, 0:S], ALU.mult, ALU.mult).then_inc(s("gd_qkn"), 1)
                    dve.tensor_tensor(kTh, kTh, e3[:, S:2 * S], ALU.mult).then_inc(s("gd_qkn"), 1)

                def gram_decay(n, par):
                    kk4 = pb[7][:, :].rearrange("p (s t c) -> p s t c", s=2, t=NT)
                    dve.wait_ge(s("gd_kk_ps"), n + 1)
                    L4 = LTs[par].rearrange("p (d t) c -> p d t c", d=2)
                    dve.tensor_tensor(L4, L4, kk4[:, 0:1].broadcast_to([P, 2, NT, P]), ALU.mult).then_inc(s("gd_lt"), 1)
                    E4 = Es[par].rearrange("p (d t) c -> p d t c", d=2)
                    dve.tensor_tensor(E4, E4, kk4[:, 1:2].broadcast_to([P, 2, NT, P]), ALU.mult).then_inc(s("gd_eq"), 1)

                ab_f = ab[:, :, :, :].rearrange("p c t h -> p (c t h)")

                def beta_kv(h, n):
                    dve.wait_ge(s("gd_kv"), n + 1)
                    dve.tensor_tensor(vbeta.rearrange("p (d t) c -> p d t c", d=2),
                                      kv.rearrange("p (s t) c -> p s t c", s=2)[:, 1:2].broadcast_to([P, 2, NT, P]),
                                      bb.rearrange("p (d t) c -> p d t c", d=2), ALU.mult).then_inc(s("gd_vb"), 1)
                    for d in range(2):
                        dve.tensor_scalar(kbg[:, d, :], kv[:, 1 - d, :], ab_f[:, ds(h + (1 + d) * H, 1)],
                                          eg[:, ds(h + (1 + d) * H, 1)], ALU.mult, ALU.mult).then_inc(s("gd_vb"), 1)

                def k_end(h):
                    for d in range(2):
                        dve.tensor_scalar(kend[:, d, :], kv[:, d, :], gend[:, ds(h + 3 * d * H, 1)], None, ALU.mult).then_inc(s("gd_vb"), 1)

                def first_level(n):
                    dve.wait_ge(s("gd_lvl"), n * LEVELS + 1)
                    dve.tensor_tensor(U, ident.unsqueeze(1).broadcast_to([P, 4, P]), Lv[0], ALU.subtract).then_inc(s("gd_u"), 1)

                def head_step(h, par, n, prep=True):
                    in_diff.start(n * DIFF_STEPS)
                    first_level(n)
                    if prep:
                        in_gdn.start((n + 1) * GDN_STEPS)
                        conv_taps(h + 1, (0, 1))
                    for v in range(1, LEVELS):
                        if v < LEVELS - 1:
                            dve.wait_ge(s("gd_tv_ps"), n * (LEVELS - 2) + v)
                            dve.tensor_tensor(T, T, units(pb[1][:, :]), ALU.subtract).then_inc(s("gd_t"), 1)
                        dve.wait_ge(s("gd_vu_ps"), n * (LEVELS - 1) + v)
                        dve.tensor_tensor(U, U, units(pb[2][:, :]), ALU.subtract).then_inc(s("gd_u"), 1)
                        if prep:
                            if v == 1:
                                conv_taps(h + 1, (2, 3))
                                decay_diff(h + 1, n + 1, 1 - par)
                            elif v == 2:
                                conv_taps(h + 1, (4,))
                                conv_end(n + 1)
                                in_gdn.ended(GDN_STEPS)
                            elif v == 3:
                                beta_decay(n + 1, 1 - par)
                            elif v == 4:
                                silu_end(n + 1)
                        if v == 3:
                            for m in range(2):
                                dve.wait_ge(s("at_s_ps"), 2 * n + m + 1)
                                in_diff.do(dve.tensor_reduce(mx[:, 2 * m:2 * m + 2], pb[5 + m][:, :].rearrange("p (t k) -> p t k", t=NT),
                                                             AXX, ALU.max))
                            in_diff.fence()
                            dve.tensor_scalar(nmx, mx, -DIFF_SCALE, None, ALU.mult).then_inc(s("at_max"), 1)
                    if prep:
                        unit_qk(n + 1, 1 - par)
                    dve.wait_ge(s("at_exp"), n + 1)
                    in_diff.link(dve.reciprocal(rsum, ssum))
                    in_diff.link(dve.tensor_scalar(rsum[:, 2:4], rsum[:, 2:4], neg_lam[:, ds(l, 1)], None, ALU.mult))
                    for t in range(NT):
                        in_diff.do(dve.tensor_scalar(pm[:, 0, t, :], pm[:, 0, t, :], rsum[:, t:t + 1], None, ALU.mult))
                    in_diff.fence()
                    for t in range(NT):
                        ins = dve.scalar_tensor_tensor(pm[:, 0, t, :], pm[:, 1, t, :], rsum[:, 2 + t:3 + t], pm[:, 0, t, :], ALU.mult, ALU.add)
                    ins.then_inc(s("at_p"), 1)
                    if prep:
                        dve.wait_ge(s("gd_uw_ps"), n + 1)
                        beta_kv(h + 1, n + 1)
                        gram_decay(n + 1, 1 - par)
                    dve.wait_ge(s("gd_ws_ps"), n + 1)
                    dve.tensor_tensor(us[:, 1:3, :], us[:, 1:3, :], units(pb[1][:, 0:2 * P]), ALU.subtract).then_inc(s("gd_vnew"), 1)
                    if prep:
                        dve.wait_ge(s("gd_s_ps"), n + 1)
                        k_end(h + 1)
                    dve.wait_ge(s("z_ps"), n + 1)
                    dve.tensor_scalar(mz, pb[3][:, :], -40.0, None, ALU.max).then_inc(s("z_low"), 1)
                    dve.wait_ge(s("gd_o_ps"), n + 1)
                    dve.wait_ge(s("gd_qs"), n + 1)
                    for t in range(NT):
                        ins = dve.tensor_tensor(oh[:, t, :], pb[0][:, t * P:(t + 1) * P], qs[:, 1 - t, :], ALU.add)
                    ins.then_inc(s("gd_osum"), 1)
                    dve.wait_ge(s("gd_rs"), n + 1)
                    for t in range(NT):
                        ins = dve.scalar_tensor_tensor(conv_in[:, ds(h * XC + (PAD + t * P), P)], oh[:, t, :], rs_o[:, t:t + 1],
                                                       rows[:, ds(l * R_N + R_GDN, P)], ALU.mult, ALU.mult)
                    ins.then_inc(s("gd_y"), 1)
                    dve.wait_ge(s("z_exp"), n + 1)
                    for m in range(2):
                        ins = dve.tensor_tensor(conv_in[:, ds(h * XC + ((m + 1) * H * XC + PAD), S)], mz[:, m * S:(m + 1) * S],
                                                pb[3][:, m * S:(m + 1) * S], ALU.mult)
                    ins.then_inc(s("z_sb"), 1)
                    dve.wait_ge(s("at_rs"), n + 1)
                    for t in range(NT):
                        ins = dve.scalar_tensor_tensor(qb[:, t, ds(h * P, P)], pb[5][:, t * P:(t + 1) * P], rs_d[:, t:t + 1],
                                                       rows[:, ds(l * R_N + R_SUB, P)], ALU.mult, ALU.mult)
                    ins.then_inc(s("at_y"), 1)
                    in_diff.ended(DIFF_STEPS)

                dve.wait_ge(s("gcum_sb"), l + 1)
                dve.wait_ge(s("qkv_sb_act"), (l + 1) * 6)
                dve.wait_ge(s("qkv_sb_dve"), (l + 1) * 6)
                in_gdn.start(l * H * GDN_STEPS)
                conv_taps(0, range(TAPS))
                conv_end(l * H)
                decay_diff(0, l * H, 0)
                beta_decay(l * H, 0)
                silu_end(l * H)
                dve.wait_ge(s("gd_silu"), l * H + 1)
                unit_qk(l * H, 0)
                beta_kv(0, l * H)
                k_end(0)
                gram_decay(l * H, 0)
                with dve.Fori(0, H // 2 - 1) as j:
                    for par in range(2):
                        head_step(2 * j + par, par, l * H + 2 * j + par)
                for par in range(2):
                    head_step(H - 2 + par, par, l * H + H - 2 + par, prep=(par == 0))

                dve.wait_ge(s("gd_y"), (l + 1) * H)
                dve.wait_ge(s("z_sb"), (l + 1) * H)
                dve.wait_ge(s("at_y"), (l + 1) * H)
                for u in range(8):
                    g, t = u // 2 % 2, u % 2
                    if u < 4:
                        y = ya[:, 4 * g:4 * g + 4, t, :].rearrange("p (s a) c -> p s a c", s=2)
                    else:
                        y = qb[:, t, g * NB:(g + 1) * NB].rearrange("p (s a c) -> p s a c", s=2, a=2)
                    dve.tensor_tensor(y, y, sz[:, u], ALU.mult).then_inc(s("z_gated"), 1)
                    if u == 7:
                        copies16(4 * l + 1, lambda k: (yaT[:, k, :], None))
                copies16(4 * l + 2, lambda k: (ybT[:, k, :], None))
                in_layer.start(l * (LAYER_STEPS + MERGE_STEPS) + LAYER_STEPS)
                for g in range(2):
                    for t in range(NT):
                        dve.wait_ge(s(f"merge_ps{t}"), l * 8 + 4 * g + 3)
                        if g == 1:
                            dve.wait_ge(s("merged"), 4 * l + t + 1)
                        dve.tensor_scalar(mg[4 * t], pb[4 * t][:, :], -40.0, None, ALU.max)
                        dve.tensor_scalar(mg[4 * t + 1], pb[4 * t + 2][:, :], -40.0, None, ALU.max).then_inc(s("gates_low"), 1)
                        dve.wait_ge(s(f"merge_ps{t}"), l * 8 + 4 * g + 4)
                        dve.wait_ge(s("merge_exp"), 4 * l + 2 * g + t + 1)
                        for m in range(2):
                            in_layer.do(dve.tensor_tensor(mg[4 * t + m], mg[4 * t + m], pb[4 * t + 1 + 2 * m][:, :], ALU.mult))
                        in_layer.fence()
                        dve.tensor_tensor(qb[:, t, g * NB:(g + 1) * NB], mg[4 * t], mg[4 * t + 1], ALU.add).then_inc(s("merged"), 1)
                copies16(4 * l + 3, lambda k: (mT[:, k, :], None))
                for u in range(4):
                    dve.wait_ge(s("xo_ps"), 4 * l + u + 1)
                    xs = x[:, u % 2, (u // 2) * NB:(u // 2 + 1) * NB]
                    dve.tensor_tensor(xs, xs, pb[4 + u][:, :], ALU.add).then_inc(s("x_added"), 1)
                dve.wait_ge(s("x_added"), 4 * (l + 1))
                in_layer.ended(MERGE_STEPS)

            dve.wait_ge(s("fnorm_in"), 16)
            normed(x, 2, grow_l)
            dve.wait_ge(s("normed"), 2 * DEPTH + 2)
            normed(xn2, 3)
            copies16(8, lambda k: (hT[:, k, :], vec[:, V_MIX + k:V_MIX + k + 1]))
            for u in range(1, 8, 2):
                dve.wait_ge(s("z2_ps"), u + 1)
                dve.tensor_copy(z2[:, u // 2, 1, :], pb[4 + u % 4][:, :]).then_inc(s("z2_sb_dve"), 1)
            with dve.Fori(DEPTH * H, DEPTH * H + H // 2) as n:
                in_dil.start((n - DEPTH * H) * DIL_STEPS)
                for m in range(2):
                    dve.wait_ge(s("at_s_ps"), 2 * n + m + 1)
                    in_dil.do(dve.scalar_tensor_tensor(p2[:, m * NB:(m + 1) * NB], pb[1 + m][:, :], 0.125,
                                                       bias2[:, ds(n * (2 * NB) + (m - 2 * DEPTH * H) * NB, NB)], ALU.mult, ALU.add))
                in_dil.fence()
                in_dil.link(dve.tensor_reduce(mx, p2.rearrange("p (j k) -> p j k", j=4), AXX, ALU.max))
                dve.tensor_scalar(nmx, mx, -1.0, None, ALU.mult).then_inc(s("at_max"), 1)
                dve.wait_ge(s("at_exp"), n + 1)
                for m in range(2):
                    ins = dve.tensor_tensor(p2[:, m * NB:(m + 1) * NB], p2[:, m * NB:(m + 1) * NB], count, ALU.mult)
                ins.then_inc(s("at_p"), 1)
                dve.wait_ge(s("at_p"), n + 1)
                in_dil.link(dve.tensor_reduce(ssum, p2.rearrange("p (j k) -> p j k", j=4), AXX, ALU.add))
                in_dil.link(dve.reciprocal(rsum, ssum))
                dve.wait_ge(s("at_o_ps"), n + 1)
                for t in range(NT):
                    for m in range(2):
                        ins = dve.tensor_scalar(bout[:, ds(n * P + (t * 512 + m * 64 - DEPTH * H * P), 64)], pb[5][:, t * P + m * 64:t * P + (m + 1) * 64],
                                                rsum[:, 2 * m + t:2 * m + t + 1], None, ALU.mult)
                ins.then_inc(s("at_y"), 1)
                in_dil.ended(DIL_STEPS)
            for u in range(4):
                dve.wait_ge(s("xm_ps"), u + 1)
                xs = x[:, u % 2, (u // 2) * NB:(u // 2 + 1) * NB]
                dve.tensor_tensor(xs, xs, pb[4 + u][:, :], ALU.add).then_inc(s("x_mixed"), 1)
            dve.memset(bpad, 0.0).then_inc(s("bpad_zero"), 1)
            dve.memset(e0, 0.0).then_inc(s("bpad_zero"), 1)
            dve.memset(CT, 0.0)
            dve.memset(ysb, 0.0).then_inc(s("y_sb"), 1)
            dve.wait_ge(s("bpad_zero"), 2)
            dve.memset(e0[0:1, :], 1.0).then_inc(s("bpad_zero"), 1)
            dve.wait_ge(s("x_mixed"), 4)
            dve.wait_ge(s("ffn_in"), 16 * 6)
            normed(h2, 4, grow)
            copies16(9, lambda k: (hT[:, k, :], None))
            r2 = Steps(dve, "dve_router_steps")
            await_once(dve, "logits_ps")
            r2.link(dve.tensor_tensor(logits, pb[0][:, 0:2 * NE].rearrange("p (t e) -> p t e", t=NT),
                                      brow.unsqueeze(1).broadcast_to([P, NT, NE]), ALU.add))
            for t in range(NT):
                r2.do(dve.max(top8[:, t, :], logits[:, t, :]))
            r2.fence()
            dve.tensor_scalar(rt[:, 0:2].unsqueeze(2), top8[:, :, 0:1], -1.0, None, ALU.mult).then_inc(once("top_neg"), 1)
            for t in range(NT):
                r2.do(dve.tensor_scalar(m_gt[:, t, :], logits[:, t, :], top8[:, t, 3:4], None, ALU.is_gt))
                r2.do(dve.tensor_scalar(m_eq[:, t, :], logits[:, t, :], top8[:, t, 3:4], None, ALU.is_equal))
            r2.fence()
            r2.link(dve.tensor_reduce(rt[:, 2:4], m_gt, AXX, ALU.add))
            r2.link(dve.tensor_scalar(rt[:, 4:6], rt[:, 2:4], -1.0, float(TOPK), ALU.mult, ALU.add))
            src, dst = m_eq, pre0
            for sh in (1, 2, 4, 8, 16):
                r2.do(dve.tensor_copy(dst[:, :, 0:sh], src[:, :, 0:sh]))
                r2.link(dve.tensor_tensor(dst[:, :, sh:NE], src[:, :, sh:NE], src[:, :, 0:NE - sh], ALU.add))
                src, dst = dst, (pre1 if dst is pre0 else pre0)
            for t in range(NT):
                r2.do(dve.scalar_tensor_tensor(msk[:, t, :], src[:, t, :], rt[:, 4 + t:5 + t], m_eq[:, t, :], ALU.is_le, ALU.mult))
            r2.fence()
            dve.tensor_tensor(msk, msk, m_gt, ALU.add).then_inc(once("mask_sb"), 1)
            await_once(dve, "mask_sb")
            await_once(dve, "gate_exp")
            r2.link(dve.tensor_tensor(gates, gates, msk, ALU.mult))
            r2.link(dve.tensor_reduce(rt[:, 6:8], gates, AXX, ALU.add))
            r2.link(dve.reciprocal(rt[:, 8:10], rt[:, 6:8]))
            for t in range(NT):
                ins = dve.tensor_scalar(gates[:, t, :], gates[:, t, :], rt[:, 8 + t:9 + t], None, ALU.mult)
            ins.then_inc(once("gates_sb"), 1)
            await_once(dve, "rank_ps")
            r2.link(dve.scalar_tensor_tensor(ranks, pb[1][:, 0:2 * NE].rearrange("p (t e) -> p t e", t=NT), 1.0, msk, ALU.add, ALU.mult))
            await_once(dve, "gates_sb")
            for r in range(ROUNDS + 1):
                r2.do(dve.tensor_scalar(rkx[:, :, r * NE:(r + 1) * NE], ranks, -1.0 - CAP * r, None, ALU.add))
                r2.do(dve.tensor_copy(gx[:, :, r * NE:(r + 1) * NE], gates))
            r2.link(dve.tensor_reduce(rt[:, 10:11], pb[1][:, 2 * NE:3 * NE], AXX, ALU.max))
            r2.link(dve.tensor_scalar(rt[:, 11:12], rt[:, 10:11], float(CAP), 1.0, ALU.is_gt, ALU.add))
            for r in range(2, ROUNDS):
                r2.link(dve.scalar_tensor_tensor(rt[:, 11:12], rt[:, 10:11], float(CAP * r), rt[:, 11:12], ALU.is_gt, ALU.add))
            for t in range(NT):
                ins = dve.tensor_scalar(P1[:, t, :], iota[:, 0:CAP], rkx[:, t, 0:1], None, ALU.is_equal)
            ins.then_inc(s("onehot"), 1)
            dve.tensor_copy(rounds_i[:, :], rt[:, 11:12]).then_inc(s("rounds_known"), 1)
            dve.wait_ge(s("rounds_known"), 1)
            rounds = dve.value_load(rounds_i[0:1, 0:1], min_val=1, max_val=ROUNDS)
            n_items = dve.snap(rounds * NE)
            NX = (ROUNDS + 1) * NE
            with dve.Fori(0, n_items) as i:
                in_moe.start(i * 2)
                dve.wait_ge(s("gather_ps"), i + 1)
                for t in range(NT):
                    ins = dve.tensor_scalar(Pg[:, t, :], iota, rkx_f[:, ds(i + t * NX, 1)], gx_f[:, ds(i + t * NX, 1)], ALU.is_equal, ALU.mult)
                ins.then_inc(s("onehot_g"), 1)
                for t in range(NT):
                    ins = dve.tensor_scalar(P1[:, t, :], iota[:, 0:CAP], rkx_f[:, ds(i + (t * NX + 1), 1)], None, ALU.is_equal)
                ins.then_inc(s("onehot"), 1)
                dve.wait_ge(s("gate_up_ps"), i + 1)
                dve.tensor_scalar(gm, pb[0][:, :], 7.0, None, ALU.min).then_inc(s("g_clamped"), 1)
                in_moe.link(dve.tensor_scalar(uc, pb[1][:, :], 7.0, -7.0, ALU.min, ALU.max))
                dve.wait_ge(s("g_clamped"), i + 1)
                in_moe.link(dve.scalar_tensor_tensor(uc, uc, 1.0, gm, ALU.add, ALU.mult))
                dve.wait_ge(s("sig"), i + 1)
                dve.tensor_tensor(gm, uc, sg, ALU.mult).then_inc(s("act"), 1)
                dve.wait_ge(s("CT_ps"), i + 1)
                dve.tensor_copy(CT, pb[2][:, 0:2 * P].rearrange("p (t c) -> p t c", t=NT)).then_inc(s("CT_sb"), 1)
                dve.wait_ge(s("actT_ps"), i + 1)
                dve.tensor_copy(actT, pb[3][:, :].rearrange("p (c h t) -> p c h t", c=4, h=2)).then_inc(s("actT_sb"), 1)
                in_moe.ended(2)
            dve.wait_ge(s("combined"), n_items + 1)
            for u in range(4):
                xs = x[:, u // 2, (u % 2) * NB:(u % 2 + 1) * NB]
                dve.tensor_tensor(xs, xs, pb[4 + u][:, :], ALU.add).then_inc(s("x_moe"), 1)
            dve.wait_ge(s("x_moe"), 4)
            normed(xn3, 5)
            copies16(10, lambda k: (hT[:, k, :], vec[:, V_PLE + k:V_PLE + k + 1]))
            r3 = Steps(dve, "dve_ple_steps")
            for u in range(4):
                dve.wait_ge(s("ple_exp"), u + 1)
                dve.wait_ge(s("ple_ps"), 2 * u + 2)
                r3.link(dve.tensor_scalar(pl[u], pl[u], 1.0, None, ALU.add))
                r3.link(dve.reciprocal(pl[u], pl[u]))
                r3.link(dve.tensor_tensor(pl[u], pl[u], pb[4 + u][:, :], ALU.mult))
                xs = x[:, u % 2, (u // 2) * NB:(u // 2 + 1) * NB]
                dve.tensor_tensor(xs, xs, pl[u], ALU.add).then_inc(s("x_ple"), 1)
            dve.wait_ge(s("x_ple"), 4)
            dve.wait_ge(s("rstd"), 7)
            for t in range(NT):
                dve.scalar_tensor_tensor(x[:, t, :], x[:, t, :], rstd[:, t:t + 1], grow_l, ALU.mult, ALU.mult).then_inc(s("y_final"), 1)

        @block.gpsimd
        def _(pool):
            with pool.Fori(0, DEPTH) as l:
                def rows_of(h):
                    ab_u = ab[:, :, :, :].rearrange("p c t h -> p (c t) h")
                    pool.tensor_tensor(gb, ab_u[:, 4:8, ds(h, 1)].broadcast_to([P, 4, P]), ones[:, :].unsqueeze(1).broadcast_to([P, 4, P]),
                                       ALU.mult).then_inc(s("gd_gb"), 1)
                    pool.tensor_copy(bb, ab_u[:, 0:4, ds(h, 1)].broadcast_to([P, 4, P])).then_inc(s("gd_gb"), 1)

                def within(n, par):
                    pool.wait_ge(s("gd_ex"), n + 1)
                    E4 = Es[par].rearrange("p (d t) c -> p d t c", d=2)
                    pool.tensor_tensor(E4, E4, tri.unsqueeze(2).broadcast_to([P, 2, NT, P]), ALU.mult).then_inc(s("gd_em"), 1)

                def head_step(h, par, n, prep=True):
                    pool.wait_ge(s("gd_lt"), n + 1)
                    for v in range(LEVELS):
                        if v == 1:
                            pool.wait_ge(s("gd_u"), n * LEVELS + 1)
                        elif v > 2:
                            pool.wait_ge(s("gd_v_ps"), n * LEVELS + v - 1)
                        pool.tensor_tensor(Lv[v % 2].rearrange("p (d t) c -> p d t c", d=2),
                                           LTs[par].rearrange("p (d t) c -> p d t c", d=2),
                                           lvl[:, v].unsqueeze(2).broadcast_to([P, 2, NT, P]), ALU.mult).then_inc(s("gd_lvl"), 1)
                        if v == 1:
                            pool.tensor_copy(qk_h[:, 0:2, :], qb[:, :, ds(h * P, P)]).then_inc(s("at_qk"), 1)
                            pool.tensor_copy(qk_h[:, 2:4, :], kb[:, :, ds(h * P, P)]).then_inc(s("at_qk"), 1)
                            if prep:
                                rows_of(h + 1)
                        elif v == 3 and prep:
                            within(n + 1, 1 - par)

                pool.wait_ge(s("gcum_sb"), l + 1)
                pool.wait_ge(s("roped"), l + 1)
                rows_of(0)
                within(l * H, 0)
                with pool.Fori(0, H // 2 - 1) as j:
                    for par in range(2):
                        head_step(2 * j + par, par, l * H + 2 * j + par)
                for par in range(2):
                    head_step(H - 2 + par, par, l * H + H - 2 + par, prep=(par == 0))
                pool.wait_ge(s("at_y"), (l + 1) * H)
            pool.wait_ge(s("z2_sb_act"), 4)
            pool.wait_ge(s("z2_sb_dve"), 4)
            with pool.Fori(DEPTH * H, DEPTH * H + H // 2) as n:
                pool.tensor_copy(q2h[:, 0:2, :], z2[:, 1, :, ds(n * P - DEPTH * H * P, P)]).then_inc(s("at_qk"), 1)
                pool.tensor_copy(q2h[:, 2:4, :], z2[:, 2, :, ds(n * P - DEPTH * H * P, P)]).then_inc(s("at_qk"), 1)
                pool.wait_ge(s("at_y"), n + 1)


_INS = ["x", "positions", "norm_w", "w_in", "conv_w", "a_log", "dt_bias", "gdn_norm_w", "diff_lambda", "diff_subln_w",
        "w_pa", "w_pb", "w_out", "final_norm_w", "p_2", "g_mix_2", "w_in_2", "w_pool_2", "pool_scale_2", "rel_bias_2",
        "w_out_2", "g_ffn_2", "w_router_2", "b_router_2", "w_gate_up_2", "b_gate_up_2", "w_down_2", "b_down_2",
        "g_ple_2", "w_ple_gate_2", "w_ple_proj_2", "g_final_2"]


def kernel(**inputs):
    import concourse.bacc as bacc
    from concourse.bass_utils import run_bass_kernel_spmd

    nc = bacc.Bacc("TRN2", target_bir_lowering=False, num_devices=1)
    arrays = {name: np.ascontiguousarray(inputs[name]) for name in _INS}
    arrays.update(shape_constants())
    aps = {name: nc.dram_tensor(name + "_dram", v.shape, mybir.dt.from_np(v.dtype), kind="ExternalInput").ap()
           for name, v in arrays.items()}
    out = nc.dram_tensor("out_dram", (1, S, D), F32, kind="ExternalOutput").ap()
    block_kernel(nc, aps, out)
    r = run_bass_kernel_spmd(nc, [{name + "_dram": v for name, v in arrays.items()}], core_ids=[0])
    return np.asarray(r.results[0]["out_dram"])
```

```python
import math
from contextlib import ExitStack

import numpy as np
import concourse.bass as bass
from concourse import mybir

F32 = mybir.dt.float32
I32 = mybir.dt.int32
ALU = mybir.AluOpType
ACT = mybir.ActivationFunctionType
AXX = mybir.AxisListType.X

P = 128
S = 256
NT = S // P
D = 1024
KC = D // P
DEPTH = 2
H = 8
PAIRS = 4
NB = 512
CH = 3 * D
CB = CH // P
TAPS = 5
PAD = TAPS // 2
AB = 3 * D
Z_A = AB + 4 * H
Q_B = Z_A + D
Z_B = Q_B + 3 * D
GATES = Z_B + D
LEVELS = 7
EPS = 1e-6
NE = 32
TOPK = 4
CAP = 64
ROUNDS = S // CAP
SLOTS = 6
RING = 5
ROPE_HALF = 8
NEG = -1e30
DIFF_SCALE = 64 ** -0.5

C_ID, C_TRI, C_STRICT, C_IOTA, C_LVL = 0, 128, 384, 512, 640
C_MISC = C_LVL + LEVELS * 2 * P
C_N = C_MISC + 12

V_NORM, V_MIX, V_FFN, V_PLE, V_POOL, V_N = 0, 16, 24, 32, 40, 44

GDN_STEPS = 15
DIFF_STEPS = 6
LAYER_STEPS = 32
MERGE_STEPS = 8


def shape_constants():
    j = np.arange(P)[:, None]
    i = np.arange(P)[None, :]
    c = np.zeros((P, C_N), np.float32)
    c[:, C_ID:C_ID + P] = j == i
    c[:, C_TRI:C_TRI + P] = j <= i
    c[:, C_TRI + P:C_TRI + 2 * P] = j >= i
    c[:, C_STRICT:C_STRICT + P] = j < i
    c[:, C_IOTA:C_IOTA + P] = i % CAP
    for n in range(LEVELS):
        s = 1 << n
        m = ((j // s) % 2 == 0) & ((i // s) % 2 == 1) & (i // (2 * s) == j // (2 * s))
        c[:, C_LVL + (2 * n) * P:C_LVL + (2 * n + 1) * P] = m
        c[:, C_LVL + (2 * n + 1) * P:C_LVL + (2 * n + 2) * P] = m.T
    inv = np.float64(500000.0) ** (-(np.arange(0, 2 * ROPE_HALF, 2) / (2.0 * ROPE_HALF)))
    c[:, C_MISC:C_MISC + ROPE_HALF] = inv.astype(np.float32)
    for l in range(DEPTH):
        lam = 0.8 - 0.6 * math.exp(-0.3 * l)
        c[:, C_MISC + 8 + l] = lam
        c[:, C_MISC + 10 + l] = 1.0 - lam
    band = np.zeros((S, 4, S), np.float32)
    for g, w in enumerate((2, 4, 8, 16)):
        for t in range(S):
            band[max(0, t - w + 1):t + 1, g, t] = np.float32(1.0) / np.float32(min(t + 1, w))
            band[t, g, t] -= 1.0
    q = np.arange(S)[:, None]
    k = np.arange(S)[None, :]
    d = q - k
    count = ((d >= 0) & (d <= 128)).astype(np.float32) + ((d >= 0) & (d % 4 == 0)) + ((d >= 0) & (d % 16 == 0))
    oh = np.zeros((33, 512), np.float32)
    for m in range(512):
        dist = 255 - m
        if dist < 0 or (dist > 128 and dist % 4):
            oh[32, m] = NEG
            continue
        b = dist if dist < 16 else min(31, 16 + int(math.log(dist / 16) / math.log(2048 / 16) * 16))
        oh[b, m] = 1.0
    return {"c_main": c, "c_band": band.reshape(S, 4 * S), "c_count": count.astype(np.float32), "c_bucket": oh}


def block_kernel(nc, a, out):
    ctx = ExitStack()
    with ctx:
        def sb(name, shape, dt=F32):
            return ctx.enter_context(nc.sbuf_tensor(name, shape, dt))

        sems = {}

        def s(name):
            if name not in sems:
                sems[name] = ctx.enter_context(nc.semaphore(name))
            return sems[name]

        ONCE = {
            "pe_once": ("vec_ps", "pool_ps", "pmix_ps", "boutT_ps", "logits_ps", "rank_ps", "gatesT_ps", "pT_ps"),
            "act_once": ("sincos", "vec_sb", "lam_exp", "pooled", "pmixed", "boutT", "gate_exp", "gatesT", "pT_sb"),
            "dve_once": ("ones_set", "angles", "lam_sums", "top_neg", "mask_sb", "gates_sb"),
        }

        def once(signal):
            return next(s(name) for name, signals in ONCE.items() if signal in signals)

        def await_once(eng, signal):
            for name, signals in ONCE.items():
                if signal in signals:
                    eng.wait_ge(s(name), signals.index(signal) + 1)

        class Steps:

            def __init__(self, eng, name):
                self.eng, self.sem, self.base, self.n = eng, s(name), 0, 0

            def start(self, base):
                self.base, self.n = base, 0

            def do(self, ins):
                self.n += 1
                ins.then_inc(self.sem, 1)

            def fence(self):
                self.eng.wait_ge(self.sem, self.base + self.n)

            def link(self, ins):
                self.do(ins)
                self.fence()

            def ended(self, n):
                assert self.n == n, (self.n, n)

        ds = bass.ds

        def unit_half(ap, u, v, odd):
            c = 1 << v
            e = odd ^ (u // 2)
            return ap[:, u * P:(u + 1) * P].rearrange("p (b e c) -> p b e c", e=2, c=c)[:, :, e, :]

        def half(ap, d, v, odd):
            c = 1 << v
            e = odd ^ d
            return ap[:, 2 * d * P:2 * (d + 1) * P].rearrange("p (b e c) -> p b e c", e=2, c=c)[:, :, e, :]

        ring = sb("ring", [P, RING * KC * NB])
        x = sb("x", [P, NT, D])
        hT = sb("hT", [P, KC, S])
        c_main = sb("c_main_sb", [P, C_N])
        ident = c_main[:, C_ID:C_ID + P]
        tri = c_main[:, C_TRI:C_TRI + 2 * P].rearrange("p (d j) -> p d j", d=2)
        strict = c_main[:, C_STRICT:C_STRICT + P]
        iota = c_main[:, C_IOTA:C_IOTA + P]
        lvl = c_main[:, C_LVL:C_MISC].rearrange("p (n d j) -> p n d j", n=LEVELS, d=2)
        inv_freq = c_main[:, C_MISC:C_MISC + 8]
        lam_init = c_main[:, C_MISC + 8:C_MISC + 10]
        one_lam = c_main[:, C_MISC + 10:C_MISC + 12]
        ones = sb("ones", [P, P])
        vec = sb("vec", [P, V_N])
        conv_wT = sb("conv_wT", [P, DEPTH * TAPS * CB])
        small = sb("small", [P, 64])
        eps, one1, ss, rstd = small[:, 0:1], small[:, 1:2], small[:, 4:6], small[:, 6:8]
        st_o, rs_o = small[:, 8:10], small[:, 10:12]
        mx, nmx, ssum, rsum = small[:, 12:16], small[:, 16:20], small[:, 20:24], small[:, 24:28]
        lam_s, neg_lam = small[:, 28:32], small[:, 32:34]
        st_d, rs_d = small[:, 34:36], small[:, 36:38]
        cosb = sb("cosb", [P, NT, ROPE_HALF])
        sinb = sb("sinb", [P, NT, ROPE_HALF])
        wab = sb("wab", [P, DEPTH * KC * 4 * H])
        ab = sb("ab", [P, 4, NT, H])
        ab_t = sb("ab_t", [P, 3, 2, NT, H])
        gcum = sb("gcum", [P, 2 * NT * H])
        eg = sb("eg", [P, 2 * NT * H])
        gend = sb("gend", [P, 2 * NT * H])
        ea = sb("ea", [P, 2, H])
        R_GDN, R_SUB, R_ALOG, R_DT, R_LAM, R_N = 0, 128, 256, 272, 288, 544
        rows = sb("rows", [P, DEPTH * R_N])
        rounds_i = sb("rounds_i", [P, 1], I32)
        rel = sb("rel", [33, H])
        pos_i = sb("pos_i", [P, NT], I32)
        scratch = nc.dram_tensor("bias_scratch", (H, P, NB), F32).ap()
        region = sb("region", [P, 19552 + KC * NB])

        def view(at, n):
            return region[:, at:at + n]

        qb, kb, vb = (view(n * NT * D, NT * D).rearrange("p (t c) -> p t c", t=NT) for n in range(3))
        XC = S + 2 * PAD
        conv_in = view(6144, CB * XC)
        conv_b = conv_in.rearrange("p (b c) -> p b c", b=CB)
        ya = conv_b[:, 0:H, PAD:PAD + S].rearrange("p h (t c) -> p h t c", t=NT)
        sz = conv_b[:, H:CB, PAD:PAD + S].rearrange("p (s h) (a c) -> p h s a c", s=2, a=2)
        yaT = view(NT * D, KC * S).rearrange("p (k t) -> p k t", k=KC)
        ybT = view(2 * NT * D, KC * S).rearrange("p (k t) -> p k t", k=KC)
        mT = view(6144, KC * S).rearrange("p (k t) -> p k t", k=KC)
        W0 = 12384

        def wk(n, k=1):
            return view(W0 + int(n * NB), int(k * NB))

        def units(ap):
            return ap.rearrange("p (u c) -> p u c", c=P)

        c3 = wk(0, 1.5)
        kTh, vTh = c3[:, S:2 * S], c3[:, 2 * S:3 * S]
        q2 = [wk(1.5 + 0.5 * n, 0.5) for n in range(2)]
        e3 = wk(2.5, 1.5)
        gb, bb, vbeta, kk2, Lv0, Lv1, T, U, V = (units(wk(4 + n)) for n in range(9))
        kv = gb
        kbg, kend = kk2[:, 0:2, :], kk2[:, 2:4, :]
        Es = [units(wk(13 + n)) for n in range(2)]
        LTs = [units(wk(15 + n)) for n in range(2)]
        Lv = (Lv0, Lv1)
        T_f, U_f, V_f = (wk(10 + n) for n in range(3))
        us = Lv1
        wT, St = V[:, 0:2, :], V[:, 2:4, :]
        qs, oh = units(e3)[:, 0:2, :], units(e3)[:, 2:4, :]
        qk_h = units(wk(17))
        qkTh = wk(18)
        pm = wk(19, 2).rearrange("p (m t k) -> p m t k", m=2, t=NT)
        aT = units(wk(20))
        mz = wk(21)
        rp = [wk(19 + 0.5 * n, 0.5).rearrange("p (t g c) -> p t g c", t=NT, g=16) for n in range(4)]
        mg = [wk(n) for n in range(8)]

        z2 = view(0, 4096).rearrange("p (s t c) -> p s t c", s=4, t=NT)
        xn2 = view(4096, 2048).rearrange("p (t c) -> p t c", t=NT)
        band = view(6144, 2048).rearrange("p (t g c) -> p t g c", t=NT, g=4)
        mixT = view(8192, 2048).rearrange("p (k t) -> p k t", k=KC)
        pooledT = view(10240, 1024)
        count = view(11264, 512)
        wpool = view(11776, 512).rearrange("p (g c) -> p g c", g=4)
        bout = view(12288, 1024)
        bias2 = view(13312, 4096)
        bucket = view(17920, NB)[0:33, :]
        qkT2 = view(17920, 512)
        aT2 = units(view(18432, 1024))
        p2 = [view(4096 + n * 1024, 1024) for n in range(2)]
        h2 = view(0, 2048).rearrange("p (t c) -> p t c", t=NT)
        bpad = view(2048, 2048)
        XT = view(4096, 512).rearrange("p (k c) -> p k c", k=KC)
        gm, uc, sg, ysb = (view(4608 + n * NB, NB) for n in range(4))
        actT = view(6656, 512).rearrange("p (c h t) -> p c h t", c=4, h=2)
        CT, Pg = view(7168, 256).rearrange("p (t c) -> p t c", t=NT), view(7424, 256).rearrange("p (t c) -> p t c", t=NT)
        P1 = view(7680, 128).rearrange("p (t c) -> p t c", t=NT)
        e0 = view(7808, 64)
        wr = view(7872, 256).rearrange("p (k e) -> p k e", k=KC)

        def te(at):
            return view(at, NT * NE).rearrange("p (t e) -> p t e", t=NT)

        logits, m_gt, m_eq, msk, gates, pre0, pre1, ranks = (te(8128 + 64 * n) for n in range(8))
        top8 = view(8640, 16).rearrange("p (t e) -> p t e", t=NT)
        rt = view(8656, 16)
        gatesT = view(8672, 256)
        rkx = view(8928, 320).rearrange("p (t e) -> p t e", t=NT)
        gx = view(9248, 320).rearrange("p (t e) -> p t e", t=NT)
        rkx_f, gx_f = view(8928, 320), view(9248, 320)
        brow = view(9568, 32)
        b_down = view(9600, 1024)
        grow = view(6144, 1024)
        ptok = view(11648, 512).rearrange("p (t c) -> p t c", t=NT)
        pT = view(12160, 512).rearrange("p (k t) -> p k t", k=2)
        pl = [view(12672 + n * NB, NB) for n in range(4)]
        xn3 = view(14720, 2048).rearrange("p (t c) -> p t c", t=NT)
        grow_l = view(16768, 1024)

        pb = [ctx.enter_context(nc.psum_tensor(f"bank{n}", [P, NB], F32)) for n in range(8)]
        block = ctx.enter_context(nc.Block())

        LAYER_TILES, seen = [], [0] * SLOTS
        for pos in range(26):
            slot = -pos % RING
            LAYER_TILES.append((slot, seen[slot]))
            seen[slot] += 1
        PER_LAYER = seen
        MIX_SLOTS = (4, 3, 2, 1, 0, 5)
        LOADED = [DEPTH * n + 1 for n in PER_LAYER]

        def slot_mem(slot):
            return ring[:, slot * KC * NB:(slot + 1) * KC * NB] if slot < RING else view(19552, KC * NB)

        def slot_w(slot):
            return slot_mem(slot).rearrange("p (k n) -> p k n", k=KC)

        def tile_src(l, pos):
            if pos < 6:
                c = pos * NB
            elif pos < 12:
                c = Q_B + (pos - 6) * NB
            elif pos < 16:
                c = (Z_A if pos < 14 else Z_B) + (pos % 2) * NB
            elif pos < 24:
                g, kind = divmod(pos - 16, 4)
                if kind % 2:
                    return a["w_pa" if kind == 1 else "w_pb"][l, :, g * NB:(g + 1) * NB]
                c = GATES + kind // 2 * D + g * NB
            else:
                return a["w_out"][l, :, (pos - 24) * NB:(pos - 23) * NB]
            return a["w_in"][l, :, c:c + NB]

        def tile_read(l, pos):
            if pos < 6:
                return "qkv_ps", l * 12 + 2 * (pos + 1)
            if pos < 12:
                return "seg_ps", l * 12 + 2 * (pos - 5)
            if pos < 16:
                return "z_ps", l * 8 + 2 * (pos - 11)
            if pos < 24:
                return "merge_ps1", l * 8 + pos - 15
            return "xo_ps", l * 4 + pos - 21

        lay = "(k p) n -> p k n"
        NCONST = 7 + DEPTH * 7 + 2

        @block.sync
        def _(sp):
            def load(dst, src, name, **kw):
                sp.dma_start(dst, src, **kw).then_inc(s(name), 16)

            load(c_main[:, :], a["c_main"], "const_in")
            load(x[:, :, :], a["x"][0].rearrange("(t p) c -> p t c", p=P), "const_in")
            load(wk(0)[V_NORM:V_MIX, 0:P], a["norm_w"].rearrange("l (k p) -> (l k) p", p=P), "const_in")
            for row, name in ((V_MIX, "g_mix_2"), (V_FFN, "g_ffn_2"), (V_PLE, "g_ple_2")):
                load(wk(0)[row:row + 8, 0:P], a[name].rearrange("l (k p) -> (l k) p", p=P), "const_in")
            load(wk(0)[V_POOL:V_N, 0:P], a["pool_scale_2"].rearrange("l (k p) -> (l k) p", p=P), "const_in")
            for l in range(DEPTH):
                load(wk(0)[0:TAPS * CB, (1 + l) * P:(2 + l) * P], a["conv_w"][l].rearrange("w (b p) -> (w b) p", p=P), "const_in")
                load(wab[:, l * 256:(l + 1) * 256].rearrange("p (k n) -> p k n", k=KC),
                     a["w_in"][l, :, AB:AB + 4 * H].rearrange(lay, p=P), "const_in")
                for off, n, src in ((R_GDN, P, a["gdn_norm_w"][l:l + 1, :]), (R_SUB, P, a["diff_subln_w"][l:l + 1, :]),
                                    (R_ALOG, 16, a["a_log"][l:l + 1].rearrange("o d h -> o (d h)")),
                                    (R_DT, 16, a["dt_bias"][l:l + 1].rearrange("o d h -> o (d h)")),
                                    (R_LAM, 256, a["diff_lambda"][l:l + 1].rearrange("o d h -> o (d h)"))):
                    load(rows[:, l * R_N + off:l * R_N + off + n], src.broadcast_to([P, n]), "const_in")
            load(rel[0:32, :], a["rel_bias_2"], "const_in")
            load(pos_i[:, :], a["positions"][0].rearrange("(t p) -> p t", p=P), "const_in", allow_slow_non_contiguous=True)

            read = {}

            def load_tile(dst, src, slot, reader):
                if slot in read:
                    sp.wait_ge(s(read[slot][0]), read[slot][1])
                load(dst, src, f"w_in_slot{slot}")
                read[slot] = reader

            for l in range(DEPTH):
                for pos in list(range(26)) if l == 0 else [1, 2, 3, 4, 0] + list(range(5, 26)):
                    slot = LAYER_TILES[pos][0]
                    load_tile(slot_w(slot), tile_src(l, pos).rearrange(lay, p=P), slot, tile_read(l, pos))
            sp.wait_ge(s("z_gated"), 8 * DEPTH)
            load(bucket, a["c_bucket"], "bucket_in")
            load(grow_l, a["final_norm_w"].rearrange("(o n) -> o n", o=1).broadcast_to([P, D]), "fnorm_in")
            for n in range(4):
                load_tile(slot_w(MIX_SLOTS[n]), a["w_in_2"][0, :, n * NB:(n + 1) * NB].rearrange(lay, p=P), MIX_SLOTS[n],
                          ("z2_ps", 2 * (n + 1)))
            read[5] = ("x_added", 4 * DEPTH)
            for n in range(2):
                load_tile(slot_w(MIX_SLOTS[4 + n]), a["w_out_2"][0, :, n * NB:(n + 1) * NB].rearrange(lay, p=P),
                          MIX_SLOTS[4 + n], ("xm_ps", n + 3))
            sp.wait_ge(s("x_added"), 4 * DEPTH)
            load(band, a["c_band"].rearrange("(t p) (g c) -> p t g c", p=P, g=4), "mix_in")
            load(count.rearrange("p (t c) -> p t c", t=NT), a["c_count"].rearrange("(t p) c -> p t c", p=P), "mix_in")
            load(wpool, a["w_pool_2"][0].rearrange("g p c -> p g c"), "mix_in")
            sp.wait_ge(s("bias_rows"), H)
            load(scratch.rearrange("h p n -> p h n"), view(0, H * NB).rearrange("p (h n) -> p h n", h=H), "bias_stored")
            sp.wait_ge(s("bias_stored"), 16)
            sp.wait_ge(s("normed"), 2 * DEPTH + 2)
            for t in range(NT):
                src = bass.AP(scratch.tensor, 255 - t * P, [[NB - 1, P], [P * NB, H], [1, S]])
                load(bias2.rearrange("p (h t k) -> p h t k", h=H, t=NT)[:, :, t, :], src, "mix_in")

            def expert(e, i, slots=range(6)):
                for j in slots:
                    if i is None and j in read:
                        sp.wait_ge(s(read[j][0]), read[j][1])
                    if j < 4:
                        src = gate_up_src[ds(e * D + j * 256, 256), :]
                        dst = slot_mem(j).rearrange("p (k n) -> p k n", k=2)
                    else:
                        src = down_src[ds(e * D + (j - 4) * 512, 512), :]
                        dst = slot_mem(j).rearrange("p (k n) -> p k n", k=4)
                    src = src.rearrange(lay, p=P)
                    if i is not None:
                        sp.wait_ge(s({3: "gate_up_ps", 5: "y_ps"}.get(j, f"w_used{j}")), i)
                    load(dst, src, f"w_in_slot{j}")
                    if i is not None and j == 3:
                        load(bpad[0:1, :], bgu[ds(e, 1), :], "bias_in")

            gate_up_src = a["w_gate_up_2"][0].rearrange("e d n -> (e d) n")
            down_src = a["w_down_2"][0].rearrange("e d n -> (e d) n")
            bgu = a["b_gate_up_2"][0]
            expert(0, None, (1, 2, 3, 4))
            await_once(sp, "pooled")
            load(grow, a["g_ffn_2"].broadcast_to([P, D]), "g_ffn_in")
            sp.wait_ge(s("x_mixed"), 4)
            load(wr, a["w_router_2"][0].rearrange("(k p) e -> p k e", p=P), "ffn_in")
            load(brow, a["b_router_2"].broadcast_to([P, NE]), "ffn_in")
            load(b_down[0:NE, :], a["b_down_2"][0], "ffn_in")
            expert(0, None, (0, 5))
            load(ptok, a["p_2"][0, 0].rearrange("(t p) c -> p t c", p=P), "ple_in")
            load(grow_l, a["g_final_2"].rearrange("(o n) -> o n", o=1).broadcast_to([P, D]), "ple_in")
            sp.wait_ge(s("bpad_zero"), 1)
            load(bpad[0:1, :], bgu[0:1, :], "bias_in")
            sp.wait_ge(s("rounds_known"), 1)
            rounds = sp.value_load(rounds_i[0:1, 0:1], min_val=1, max_val=ROUNDS)
            n_items = sp.snap(rounds * NE)
            with sp.Fori(1, n_items) as i:
                e = sp.snap(i % NE)
                expert(e, i)
            for n in range(2):
                sp.wait_ge(s(f"w_used{n}"), n_items)
                load(slot_w(n), a["w_ple_gate_2"][0, :, n * NB:(n + 1) * NB].rearrange(lay, p=P), f"w_in_slot{n}")
            sp.wait_ge(s("w_used2"), n_items)
            load(slot_mem(2)[:, 0:2048].rearrange("p (k n) -> p k n", k=2), a["w_ple_proj_2"][0].rearrange(lay, p=P), "w_in_slot2")
            for t in range(NT):
                sp.wait_ge(s("y_final"), t + 1)
                load(out[0][t * P:(t + 1) * P, :], x[:, t, :], "stored")
            sp.wait_ge(s("stored"), 16 * NT)

        @block.tensor
        def _(pe):
            def w_wait(l, pos):
                slot, k = LAYER_TILES[pos]
                pe.wait_ge(s(f"w_in_slot{slot}"), 16 * (l * PER_LAYER[slot] + k + 1))
                return slot_w(slot)

            def transpose16(src, n):
                for kp in range(4):
                    for kk in range(2):
                        for t in range(NT):
                            last = pe.transpose(pb[kp][:, (2 * kk + t) * P:(2 * kk + t + 1) * P], src(t, 2 * kp + kk), ident)
                    last.then_inc(s("tr_ps"), 1)
                pe.wait_ge(s("tr_act"), 2 * (n + 1))
                pe.wait_ge(s("tr_dve"), 2 * (n + 1))

            def product(dst, lhs, w, n_k=KC):
                for k in range(n_k):
                    mm = pe.matmul(dst, lhs(k), w(k), start=(k == 0), stop=(k == n_k - 1))
                return mm

            def blk(ap):
                return lambda t, k: ap[:, t, k * P:(k + 1) * P]

            pe.wait_ge(s("const_in"), 16 * NCONST)
            await_once(pe, "ones_set")
            pe.transpose(pb[0][:, 0:V_N], wk(0)[0:V_N, 0:P], ident[0:V_N, 0:V_N])
            for l in range(DEPTH):
                last = pe.transpose(pb[1][:, l * P:l * P + TAPS * CB], wk(0)[0:TAPS * CB, (1 + l) * P:(2 + l) * P],
                                    ident[0:TAPS * CB, 0:TAPS * CB])
            last.then_inc(once("vec_ps"), 1)
            await_once(pe, "vec_sb")

            with pe.Fori(0, DEPTH) as l:
                pe.wait_ge(s("normed"), 2 * (l + 1))
                transpose16(blk(kb), 4 * l)
                for u in range(12):
                    if u % 2 == 0:
                        w = w_wait(l, u // 2)
                    if u >= 4:
                        pe.wait_ge(s("qkv_sb_act" if u % 2 == 0 else "qkv_sb_dve"), l * 6 + (u - 4) // 2 + 1)
                    for b in range(2):
                        c = (2 * (u % 2) + b) * P
                        mm = product(pb[u % 4][:, b * S:(b + 1) * S], lambda k: w[:, k, c:c + P], lambda k: hT[:, k, :])
                    mm.then_inc(s("qkv_ps"), 1)
                for t in range(NT):
                    mm = product(pb[6][:, t * 32:(t + 1) * 32], lambda k: hT[:, k, t * P:(t + 1) * P],
                                 lambda k: wab[:, ds(l * 256 + k * 32, 32)])
                mm.then_inc(s("ab_ps"), 1)
                def decay_rows(n):
                    pe.wait_ge(s("gd_gb"), 2 * n + 1)
                    for u in range(4):
                        mm = pe.matmul(pb[7][:, u * P:(u + 1) * P], gb[:, u, :], tri[:, u // 2, :], start=True, stop=True)
                    mm.then_inc(s("gd_rows_ps"), 1)

                def beta_rows(n):
                    pe.wait_ge(s("gd_gb"), 2 * n + 2)
                    pe.wait_ge(s("gd_diff"), n + 1)
                    for u in range(4):
                        mm = pe.matmul(pb[7][:, u * P:(u + 1) * P], bb[:, u, :], ident, start=True, stop=True)
                    mm.then_inc(s("gd_brow_ps"), 1)

                def norms(n):
                    pe.wait_ge(s("gd_sq"), n + 1)
                    pe.wait_ge(s("gd_bm"), n + 1)
                    pe.matmul(pb[7][:, :], ones[:, :], e3[:, 0:2 * S], start=True, stop=True).then_inc(s("gd_norm_ps"), 1)

                def kv_rows(n):
                    pe.wait_ge(s("gd_qkn"), 2 * (n + 1))
                    for t in range(NT):
                        pe.transpose(pb[7][:, t * P:(t + 1) * P], kTh[:, t * P:(t + 1) * P], ident)
                        mm = pe.transpose(pb[7][:, (2 + t) * P:(3 + t) * P], vTh[:, t * P:(t + 1) * P], ident)
                    mm.then_inc(s("gd_kv_ps"), 1)

                def gram(n, par):
                    pe.wait_ge(s("gd_kv"), n + 1)
                    for t in range(NT):
                        kt = kTh[:, t * P:(t + 1) * P]
                        pe.matmul(pb[7][:, t * P:(t + 1) * P], kt, kt, start=True, stop=True)
                        mm = pe.matmul(pb[7][:, (2 + t) * P:(3 + t) * P], kt, q2[par][:, t * P:(t + 1) * P], start=True, stop=True)
                    mm.then_inc(s("gd_kk_ps"), 1)

                for u in range(12):
                    t = u % 2
                    if t == 0:
                        w = w_wait(l, 6 + u // 2)
                    if u >= 4:
                        pe.wait_ge(s("seg_sb_act" if t == 0 else "seg_sb_dve"), l * 6 + (u - 4) // 2 + 1)
                    else:
                        pe.wait_ge(s("qkv_sb_act" if t == 0 else "qkv_sb_dve"), l * 6 + 5 + u // 2)
                    mm = product(pb[u % 4][:, :], lambda k: hT[:, k, t * P:(t + 1) * P], lambda k: w[:, k, :])
                    mm.then_inc(s("seg_ps"), 1)
                    if u == 1:
                        pe.wait_ge(s("g_sb"), l + 1)
                        for d in range(2):
                            g_d = ab[:, 2 + d, :, :].rearrange("p t h -> p (t h)")
                            pe.matmul(pb[5][:, d * 16:(d + 1) * 16], tri[:, d, :], g_d, start=True, stop=True)
                            mm = pe.matmul(pb[5][:, 32 + d * 16:32 + (d + 1) * 16], ones[:, :], g_d, start=True, stop=True)
                        mm.then_inc(s("gcum_ps"), 1)
                    elif u == 3:
                        decay_rows(l * H)
                    elif u == 5:
                        beta_rows(l * H)
                    elif u == 7:
                        norms(l * H)
                    elif u == 9:
                        kv_rows(l * H)
                pe.wait_ge(s("seg_sb_act"), (l + 1) * 6)
                pe.wait_ge(s("seg_sb_dve"), (l + 1) * 6)
                for j in range(4):
                    w_wait(l, 12 + j)
                gram(l * H, 0)

                def z_part(j, t, parts):
                    for k in parts:
                        mm = pe.matmul(pb[3][:, :], hT[:, k, t * P:(t + 1) * P], ring[:, ds(j * (-KC * NB) + (3 * KC + k) * NB, NB)],
                                       start=(k == 0), stop=(k == KC - 1))
                    if parts[-1] == KC - 1:
                        mm.then_inc(s("z_ps"), 1)

                Z_PARTS = {3: [0, 1], 4: [2], 5: [3], 6: [4]}

                def scores(n):
                    pe.wait_ge(s("at_qkT"), n + 1)
                    for m in range(2):
                        for t in range(NT):
                            mm = pe.matmul(pb[5 + m][:, t * S:(t + 1) * S], qkTh[m * 64:(m + 1) * 64, t * P:(t + 1) * P],
                                           qkTh[m * 64:(m + 1) * 64, S:2 * S], start=True, stop=True)
                        mm.then_inc(s("at_s_ps"), 1)

                def head_step(h, j, par, n, prep=True):
                    pe.wait_ge(s("gd_u"), n * LEVELS + 1)
                    for u in range(4):
                        mm = pe.transpose(pb[0][:, u * P:(u + 1) * P], U[:, u, :], ident)
                    mm.then_inc(s("gd_v_ps"), 1)
                    pe.wait_ge(s("at_qk"), 2 * (n + 1))
                    for i in range(4):
                        mm = pe.transpose(pb[4][:, i * P:(i + 1) * P], qk_h[:, i, :], ident)
                    mm.then_inc(s("at_qkT_ps"), 1)
                    for v in range(1, LEVELS):
                        pe.wait_ge(s("gd_lvl"), n * LEVELS + v + 1)
                        if v == 1:
                            pe.wait_ge(s("gd_vcopy"), n * LEVELS + 1)
                        else:
                            pe.wait_ge(s("gd_t"), n * (LEVELS - 2) + v - 1)
                        for u in range(4):
                            mm = pe.matmul(pb[0][:, u * P:(u + 1) * P], Lv[v % 2][:, u, :], T[:, u, :], start=True, stop=True)
                        mm.then_inc(s("gd_v_ps"), 1)
                        if v > 2:
                            z_part(j, par, Z_PARTS[v])
                        if prep and v == 1:
                            decay_rows(n + 1)
                        pe.wait_ge(s("gd_vcopy"), n * LEVELS + v + 1)
                        pe.wait_ge(s("gd_u"), n * LEVELS + v)
                        if v < LEVELS - 1:
                            for u in range(4):
                                mm = pe.matmul(unit_half(pb[1], u, v, 0), U[:, u, :], unit_half(V_f, u, v, 0), start=True, stop=True)
                            mm.then_inc(s("gd_tv_ps"), 1)
                        for u in range(4):
                            mm = pe.matmul(unit_half(pb[2], u, v, 1), V[:, u, :], unit_half(U_f, u, v, 1), start=True, stop=True)
                        mm.then_inc(s("gd_vu_ps"), 1)
                        if v == 3:
                            scores(n)
                        if prep:
                            if v == 3:
                                beta_rows(n + 1)
                            elif v == 5:
                                norms(n + 1)
                    z_part(j, par, [5])
                    pe.wait_ge(s("gd_u"), (n + 1) * LEVELS)
                    pe.wait_ge(s("gd_vb"), 5 * (n + 1))
                    for u in range(4):
                        pe.matmul(pb[1][:, u * P:(u + 1) * P], U[:, u, :], vbeta[:, u, :], start=True, stop=True)
                    for d in range(2):
                        mm = pe.matmul(pb[2][:, d * P:(d + 1) * P], kbg[:, d, :], U[:, 1 + d, :], start=True, stop=True)
                    mm.then_inc(s("gd_uw_ps"), 1)
                    if prep:
                        kv_rows(n + 1)
                    z_part(j, par, [6])
                    pe.wait_ge(s("gd_uw_sb"), 2 * (n + 1))
                    for d in range(2):
                        mm = pe.matmul(pb[0][:, d * P:(d + 1) * P], kend[:, d, :], us[:, 3 * d, :], start=True, stop=True)
                    mm.then_inc(s("gd_s_ps"), 1)
                    if prep:
                        gram(n + 1, 1 - par)
                    z_part(j, par, [7])
                    pe.wait_ge(s("gd_s_sb"), n + 1)
                    for d in range(2):
                        pe.matmul(pb[1][:, d * P:(d + 1) * P], wT[:, d, :], St[:, d, :], start=True, stop=True)
                        mm = pe.matmul(pb[2][:, d * P:(d + 1) * P], q2[par][:, (1 - d) * P:(2 - d) * P], St[:, d, :],
                                       start=True, stop=True)
                    mm.then_inc(s("gd_ws_ps"), 1)
                    pe.wait_ge(s("at_p"), n + 1)
                    for kt in range(NT):
                        for t in range(NT):
                            mm = pe.transpose(pb[4][:, (kt * 2 + t) * P:(kt * 2 + t + 1) * P], pm[:, 0, t, kt * P:(kt + 1) * P], ident)
                    mm.then_inc(s("at_pT_ps"), 1)
                    pe.wait_ge(s("gd_vnew"), n + 1)
                    for t in range(NT):
                        for d in range(2):
                            mm = pe.matmul(pb[0][:, t * P:(t + 1) * P], Es[par][:, 2 * d + t, :], us[:, 2 * d + t, :],
                                           start=(d == 0), stop=(d == 1))
                    mm.then_inc(s("gd_o_ps"), 1)
                    pe.wait_ge(s("at_pT"), n + 1)
                    for t in range(NT):
                        for kt in range(NT):
                            mm = pe.matmul(pb[5][:, t * P:(t + 1) * P], aT[:, kt * 2 + t, :], vb[:, kt, ds(h * P, P)],
                                           start=(kt == 0), stop=(kt == 1))
                    mm.then_inc(s("at_o_ps"), 1)

                with pe.Fori(0, H // 2 - 1) as j:
                    for par in range(2):
                        head_step(2 * j + par, j, par, l * H + 2 * j + par)
                for par in range(2):
                    head_step(H - 2 + par, H // 2 - 1, par, l * H + H - 2 + par, prep=(par == 0))

                pe.wait_ge(s("z_gated"), l * 8 + 6)
                transpose16(lambda t, k: ya[:, k, t, :], 4 * l + 1)
                pe.wait_ge(s("z_gated"), l * 8 + 8)
                transpose16(blk(qb), 4 * l + 2)
                for g in range(2):
                    if g == 1:
                        pe.wait_ge(s("merged"), 4 * l + 2)
                    for kind in range(4):
                        w = w_wait(l, 16 + 4 * g + kind)
                        src = (hT, yaT, hT, ybT)[kind]
                        for t in range(NT):
                            product(pb[4 * t + kind][:, :], lambda k: src[:, k, t * P:(t + 1) * P],
                                    lambda k: w[:, k, :]).then_inc(s(f"merge_ps{t}"), 1)
                pe.wait_ge(s("merged"), 4 * (l + 1))
                transpose16(blk(qb), 4 * l + 3)
                for u in range(4):
                    t, g = divmod(u, 2)
                    w = w_wait(l, 24 + g)
                    product(pb[4 + u][:, :], lambda k: mT[:, k, t * P:(t + 1) * P], lambda k: w[:, k, :]).then_inc(s("xo_ps"), 1)
                pe.wait_ge(s("x_added"), 4 * (l + 1))

            pe.wait_ge(s("bucket_in"), 16)
            for h in range(H):
                if h >= 4:
                    pe.wait_ge(s("bias_rows"), h - 3)
                pe.matmul(pb[4 + h % 4][:, :], rel[:, h:h + 1].broadcast_to([33, P]), bucket[0:33, :],
                          start=True, stop=True).then_inc(s("bias_ps"), 1)
            pe.wait_ge(s("normed"), 2 * DEPTH + 4)
            transpose16(blk(xn2), 8)
            pe.wait_ge(s("bias_rows"), H)
            for u in range(8):
                t = u % 2
                if t == 0:
                    slot = MIX_SLOTS[u // 2]
                    pe.wait_ge(s(f"w_in_slot{slot}"), 16 * LOADED[slot])
                if u >= 4:
                    pe.wait_ge(s("z2_sb_act" if t == 0 else "z2_sb_dve"), (u - 4) // 2 + 1)
                product(pb[4 + u % 4][:, :], lambda k: hT[:, k, t * P:(t + 1) * P], lambda k: slot_w(slot)[:, k, :]).then_inc(s("z2_ps"), 1)
            pe.wait_ge(s("z2_sb_act"), 4)
            pe.wait_ge(s("z2_sb_dve"), 4)
            pe.wait_ge(s("mix_in"), 16 * 5)
            for g in range(4):
                mm = product(pb[g // 2][:, (g % 2) * S:(g % 2 + 1) * S], lambda t: z2[:, 0, t, g * P:(g + 1) * P],
                             lambda t: band[:, t, g, :], NT)
            mm.then_inc(once("pool_ps"), 1)
            await_once(pe, "pooled")
            for g in range(4):
                mm = pe.matmul(pb[2 + g // 2][:, (g % 2) * S:(g % 2 + 1) * S], wpool[:, g, :], pooledT[:, g * S:(g + 1) * S],
                               start=True, stop=True)
            mm.then_inc(once("pmix_ps"), 1)
            await_once(pe, "pmixed")
            def pair_scores(i):
                n = DEPTH * H + i
                for j in range(4):
                    mm = pe.transpose(pb[0][:, j * P:(j + 1) * P], z2[:, 1 + j // 2, j % 2, i * P:(i + 1) * P], ident)
                mm.then_inc(s("at_qkT_ps"), 1)
                pe.wait_ge(s("at_qkT"), n + 1)
                if i > 0:
                    pe.wait_ge(s("at_max"), n)
                for m in range(2):
                    for t in range(NT):
                        mm = pe.matmul(pb[1 + m][:, t * S:(t + 1) * S], qkT2[m * 64:(m + 1) * 64, t * P:(t + 1) * P],
                                       qkT2[m * 64:(m + 1) * 64, S:2 * S], start=True, stop=True)
                    mm.then_inc(s("at_s_ps"), 1)

            pair_scores(0)
            for i in range(PAIRS):
                n = DEPTH * H + i
                if i < PAIRS - 1:
                    pair_scores(i + 1)
                pe.wait_ge(s("at_p"), n + 1)
                for m in range(2):
                    for kt in range(NT):
                        for t in range(NT):
                            c = (kt * 2 + t) * P
                            mm = pe.transpose(pb[3 + m][:, c:c + P], p2[i % 2][:, m * 512 + t * S + kt * P:m * 512 + t * S + (kt + 1) * P], ident)
                mm.then_inc(s("at_pT_ps"), 1)
                pe.wait_ge(s("at_pT"), n + 1)
                if i > 0:
                    pe.wait_ge(s("at_y"), n)
                for t in range(NT):
                    for m in range(2):
                        mm = product(pb[5][:, t * P + m * 64:t * P + (m + 1) * 64], lambda kt: aT2[:, m * 4 + kt * 2 + t, :],
                                     lambda kt: z2[:, 3, kt, i * P + m * 64:i * P + (m + 1) * 64], NT)
                mm.then_inc(s("at_o_ps"), 1)
            pe.wait_ge(s("at_y"), DEPTH * H + PAIRS)
            for t in range(NT):
                for c in range(4):
                    mm = pe.transpose(pb[c // 2][:, (c % 2) * S + t * P:(c % 2) * S + (t + 1) * P],
                                      bout[:, t * 512 + c * P:t * 512 + (c + 1) * P], ident)
            mm.then_inc(once("boutT_ps"), 1)
            await_once(pe, "boutT")
            for u in range(4):
                t, slot = u // 2, MIX_SLOTS[4 + u % 2]
                if t == 0:
                    pe.wait_ge(s(f"w_in_slot{slot}"), 16 * LOADED[slot])
                product(pb[4 + u][:, :], lambda k: mixT[:, k, t * P:(t + 1) * P], lambda k: slot_w(slot)[:, k, :]).then_inc(s("xm_ps"), 1)

            pe.wait_ge(s("normed"), 2 * DEPTH + 6)
            transpose16(blk(h2), 9)
            pe.wait_ge(s("ffn_in"), 16 * 3)
            for t in range(NT):
                mm = product(pb[0][:, t * NE:(t + 1) * NE], lambda k: hT[:, k, t * P:(t + 1) * P], lambda k: wr[:, k, :])
            mm.then_inc(once("logits_ps"), 1)
            await_once(pe, "mask_sb")
            pe.matmul(pb[1][:, 0:NE], strict, msk[:, 0, :], start=True, stop=True)
            pe.matmul(pb[1][:, NE:2 * NE], strict, msk[:, 1, :], start=True, stop=False)
            pe.matmul(pb[1][:, NE:2 * NE], ones[:, :], msk[:, 0, :], start=False, stop=True)
            pe.matmul(pb[1][:, 2 * NE:3 * NE], ones[:, :], msk[:, 0, :], start=True, stop=False)
            pe.matmul(pb[1][:, 2 * NE:3 * NE], ones[:, :], msk[:, 1, :], start=False, stop=True).then_inc(once("rank_ps"), 1)
            await_once(pe, "gates_sb")
            for t in range(NT):
                mm = pe.transpose(pb[2][0:NE, t * P:(t + 1) * P], gates[:, t, :], ident)
            mm.then_inc(once("gatesT_ps"), 1)
            await_once(pe, "gatesT")
            for t in range(NT):
                for g in range(2):
                    pe.matmul(pb[4 + 2 * t + g][:, :], gatesT[0:NE, t * P:(t + 1) * P], b_down[0:NE, g * NB:(g + 1) * NB],
                              start=True, stop=False, skip_group_check=True)

            def gather():
                for k in range(KC):
                    for t in range(NT):
                        mm = pe.matmul(pb[3][:, k * CAP:(k + 1) * CAP], h2[:, t, k * P:(k + 1) * P], P1[:, t, :],
                                       start=(t == 0), stop=(t == 1))
                mm.then_inc(s("gather_ps"), 1)

            def combine():
                for hf in range(2):
                    for t in range(NT):
                        mm = pe.matmul(pb[4 + 2 * t + hf][:, :], CT[hf * 64:(hf + 1) * 64, t, :], ysb[hf * 64:(hf + 1) * 64, :],
                                       start=False, stop=False, skip_group_check=True)
                mm.then_inc(s("combined"), 1)

            pe.wait_ge(s("onehot"), 1)
            gather()
            pe.wait_ge(s("rounds_known"), 1)
            rounds = pe.value_load(rounds_i[0:1, 0:1], min_val=1, max_val=ROUNDS)
            n_items = pe.snap(rounds * NE)
            with pe.Fori(0, n_items) as i:
                pe.wait_ge(s("XT_sb"), i + 1)
                pe.wait_ge(s("y_sb"), i + 1)
                pe.wait_ge(s("bias_in"), 16 * (i + 1))
                for g in range(2):
                    for hf in range(2):
                        pe.matmul(pb[g][hf * 64:(hf + 1) * 64, :], e0, bpad[:, g * D + hf * NB:g * D + (hf + 1) * NB],
                                  start=True, stop=False)
                for j in range(4):
                    pe.wait_ge(s(f"w_in_slot{j}"), 16 * (LOADED[j] + 1 + i))
                    wj = slot_mem(j).rearrange("p (k n) -> p k n", k=2)
                    for kk in range(2):
                        for g in range(2):
                            for hf in range(2):
                                c = g * D + hf * NB
                                mm = pe.matmul(pb[g][hf * 64:(hf + 1) * 64, :], XT[:, 2 * j + kk, :], wj[:, kk, c:c + NB],
                                               start=False, stop=(j == 3 and kk == 1))
                    mm.then_inc(s("gate_up_ps" if j == 3 else f"w_used{j}"), 1)
                combine()
                pe.wait_ge(s("onehot"), i + 2)
                gather()
                pe.wait_ge(s("onehot_g"), i + 1)
                for t in range(NT):
                    mm = pe.transpose(pb[2][:, t * P:(t + 1) * P], Pg[:, t, :], ident)
                mm.then_inc(s("CT_ps"), 1)
                pe.wait_ge(s("act"), i + 1)
                pe.wait_ge(s("XT_sb"), i + 2)
                for c in range(4):
                    mm = pe.transpose(pb[3][:, c * P:(c + 1) * P], gm[:, c * P:(c + 1) * P], ident)
                mm.then_inc(s("actT_ps"), 1)
                pe.wait_ge(s("CT_sb"), i + 1)
                pe.wait_ge(s("actT_sb"), i + 1)
                for j in range(2):
                    pe.wait_ge(s(f"w_in_slot{4 + j}"), 16 * (LOADED[4 + j] + 1 + i))
                    wj = slot_mem(4 + j).rearrange("p (k n) -> p k n", k=4)
                    for c in range(4):
                        for hf in range(2):
                            mm = pe.matmul(pb[2][hf * 64:(hf + 1) * 64, :], actT[:, c, j, :], wj[:, c, hf * NB:(hf + 1) * NB],
                                           start=(j == 0 and c == 0), stop=(j == 1 and c == 3))
                    mm.then_inc(s("y_ps" if j == 1 else "w_used4"), 1)
            pe.wait_ge(s("y_sb"), n_items + 1)
            combine()

            pe.wait_ge(s("x_moe"), 4)
            pe.wait_ge(s("ple_in"), 16 * 2)
            for t in range(NT):
                for k in range(2):
                    mm = pe.transpose(pb[4][:, k * S + t * P:k * S + (t + 1) * P], ptok[:, t, k * P:(k + 1) * P], ident)
            mm.then_inc(once("pT_ps"), 1)
            pe.wait_ge(s("normed"), 2 * DEPTH + 8)
            transpose16(blk(xn3), 10)
            await_once(pe, "pT_sb")
            pe.wait_ge(s("w_in_slot2"), 16 * (LOADED[2] + 1 + n_items))
            wp = slot_mem(2)[:, 0:2048].rearrange("p (k n) -> p k n", k=2)
            for t in range(NT):
                for g in range(2):
                    if t == 0:
                        pe.wait_ge(s(f"w_in_slot{g}"), 16 * (LOADED[g] + 1 + n_items))
                    product(pb[2 * g + t][:, :], lambda k: hT[:, k, t * P:(t + 1) * P], lambda k: slot_w(g)[:, k, :]).then_inc(s("ple_ps"), 1)
                    product(pb[4 + 2 * g + t][:, :], lambda k: pT[:, k, t * P:(t + 1) * P],
                            lambda k: wp[:, k, g * NB:(g + 1) * NB], 2).then_inc(s("ple_ps"), 1)

        @block.scalar
        def _(act):
            me = Steps(act, "act_steps")
            in_layer = Steps(act, "act_layer_steps")
            in_gdn = Steps(act, "act_prep_steps")
            in_head = Steps(act, "act_head_steps")

            def copies16(n, scale):
                for j, kp in enumerate((0, 2)):
                    act.wait_ge(s("tr_ps"), 4 * n + kp + 1)
                    for kk in range(2):
                        k = 2 * kp + kk
                        dst, sc = scale(k)
                        last = act.activation(dst, pb[kp][:, kk * S:(kk + 1) * S], ACT.Copy, scale=sc)
                    last.then_inc(s("tr_act"), 1)

            def row_rstd(steps, junk, added=None):
                for t in range(NT):
                    if added:
                        act.wait_ge(s(added), 2 * (t + 1))
                    steps.do(act.activation(junk[:, t, :], x[:, t, :], ACT.Square, accum_out=ss[:, t:t + 1]))
                steps.fence()
                ss_rstd(steps)

            def ss_rstd(steps):
                steps.link(act.activation(rstd, ss, ACT.Ln, bias=eps, scale=1.0 / D))
                act.activation(rstd, rstd, ACT.Exp, scale=-0.5).then_inc(s("rstd"), 1)

            def hT_with(at):
                return lambda k: (hT[:, k, :], vec[:, at(k)])

            await_once(act, "angles")
            act.activation(cosb[:, :, :], cosb[:, :, :], ACT.Sin)
            act.activation(sinb[:, :, :], sinb[:, :, :], ACT.Sin).then_inc(once("sincos"), 1)
            await_once(act, "vec_ps")
            act.activation(vec[:, :], pb[0][:, 0:V_N], ACT.Copy)
            act.activation(conv_wT[:, 0:TAPS * CB], pb[1][:, 0:TAPS * CB], ACT.Copy)
            act.activation(conv_wT[:, TAPS * CB:2 * TAPS * CB], pb[1][:, P:P + TAPS * CB], ACT.Copy).then_inc(once("vec_sb"), 1)
            await_once(act, "lam_sums")
            act.activation(lam_s, lam_s, ACT.Exp).then_inc(once("lam_exp"), 1)
            await_once(act, "vec_sb")
            act.preload_act_table_set("natural_log_exp_and_others")

            def square_sum(t):
                in_layer.do(act.activation(kb[:, t, :], x[:, t, :], ACT.Square, accum_out=ss[:, t:t + 1]))

            in_layer.start(0)
            for t in range(NT):
                square_sum(t)
            with act.Fori(0, DEPTH) as l:
                in_layer.start(NT + l * 6)
                in_layer.fence()
                ss_rstd(in_layer)
                copies16(4 * l, lambda k: (hT[:, k, :], vec[:, ds(l * KC + V_NORM + k, 1)]))
                for u in range(0, 12, 2):
                    act.wait_ge(s("qkv_ps"), l * 12 + u + 1)
                    act.activation(conv_b[:, 2 * u:2 * u + 2, PAD:PAD + S], pb[u % 4][:, :].rearrange("p (b c) -> p b c", b=2),
                                   ACT.Copy).then_inc(s("qkv_sb_act"), 1)
                act.wait_ge(s("ab_ps"), l + 1)
                for t in range(NT):
                    last = act.activation(ab[:, :, t, :], pb[6][:, t * 32:(t + 1) * 32].rearrange("p (c h) -> p c h", c=4), ACT.Copy)
                last.then_inc(s("ab_sb"), 1)
                act.wait_ge(s("ab_neg"), l + 1)
                in_layer.link(act.activation(ab_t[:, 1], ab_t[:, 1], ACT.Exp))
                in_layer.do(act.activation(ab_t[:, 1], ab_t[:, 1], ACT.Ln, bias=one1))
                in_layer.do(act.activation(ab[:, 0:2], ab[:, 0:2], ACT.Exp, scale=-1.0))
                act.activation(ea[:, :, :], rows[:, ds(l * R_N + R_ALOG, 16)].rearrange("p (d h) -> p d h", d=2), ACT.Exp).then_inc(s("ab_exp"), 1)

                def silu_exps(n):
                    act.wait_ge(s("gd_conv"), n + 1)
                    in_gdn.link(act.activation(e3, e3, ACT.Exp, scale=-1.0))
                    in_gdn.do(act.activation(e3, e3, ACT.Ln, bias=one1))

                def silu_last_exp():
                    in_gdn.fence()
                    act.activation(e3, e3, ACT.Exp, scale=-1.0).then_inc(s("gd_e"), 1)

                def decay_exp(n, par):
                    act.wait_ge(s("gd_diff"), n + 1)
                    act.activation(Es[par], Es[par], ACT.Exp).then_inc(s("gd_ex"), 1)

                def squares(n):
                    act.wait_ge(s("gd_silu"), n + 1)
                    act.activation(e3[:, 0:2 * S], c3[:, 0:2 * S], ACT.Square).then_inc(s("gd_sq"), 1)

                def inverse_norms(n):
                    act.wait_ge(s("gd_norm_ps"), n + 1)
                    in_gdn.link(act.activation(e3[:, 0:2 * S], pb[7][:, :], ACT.Ln, bias=eps))
                    act.activation(e3[:, 0:2 * S], e3[:, 0:2 * S], ACT.Exp, scale=-0.5).then_inc(s("gd_rn"), 1)

                def kv_copy(n):
                    act.wait_ge(s("gd_kv_ps"), n + 1)
                    act.activation(kv, units(pb[7][:, :]), ACT.Copy).then_inc(s("gd_kv"), 1)

                def first_copies(n):
                    act.wait_ge(s("gd_v_ps"), n * LEVELS + 1)
                    act.activation(T, units(pb[0][:, :]), ACT.Copy).then_inc(s("gd_vcopy"), 1)
                    act.wait_ge(s("at_qkT_ps"), n + 1)
                    act.activation(qkTh, pb[4][:, :], ACT.Copy).then_inc(s("at_qkT"), 1)

                def level_copy(n, v):
                    act.wait_ge(s("gd_v_ps"), n * LEVELS + v + 1)
                    act.activation(V, units(pb[0][:, :]), ACT.Copy).then_inc(s("gd_vcopy"), 1)

                def head_step(h, par, n, prep=True):
                    in_head.start(n * 6)
                    if prep:
                        in_gdn.start((n + 1) * 3)
                    for v in range(2, LEVELS):
                        level_copy(n, v)
                        if prep:
                            if v == 2:
                                decay_exp(n + 1, 1 - par)
                            elif v == 3:
                                silu_exps(n + 1)
                            elif v == 4:
                                silu_last_exp()
                            elif v == 5:
                                squares(n + 1)
                            elif v == 6:
                                inverse_norms(n + 1)
                        if v == 5:
                            act.wait_ge(s("at_max"), n + 1)
                            for m in range(2):
                                for t in range(NT):
                                    i = 2 * m + t
                                    last = act.activation(pm[:, m, t, :], pb[5 + m][:, t * S:(t + 1) * S], ACT.Exp,
                                                          bias=nmx[:, i:i + 1], scale=DIFF_SCALE, accum_out=ssum[:, i:i + 1])
                            last.then_inc(s("at_exp"), 1)
                    act.wait_ge(s("gd_uw_ps"), n + 1)
                    act.activation(us, units(pb[1][:, :]), ACT.Copy).then_inc(s("gd_uw_sb"), 1)
                    act.activation(wT, units(pb[2][:, 0:2 * P]), ACT.Copy).then_inc(s("gd_uw_sb"), 1)
                    if prep:
                        kv_copy(n + 1)
                    act.wait_ge(s("gd_s_ps"), n + 1)
                    act.activation(St, units(pb[0][:, 0:2 * P]), ACT.Copy).then_inc(s("gd_s_sb"), 1)
                    act.wait_ge(s("gd_ws_ps"), n + 1)
                    for d in range(2):
                        last = act.activation(qs[:, d, :], pb[2][:, d * P:(d + 1) * P], ACT.Copy, scale=eg[:, ds(h + (1 + d) * H, 1)])
                    last.then_inc(s("gd_qs"), 1)
                    act.wait_ge(s("at_pT_ps"), n + 1)
                    act.activation(aT, units(pb[4][:, :]), ACT.Copy).then_inc(s("at_pT"), 1)
                    act.wait_ge(s("gd_osum"), n + 1)
                    for t in range(NT):
                        in_head.do(act.activation(qs[:, t, :], oh[:, t, :], ACT.Square, accum_out=st_o[:, t:t + 1]))
                    in_head.fence()
                    in_head.link(act.activation(rs_o, st_o, ACT.Ln, bias=eps, scale=1.0 / P))
                    act.activation(rs_o, rs_o, ACT.Exp, scale=-0.5).then_inc(s("gd_rs"), 1)
                    if prep:
                        first_copies(n + 1)
                    act.wait_ge(s("z_low"), n + 1)
                    in_head.do(act.activation(mz, mz, ACT.Exp, scale=-1.0))
                    if prep:
                        level_copy(n + 1, 1)
                    in_head.fence()
                    in_head.link(act.activation(mz, mz, ACT.Ln, bias=one1))
                    act.activation(mz, mz, ACT.Exp, scale=-1.0).then_inc(s("z_exp"), 1)
                    act.wait_ge(s("at_o_ps"), n + 1)
                    for t in range(NT):
                        last = act.activation(pm[:, 0, t, 0:P], pb[5][:, t * P:(t + 1) * P], ACT.Square, accum_out=st_d[:, t:t + 1])
                    last.then_inc(s("at_ss"), 1)
                    act.wait_ge(s("at_ss"), n + 1)
                    in_head.link(act.activation(rs_d, st_d, ACT.Ln, bias=eps, scale=1.0 / P))
                    act.activation(rs_d, rs_d, ACT.Exp, scale=-0.5).then_inc(s("at_rs"), 1)
                    in_head.ended(6)

                in_gdn.start(l * H * 3)
                for u in range(0, 12, 2):
                    act.wait_ge(s("seg_ps"), l * 12 + u + 1)
                    dst = (qb, kb, vb)[u // 4]
                    act.activation(dst[:, 0, (u // 2 % 2) * NB:(u // 2 % 2 + 1) * NB], pb[u % 4][:, :], ACT.Copy).then_inc(s("seg_sb_act"), 1)
                    if u == 0:
                        act.wait_ge(s("gcum_cp"), l + 1)
                        act.activation(eg[:, :], gcum[:, :], ACT.Exp)
                        act.activation(gend[:, :], gend[:, :], ACT.Exp).then_inc(s("gcum_sb"), 1)
                    elif u == 2:
                        silu_exps(l * H)
                        silu_last_exp()
                        decay_exp(l * H, 0)
                    elif u == 4:
                        squares(l * H)
                    elif u == 6:
                        inverse_norms(l * H)
                    elif u == 8:
                        kv_copy(l * H)
                in_gdn.ended(3)
                first_copies(l * H)
                level_copy(l * H, 1)
                with act.Fori(0, H // 2 - 1) as j:
                    for par in range(2):
                        head_step(2 * j + par, par, l * H + 2 * j + par)
                for par in range(2):
                    head_step(H - 2 + par, par, l * H + H - 2 + par, prep=(par == 0))

                copies16(4 * l + 1, lambda k: (yaT[:, k, :], 1.0))
                copies16(4 * l + 2, lambda k: (ybT[:, k, :], 1.0))
                in_merge = Steps(act, "act_merge_steps")
                in_merge.start(l * 16)
                for g in range(2):
                    for t in range(NT):
                        act.wait_ge(s("gates_low"), 4 * l + 2 * g + t + 1)
                        for m in range(2):
                            in_merge.do(act.activation(mg[4 * t + m], mg[4 * t + m], ACT.Exp, scale=-1.0))
                        in_merge.fence()
                        for m in range(2):
                            in_merge.do(act.activation(mg[4 * t + m], mg[4 * t + m], ACT.Ln, bias=one1))
                        in_merge.fence()
                        for m in range(2):
                            last = act.activation(mg[4 * t + m], mg[4 * t + m], ACT.Exp, scale=-1.0)
                        last.then_inc(s("merge_exp"), 1)
                in_merge.ended(16)
                copies16(4 * l + 3, lambda k: (mT[:, k, :], 1.0))
                for t in range(NT):
                    act.wait_ge(s("x_added"), 4 * l + 2 * (t + 1))
                    square_sum(t)
                in_layer.ended(6)

            me.start(0)
            def bias_copies(hs):
                for h in hs:
                    act.wait_ge(s("bias_ps"), h + 1)
                    act.activation(view(h * NB, NB), pb[4 + h % 4][:, :], ACT.Copy).then_inc(s("bias_rows"), 1)

            in_layer.start(NT + 6 * DEPTH)
            in_layer.fence()
            ss_rstd(me)
            bias_copies(range(4))
            act.wait_ge(s("normed"), 2 * DEPTH + 2)
            row_rstd(me, xn2)
            bias_copies(range(4, H))
            copies16(8, lambda k: (hT[:, k, :], vec[:, V_MIX + k:V_MIX + k + 1]))
            act.wait_ge(s("bias_stored"), 16)
            for u in range(0, 8, 2):
                act.wait_ge(s("z2_ps"), u + 1)
                act.activation(z2[:, u // 2, 0, :], pb[4 + u % 4][:, :], ACT.Copy).then_inc(s("z2_sb_act"), 1)
            await_once(act, "pool_ps")
            act.activation(pooledT[:, 0:NB], pb[0][:, :], ACT.Copy)
            act.activation(pooledT[:, NB:2 * NB], pb[1][:, :], ACT.Copy).then_inc(once("pooled"), 1)
            await_once(act, "pmix_ps")
            for g in range(4):
                last = act.activation(mixT[:, g, :], pb[2 + g // 2][:, (g % 2) * S:(g % 2 + 1) * S], ACT.Copy,
                                      scale=vec[:, V_POOL + g:V_POOL + g + 1])
            last.then_inc(once("pmixed"), 1)
            def pair_qk(i):
                act.wait_ge(s("at_qkT_ps"), DEPTH * H + i + 1)
                if i > 0:
                    act.wait_ge(s("at_s_ps"), 2 * (DEPTH * H + i))
                act.activation(qkT2, pb[0][:, :], ACT.Copy).then_inc(s("at_qkT"), 1)

            pair_qk(0)
            for i in range(PAIRS):
                n = DEPTH * H + i
                if i < PAIRS - 1:
                    pair_qk(i + 1)
                act.wait_ge(s("at_max"), n + 1)
                for j in range(4):
                    p_j = p2[i % 2][:, j * S:(j + 1) * S]
                    last = act.activation(p_j, p_j, ACT.Exp, bias=nmx[:, j:j + 1])
                last.then_inc(s("at_exp"), 1)
                act.wait_ge(s("at_pT_ps"), n + 1)
                if i > 0:
                    act.wait_ge(s("at_o_ps"), n)
                for m in range(2):
                    last = act.activation(aT2[:, 4 * m:4 * m + 4, :], units(pb[3 + m][:, :]), ACT.Copy)
                last.then_inc(s("at_pT"), 1)
            await_once(act, "boutT_ps")
            act.activation(mixT[:, 4:6, :], pb[0][:, :].rearrange("p (k t) -> p k t", k=2), ACT.Copy)
            act.activation(mixT[:, 6:8, :], pb[1][:, :].rearrange("p (k t) -> p k t", k=2), ACT.Copy).then_inc(once("boutT"), 1)
            row_rstd(me, h2, "x_mixed")
            copies16(9, lambda k: (hT[:, k, :], 1.0))
            await_once(act, "top_neg")
            for t in range(NT):
                last = act.activation(gates[:, t, :], logits[:, t, :], ACT.Exp, bias=rt[:, t:t + 1])
            last.then_inc(once("gate_exp"), 1)
            await_once(act, "gatesT_ps")
            act.activation(gatesT[0:NE, :], pb[2][0:NE, 0:2 * P], ACT.Copy).then_inc(once("gatesT"), 1)
            act.wait_ge(s("gather_ps"), 1)
            act.activation(XT, pb[3][:, :].rearrange("p (k c) -> p k c", k=KC), ACT.Copy).then_inc(s("XT_sb"), 1)
            act.wait_ge(s("rounds_known"), 1)
            rounds = act.value_load(rounds_i[0:1, 0:1], min_val=1, max_val=ROUNDS)
            n_items = act.snap(rounds * NE)
            with act.Fori(0, n_items) as i:
                act.wait_ge(s("g_clamped"), i + 1)
                act.activation(sg, gm, ACT.Sigmoid, scale=1.702).then_inc(s("sig"), 1)
                act.wait_ge(s("gather_ps"), i + 2)
                act.activation(XT, pb[3][:, :].rearrange("p (k c) -> p k c", k=KC), ACT.Copy).then_inc(s("XT_sb"), 1)
                act.wait_ge(s("y_ps"), i + 1)
                act.activation(ysb, pb[2][:, :], ACT.Copy).then_inc(s("y_sb"), 1)
            act.preload_act_table_set("natural_log_exp_and_others")
            row_rstd(me, xn3, "x_moe")
            await_once(act, "pT_ps")
            act.activation(pT, pb[4][:, :].rearrange("p (k t) -> p k t", k=2), ACT.Copy).then_inc(once("pT_sb"), 1)
            copies16(10, lambda k: (hT[:, k, :], vec[:, V_PLE + k:V_PLE + k + 1]))
            def last_rstd(t):
                act.wait_ge(s("x_ple"), 2 * (t + 1))
                me.link(act.activation(xn3[:, t, :], x[:, t, :], ACT.Square, accum_out=ss[:, t:t + 1]))
                me.link(act.activation(rstd[:, t:t + 1], ss[:, t:t + 1], ACT.Ln, bias=eps, scale=1.0 / D))
                act.activation(rstd[:, t:t + 1], rstd[:, t:t + 1], ACT.Exp, scale=-0.5).then_inc(s("rstd"), 1)

            for u in range(4):
                act.wait_ge(s("ple_low"), u + 1)
                me.link(act.activation(pl[u], pl[u], ACT.Exp, scale=-1.0))
                me.link(act.activation(pl[u], pl[u], ACT.Ln, bias=one1))
                act.activation(pl[u], pl[u], ACT.Exp, scale=-1.0).then_inc(s("ple_exp"), 1)
                if u == 2:
                    last_rstd(0)
            last_rstd(1)

        @block.vector
        def _(dve):
            me = Steps(dve, "dve_steps")
            in_layer = Steps(dve, "dve_layer_steps")
            in_gdn = Steps(dve, "dve_gdn_steps")
            in_diff = Steps(dve, "dve_diff_steps")
            in_dil = Steps(dve, "dve_dil_steps")
            in_moe = Steps(dve, "dve_moe_steps")

            def copies16(n, scale):
                for kp in (1, 3):
                    dve.wait_ge(s("tr_ps"), 4 * n + kp + 1)
                    for kk in range(2):
                        dst, sc = scale(2 * kp + kk)
                        src = pb[kp][:, kk * S:(kk + 1) * S]
                        last = dve.tensor_copy(dst, src) if sc is None else dve.tensor_scalar(dst, src, sc, None, ALU.mult)
                    last.then_inc(s("tr_dve"), 1)

            def normed(dst, n, row=None):
                dve.wait_ge(s("rstd"), n + 1)
                for t in range(NT):
                    if row is None:
                        ins = dve.tensor_scalar(dst[:, t, :], x[:, t, :], rstd[:, t:t + 1], None, ALU.mult)
                    else:
                        ins = dve.scalar_tensor_tensor(dst[:, t, :], x[:, t, :], rstd[:, t:t + 1], row, ALU.mult, ALU.mult)
                    ins.then_inc(s("normed"), 1)

            me.do(dve.memset(small[:, :], EPS))
            me.do(dve.memset(ones[:, :], 1.0))
            me.do(dve.memset(rel[32:33, :], 1.0))
            me.fence()
            me.link(dve.memset(one1, 1.0))
            dve.wait_ge(s("const_in"), 16 * NCONST)
            me.link(dve.tensor_copy(cosb[:, :, 0:1], pos_i[:, :].unsqueeze(2)))
            dve.tensor_scalar(ones[:, 0:1], ones[:, 0:1], 1.0, None, ALU.mult).then_inc(once("ones_set"), 1)
            ang, turn = wk(5)[:, 0:16].rearrange("p (t c) -> p t c", t=NT), wk(5)[:, 16:32].rearrange("p (t c) -> p t c", t=NT)
            me.link(dve.tensor_tensor(ang, cosb[:, :, 0:1].broadcast_to([P, NT, ROPE_HALF]),
                                      inv_freq.unsqueeze(1).broadcast_to([P, NT, ROPE_HALF]), ALU.mult))
            MAGIC = 1.5 * 2.0 ** 23
            TWO_PI = (6.28125, 0.00193500518798828125, 2 * math.pi - 6.28125 - 0.00193500518798828125)
            for dst, quarter in ((sinb, 0.0), (cosb, 0.25)):
                me.link(dve.tensor_scalar(turn, ang, 1.0 / (2 * math.pi), quarter, ALU.mult, ALU.add))
                me.link(dve.tensor_scalar(turn, turn, MAGIC, None, ALU.add))
                me.link(dve.tensor_scalar(turn, turn, MAGIC, None, ALU.subtract))
                me.link(dve.scalar_tensor_tensor(dst[:, :, :], turn, -TWO_PI[0], ang, ALU.mult, ALU.add))
                me.link(dve.scalar_tensor_tensor(dst[:, :, :], turn, -TWO_PI[1], dst[:, :, :], ALU.mult, ALU.add))
                me.link(dve.scalar_tensor_tensor(dst[:, :, :], turn, -TWO_PI[2], dst[:, :, :], ALU.mult, ALU.add))
                if quarter:
                    me.link(dve.tensor_scalar(dst[:, :, :], dst[:, :, :], math.pi / 2, None, ALU.add))
                me.link(dve.tensor_scalar(dst[:, :, :], dst[:, :, :], 3.141592, -3.141592, ALU.min, ALU.max))
            dve.tensor_scalar(sinb[:, :, :], sinb[:, :, :], 1.0, None, ALU.mult).then_inc(once("angles"), 1)
            lam_p = wk(6)
            for l in range(DEPTH):
                lp = rows[:, l * R_N + R_LAM:l * R_N + R_LAM + 256].rearrange("p (a b c) -> p a b c", a=2, b=2)
                me.link(dve.tensor_tensor(lam_p[:, 0:128].rearrange("p (a c) -> p a c", a=2), lp[:, :, 0, :], lp[:, :, 1, :], ALU.mult))
                me.link(dve.tensor_reduce(lam_s[:, 2 * l:2 * l + 2], lam_p[:, 0:128].rearrange("p (a c) -> p a c", a=2), AXX, ALU.add))
                sub = rows[:, l * R_N + R_SUB:l * R_N + R_SUB + P]
                me.link(dve.tensor_scalar(sub, sub, one_lam[:, l:l + 1], None, ALU.mult))
            dve.tensor_scalar(lam_s, lam_s, 1.0, None, ALU.mult).then_inc(once("lam_sums"), 1)
            await_once(dve, "lam_exp")
            lam2 = lam_s.rearrange("p (l a) -> p l a", a=2)
            me.link(dve.tensor_tensor(neg_lam.unsqueeze(2), lam2[:, :, 1:2], lam2[:, :, 0:1], ALU.subtract))
            me.link(dve.tensor_tensor(neg_lam, neg_lam, lam_init, ALU.subtract))
            await_once(dve, "sincos")
            await_once(dve, "vec_sb")
            me.link(dve.memset(conv_b[:, :, 0:PAD], 0.0))
            me.link(dve.memset(conv_b[:, :, PAD + S:XC], 0.0))

            with dve.Fori(0, DEPTH) as l:
                in_layer.start(l * (LAYER_STEPS + MERGE_STEPS))
                normed(kb, l)
                copies16(4 * l, lambda k: (hT[:, k, :], vec[:, ds(l * KC + V_NORM + k, 1)]))
                in_layer.do(dve.memset(conv_b[:, 0:H, 0:PAD], 0.0))
                in_layer.do(dve.memset(conv_b[:, 0:H, PAD + S:XC], 0.0))
                for u in range(1, 12, 2):
                    dve.wait_ge(s("qkv_ps"), l * 12 + u + 1)
                    dve.tensor_copy(conv_b[:, 2 * u:2 * u + 2, PAD:PAD + S],
                                    pb[u % 4][:, :].rearrange("p (b c) -> p b c", b=2)).then_inc(s("qkv_sb_dve"), 1)
                dve.wait_ge(s("ab_sb"), l + 1)
                z = ab[:, 2:4]
                dt_row = rows[:, ds(l * R_N + R_DT, 16)].rearrange("p (d h) -> p d h", d=2).unsqueeze(2).broadcast_to([P, 2, NT, H])
                in_layer.link(dve.tensor_tensor(z, z, dt_row, ALU.add))
                in_layer.do(dve.tensor_scalar(ab_t[:, 0], z, 0.0, None, ALU.max))
                in_layer.link(dve.tensor_scalar(ab_t[:, 2], z, -1.0, None, ALU.mult))
                dve.tensor_tensor(ab_t[:, 1], z, ab_t[:, 2], ALU.min).then_inc(s("ab_neg"), 1)
                dve.wait_ge(s("ab_exp"), l + 1)
                in_layer.do(dve.tensor_scalar(ab[:, 0:2], ab[:, 0:2], 1.0, None, ALU.add))
                in_layer.link(dve.tensor_tensor(ab_t[:, 0], ab_t[:, 0], ab_t[:, 1], ALU.add))
                in_layer.do(dve.reciprocal(ab[:, 0:2], ab[:, 0:2]))
                in_layer.link(dve.tensor_scalar(ab_t[:, 0], ab_t[:, 0], -1.0, None, ALU.mult))
                dve.tensor_tensor(z, ab_t[:, 0], ea[:, :, :].unsqueeze(2).broadcast_to([P, 2, NT, H]), ALU.mult).then_inc(s("g_sb"), 1)
                def rotate(t4):
                    v4 = t4.rearrange("p t (g c) -> p t g c", g=16)
                    x1, x2 = v4[:, :, :, 0:ROPE_HALF], v4[:, :, :, ROPE_HALF:2 * ROPE_HALF]
                    for t in range(NT):
                        cs = cosb[:, t:t + 1, :].broadcast_to([P, 16, ROPE_HALF])
                        sn = sinb[:, t:t + 1, :].broadcast_to([P, 16, ROPE_HALF])
                        in_layer.do(dve.tensor_tensor(rp[0][:, t], x1[:, t], cs, ALU.mult))
                        in_layer.do(dve.tensor_tensor(rp[1][:, t], x2[:, t], sn, ALU.mult))
                        in_layer.do(dve.tensor_tensor(rp[2][:, t], x2[:, t], cs, ALU.mult))
                        in_layer.link(dve.tensor_tensor(rp[3][:, t], x1[:, t], sn, ALU.mult))
                        in_layer.do(dve.tensor_tensor(x1[:, t], rp[0][:, t], rp[1][:, t], ALU.subtract))
                        ins = dve.tensor_tensor(x2[:, t], rp[2][:, t], rp[3][:, t], ALU.add)
                        if t == 0:
                            in_layer.do(ins)
                    ins.then_inc(s("roped"), 1)

                def conv_taps(h, js):
                    for j in js:
                        for m in range(3):
                            src = conv_in[:, ds(h * XC + (m * H * XC + j), S)]
                            w = conv_wT[:, ds(l * (TAPS * CB) + h + (j * CB + m * H), 1)]
                            dst = c3[:, m * S:(m + 1) * S]
                            if j == 0:
                                in_gdn.do(dve.tensor_scalar(dst, src, w, None, ALU.mult))
                            else:
                                in_gdn.do(dve.scalar_tensor_tensor(dst, src, w, dst, ALU.mult, ALU.add))
                        in_gdn.fence()

                def conv_end(n):
                    dve.tensor_scalar(e3, c3, -40.0, None, ALU.max).then_inc(s("gd_conv"), 1)

                def decay_diff(h, n, par):
                    dve.wait_ge(s("gd_rows_ps"), n + 1)
                    for u in range(4):
                        ins = dve.tensor_scalar(Es[par][:, u, :], pb[7][:, u * P:(u + 1) * P], gcum[:, ds(h + u * H, 1)], 0.0,
                                                ALU.subtract, ALU.min)
                    ins.then_inc(s("gd_diff"), 1)

                def beta_decay(n, par):
                    dve.wait_ge(s("gd_em"), n + 1)
                    dve.wait_ge(s("gd_brow_ps"), n + 1)
                    dve.tensor_tensor(LTs[par], Es[par], units(pb[7][:, :]), ALU.mult).then_inc(s("gd_bm"), 1)

                def silu_end(n):
                    dve.wait_ge(s("gd_e"), n + 1)
                    dve.tensor_tensor(c3, c3, e3, ALU.mult).then_inc(s("gd_silu"), 1)

                def unit_qk(n, par):
                    dve.wait_ge(s("gd_rn"), n + 1)
                    dve.scalar_tensor_tensor(q2[par], c3[:, 0:S], P ** -0.5, e3[:, 0:S], ALU.mult, ALU.mult).then_inc(s("gd_qkn"), 1)
                    dve.tensor_tensor(kTh, kTh, e3[:, S:2 * S], ALU.mult).then_inc(s("gd_qkn"), 1)

                def gram_decay(n, par):
                    kk4 = pb[7][:, :].rearrange("p (s t c) -> p s t c", s=2, t=NT)
                    dve.wait_ge(s("gd_kk_ps"), n + 1)
                    L4 = LTs[par].rearrange("p (d t) c -> p d t c", d=2)
                    dve.tensor_tensor(L4, L4, kk4[:, 0:1].broadcast_to([P, 2, NT, P]), ALU.mult).then_inc(s("gd_lt"), 1)
                    E4 = Es[par].rearrange("p (d t) c -> p d t c", d=2)
                    dve.tensor_tensor(E4, E4, kk4[:, 1:2].broadcast_to([P, 2, NT, P]), ALU.mult)

                ab_f = ab[:, :, :, :].rearrange("p c t h -> p (c t h)")

                def beta_kv(h, n):
                    dve.wait_ge(s("gd_kv"), n + 1)
                    dve.tensor_tensor(vbeta.rearrange("p (d t) c -> p d t c", d=2),
                                      kv.rearrange("p (s t) c -> p s t c", s=2)[:, 1:2].broadcast_to([P, 2, NT, P]),
                                      bb.rearrange("p (d t) c -> p d t c", d=2), ALU.mult).then_inc(s("gd_vb"), 1)
                    for d in range(2):
                        dve.tensor_scalar(kbg[:, d, :], kv[:, 1 - d, :], ab_f[:, ds(h + (1 + d) * H, 1)],
                                          eg[:, ds(h + (1 + d) * H, 1)], ALU.mult, ALU.mult).then_inc(s("gd_vb"), 1)

                def k_end(h):
                    for d in range(2):
                        dve.tensor_scalar(kend[:, d, :], kv[:, d, :], gend[:, ds(h + 3 * d * H, 1)], None, ALU.mult).then_inc(s("gd_vb"), 1)

                def first_level(n):
                    dve.wait_ge(s("gd_lvl"), n * LEVELS + 1)
                    dve.tensor_tensor(U, ident.unsqueeze(1).broadcast_to([P, 4, P]), Lv[0], ALU.subtract).then_inc(s("gd_u"), 1)

                def level(n, v):
                    if v < LEVELS - 1:
                        dve.wait_ge(s("gd_tv_ps"), n * (LEVELS - 2) + v)
                        for d in range(2):
                            ins = dve.tensor_tensor(half(T_f, d, v, 0), half(T_f, d, v, 0), half(pb[1], d, v, 0), ALU.subtract)
                        ins.then_inc(s("gd_t"), 1)
                    dve.wait_ge(s("gd_vu_ps"), n * (LEVELS - 1) + v)
                    for d in range(2):
                        ins = dve.tensor_tensor(half(U_f, d, v, 1), half(U_f, d, v, 1), half(pb[2], d, v, 1), ALU.subtract)
                    ins.then_inc(s("gd_u"), 1)

                def gate(us, n):
                    dve.wait_ge(s("gd_y"), n)
                    dve.wait_ge(s("z_sb"), n)
                    dve.wait_ge(s("at_y"), n)
                    for u in us:
                        g, t = u // 2 % 2, u % 2
                        if u < 4:
                            y = ya[:, 4 * g:4 * g + 4, t, :].rearrange("p (s a) c -> p s a c", s=2)
                        else:
                            y = qb[:, t, g * NB:(g + 1) * NB].rearrange("p (s a c) -> p s a c", s=2, a=2)
                        dve.tensor_tensor(y, y, sz[:, u], ALU.mult).then_inc(s("z_gated"), 1)

                def head_step(h, par, n, prep=True):
                    in_diff.start(n * DIFF_STEPS)
                    if prep:
                        in_gdn.start((n + 1) * GDN_STEPS)
                        conv_taps(h + 1, (0, 1,))
                    for v in range(2, LEVELS):
                        level(n, v)
                        if prep:
                            if v == 2:
                                decay_diff(h + 1, n + 1, 1 - par)
                                conv_taps(h + 1, (2, 3, 4,))
                                conv_end(n + 1)
                                in_gdn.ended(GDN_STEPS)
                            elif v == 4:
                                beta_decay(n + 1, 1 - par)
                                silu_end(n + 1)
                        elif v == 3:
                            gate((0, 1, 4, 5), n)
                        if v == 4:
                            for m in range(2):
                                dve.wait_ge(s("at_s_ps"), 2 * n + m + 1)
                                in_diff.do(dve.tensor_reduce(mx[:, 2 * m:2 * m + 2], pb[5 + m][:, :].rearrange("p (t k) -> p t k", t=NT),
                                                             AXX, ALU.max))
                            in_diff.fence()
                            dve.tensor_scalar(nmx, mx, -DIFF_SCALE, None, ALU.mult).then_inc(s("at_max"), 1)
                        elif v == 5:
                            dve.wait_ge(s("at_exp"), n + 1)
                            in_diff.link(dve.reciprocal(rsum, ssum))
                            in_diff.link(dve.tensor_scalar(rsum[:, 2:4], rsum[:, 2:4], neg_lam[:, ds(l, 1)], None, ALU.mult))
                            for t in range(NT):
                                in_diff.do(dve.tensor_scalar(pm[:, 0, t, :], pm[:, 0, t, :], rsum[:, t:t + 1], None, ALU.mult))
                            in_diff.fence()
                            for t in range(NT):
                                ins = dve.scalar_tensor_tensor(pm[:, 0, t, :], pm[:, 1, t, :], rsum[:, 2 + t:3 + t], pm[:, 0, t, :], ALU.mult, ALU.add)
                            ins.then_inc(s("at_p"), 1)
                    if prep:
                        unit_qk(n + 1, 1 - par)
                    if prep:
                        dve.wait_ge(s("gd_uw_ps"), n + 1)
                        beta_kv(h + 1, n + 1)
                        gram_decay(n + 1, 1 - par)
                    dve.wait_ge(s("gd_ws_ps"), n + 1)
                    dve.tensor_tensor(us[:, 1:3, :], us[:, 1:3, :], units(pb[1][:, 0:2 * P]), ALU.subtract).then_inc(s("gd_vnew"), 1)
                    if prep:
                        dve.wait_ge(s("gd_s_ps"), n + 1)
                        k_end(h + 1)
                    dve.wait_ge(s("z_ps"), n + 1)
                    dve.tensor_scalar(mz, pb[3][:, :], -40.0, None, ALU.max).then_inc(s("z_low"), 1)
                    dve.wait_ge(s("gd_o_ps"), n + 1)
                    dve.wait_ge(s("gd_qs"), n + 1)
                    for t in range(NT):
                        ins = dve.tensor_tensor(oh[:, t, :], pb[0][:, t * P:(t + 1) * P], qs[:, 1 - t, :], ALU.add)
                    ins.then_inc(s("gd_osum"), 1)
                    if prep:
                        first_level(n + 1)
                    dve.wait_ge(s("gd_rs"), n + 1)
                    for t in range(NT):
                        ins = dve.scalar_tensor_tensor(conv_in[:, ds(h * XC + (PAD + t * P), P)], oh[:, t, :], rs_o[:, t:t + 1],
                                                       rows[:, ds(l * R_N + R_GDN, P)], ALU.mult, ALU.mult)
                    ins.then_inc(s("gd_y"), 1)
                    if prep:
                        level(n + 1, 1)
                    dve.wait_ge(s("z_exp"), n + 1)
                    for m in range(2):
                        ins = dve.tensor_tensor(conv_in[:, ds(h * XC + ((m + 1) * H * XC + PAD), S)], mz[:, m * S:(m + 1) * S],
                                                pb[3][:, m * S:(m + 1) * S], ALU.mult)
                    ins.then_inc(s("z_sb"), 1)
                    dve.wait_ge(s("at_rs"), n + 1)
                    for t in range(NT):
                        ins = dve.scalar_tensor_tensor(qb[:, t, ds(h * P, P)], pb[5][:, t * P:(t + 1) * P], rs_d[:, t:t + 1],
                                                       rows[:, ds(l * R_N + R_SUB, P)], ALU.mult, ALU.mult)
                    ins.then_inc(s("at_y"), 1)
                    in_diff.ended(DIFF_STEPS)

                n0 = l * H
                for u in range(1, 12, 2):
                    dve.wait_ge(s("seg_ps"), l * 12 + u + 1)
                    dst = (qb, kb, vb)[u // 4]
                    dve.tensor_copy(dst[:, 1, (u // 2 % 2) * NB:(u // 2 % 2 + 1) * NB], pb[u % 4][:, :]).then_inc(s("seg_sb_dve"), 1)
                    if u == 1:
                        dve.wait_ge(s("gcum_ps"), l + 1)
                        in_layer.link(dve.tensor_copy(gcum[:, :], pb[5][:, 0:32]))
                        dve.tensor_tensor(gend[:, :], pb[5][:, 32:64], gcum[:, :], ALU.subtract).then_inc(s("gcum_cp"), 1)
                        dve.wait_ge(s("qkv_sb_act"), (l + 1) * 6)
                        dve.wait_ge(s("qkv_sb_dve"), (l + 1) * 6)
                        in_gdn.start(n0 * GDN_STEPS)
                        conv_taps(0, range(TAPS))
                        conv_end(n0)
                        in_gdn.ended(GDN_STEPS)
                    elif u == 3:
                        decay_diff(0, n0, 0)
                    elif u == 5:
                        beta_decay(n0, 0)
                        silu_end(n0)
                    elif u == 7:
                        dve.wait_ge(s("seg_sb_act"), l * 6 + 2)
                        dve.wait_ge(s("seg_sb_dve"), l * 6 + 2)
                        rotate(qb)
                        dve.wait_ge(s("gd_silu"), n0 + 1)
                        unit_qk(n0, 0)
                    elif u == 9:
                        dve.wait_ge(s("seg_sb_act"), l * 6 + 4)
                        dve.wait_ge(s("seg_sb_dve"), l * 6 + 4)
                        rotate(kb)
                        dve.wait_ge(s("gcum_sb"), l + 1)
                        beta_kv(0, n0)
                        k_end(0)
                in_layer.ended(LAYER_STEPS)
                gram_decay(n0, 0)
                first_level(n0)
                level(n0, 1)
                with dve.Fori(0, H // 2 - 1) as j:
                    for par in range(2):
                        head_step(2 * j + par, par, l * H + 2 * j + par)
                for par in range(2):
                    head_step(H - 2 + par, par, l * H + H - 2 + par, prep=(par == 0))

                gate((2, 3, 6, 7), (l + 1) * H)
                copies16(4 * l + 1, lambda k: (yaT[:, k, :], None))
                copies16(4 * l + 2, lambda k: (ybT[:, k, :], None))
                in_layer.start(l * (LAYER_STEPS + MERGE_STEPS) + LAYER_STEPS)
                for g in range(2):
                    for t in range(NT):
                        dve.wait_ge(s(f"merge_ps{t}"), l * 8 + 4 * g + 3)
                        if g == 1:
                            dve.wait_ge(s("merged"), 4 * l + t + 1)
                        dve.tensor_scalar(mg[4 * t], pb[4 * t][:, :], -40.0, None, ALU.max)
                        dve.tensor_scalar(mg[4 * t + 1], pb[4 * t + 2][:, :], -40.0, None, ALU.max).then_inc(s("gates_low"), 1)
                        dve.wait_ge(s(f"merge_ps{t}"), l * 8 + 4 * g + 4)
                        dve.wait_ge(s("merge_exp"), 4 * l + 2 * g + t + 1)
                        for m in range(2):
                            in_layer.do(dve.tensor_tensor(mg[4 * t + m], mg[4 * t + m], pb[4 * t + 1 + 2 * m][:, :], ALU.mult))
                        in_layer.fence()
                        dve.tensor_tensor(qb[:, t, g * NB:(g + 1) * NB], mg[4 * t], mg[4 * t + 1], ALU.add).then_inc(s("merged"), 1)
                copies16(4 * l + 3, lambda k: (mT[:, k, :], None))
                for u in range(4):
                    dve.wait_ge(s("xo_ps"), 4 * l + u + 1)
                    xs = x[:, u // 2, (u % 2) * NB:(u % 2 + 1) * NB]
                    dve.tensor_tensor(xs, xs, pb[4 + u][:, :], ALU.add).then_inc(s("x_added"), 1)
                dve.wait_ge(s("x_added"), 4 * (l + 1))
                in_layer.ended(MERGE_STEPS)

            dve.wait_ge(s("fnorm_in"), 16)
            normed(x, 2, grow_l)
            dve.wait_ge(s("normed"), 2 * DEPTH + 2)
            normed(xn2, 3)
            copies16(8, lambda k: (hT[:, k, :], vec[:, V_MIX + k:V_MIX + k + 1]))
            dve.wait_ge(s("bias_stored"), 16)
            for u in range(1, 8, 2):
                dve.wait_ge(s("z2_ps"), u + 1)
                dve.tensor_copy(z2[:, u // 2, 1, :], pb[4 + u % 4][:, :]).then_inc(s("z2_sb_dve"), 1)
            def pair_bias(i):
                n, p = DEPTH * H + i, p2[i % 2]
                if i >= 2:
                    dve.wait_ge(s("at_pT_ps"), n - 1)
                for m in range(2):
                    dve.wait_ge(s("at_s_ps"), 2 * n + m + 1)
                    in_dil.do(dve.scalar_tensor_tensor(p[:, m * NB:(m + 1) * NB], pb[1 + m][:, :], 0.125,
                                                       bias2[:, (2 * i + m) * NB:(2 * i + m + 1) * NB], ALU.mult, ALU.add))
                in_dil.fence()
                in_dil.link(dve.tensor_reduce(mx, p.rearrange("p (j k) -> p j k", j=4), AXX, ALU.max))
                dve.tensor_scalar(nmx, mx, -1.0, None, ALU.mult).then_inc(s("at_max"), 1)

            in_dil.start(0)
            pair_bias(0)
            for i in range(PAIRS):
                n, p = DEPTH * H + i, p2[i % 2]
                dve.wait_ge(s("at_exp"), n + 1)
                for m in range(2):
                    ins = dve.tensor_tensor(p[:, m * NB:(m + 1) * NB], p[:, m * NB:(m + 1) * NB], count, ALU.mult)
                ins.then_inc(s("at_p"), 1)
                if i < PAIRS - 1:
                    pair_bias(i + 1)
                dve.wait_ge(s("at_p"), n + 1)
                in_dil.link(dve.tensor_reduce(ssum, p.rearrange("p (j k) -> p j k", j=4), AXX, ALU.add))
                in_dil.link(dve.reciprocal(rsum, ssum))
                dve.wait_ge(s("at_o_ps"), n + 1)
                for t in range(NT):
                    for m in range(2):
                        ins = dve.tensor_scalar(bout[:, t * 512 + i * P + m * 64:t * 512 + i * P + (m + 1) * 64],
                                                pb[5][:, t * P + m * 64:t * P + (m + 1) * 64],
                                                rsum[:, 2 * m + t:2 * m + t + 1], None, ALU.mult)
                ins.then_inc(s("at_y"), 1)
            for u in range(4):
                dve.wait_ge(s("xm_ps"), u + 1)
                xs = x[:, u // 2, (u % 2) * NB:(u % 2 + 1) * NB]
                dve.tensor_tensor(xs, xs, pb[4 + u][:, :], ALU.add).then_inc(s("x_mixed"), 1)
            dve.memset(bpad, 0.0).then_inc(s("bpad_zero"), 1)
            dve.memset(e0, 0.0).then_inc(s("bpad_zero"), 1)
            dve.wait_ge(s("bpad_zero"), 2)
            dve.memset(e0[0:1, :], 1.0).then_inc(s("bpad_zero"), 1)
            dve.wait_ge(s("x_mixed"), 4)
            dve.wait_ge(s("g_ffn_in"), 16)
            normed(h2, 4, grow)
            copies16(9, lambda k: (hT[:, k, :], None))
            dve.memset(CT, 0.0)
            dve.wait_ge(s("normed"), 2 * DEPTH + 6)
            dve.memset(ysb, 0.0).then_inc(s("y_sb"), 1)
            dve.wait_ge(s("ffn_in"), 16 * 3)
            r2 = Steps(dve, "dve_router_steps")
            await_once(dve, "logits_ps")
            r2.link(dve.tensor_tensor(logits, pb[0][:, 0:2 * NE].rearrange("p (t e) -> p t e", t=NT),
                                      brow.unsqueeze(1).broadcast_to([P, NT, NE]), ALU.add))
            for t in range(NT):
                r2.do(dve.max(top8[:, t, :], logits[:, t, :]))
            r2.fence()
            dve.tensor_scalar(rt[:, 0:2].unsqueeze(2), top8[:, :, 0:1], -1.0, None, ALU.mult).then_inc(once("top_neg"), 1)
            for t in range(NT):
                r2.do(dve.tensor_scalar(m_gt[:, t, :], logits[:, t, :], top8[:, t, 3:4], None, ALU.is_gt))
                r2.do(dve.tensor_scalar(m_eq[:, t, :], logits[:, t, :], top8[:, t, 3:4], None, ALU.is_equal))
            r2.fence()
            r2.link(dve.tensor_reduce(rt[:, 2:4], m_gt, AXX, ALU.add))
            r2.link(dve.tensor_scalar(rt[:, 4:6], rt[:, 2:4], -1.0, float(TOPK), ALU.mult, ALU.add))
            src, dst = m_eq, pre0
            for sh in (1, 2, 4, 8, 16):
                r2.do(dve.tensor_copy(dst[:, :, 0:sh], src[:, :, 0:sh]))
                r2.link(dve.tensor_tensor(dst[:, :, sh:NE], src[:, :, sh:NE], src[:, :, 0:NE - sh], ALU.add))
                src, dst = dst, (pre1 if dst is pre0 else pre0)
            for t in range(NT):
                r2.do(dve.scalar_tensor_tensor(msk[:, t, :], src[:, t, :], rt[:, 4 + t:5 + t], m_eq[:, t, :], ALU.is_le, ALU.mult))
            r2.fence()
            dve.tensor_tensor(msk, msk, m_gt, ALU.add).then_inc(once("mask_sb"), 1)
            await_once(dve, "mask_sb")
            await_once(dve, "gate_exp")
            r2.link(dve.tensor_tensor(gates, gates, msk, ALU.mult))
            r2.link(dve.tensor_reduce(rt[:, 6:8], gates, AXX, ALU.add))
            r2.link(dve.reciprocal(rt[:, 8:10], rt[:, 6:8]))
            for t in range(NT):
                ins = dve.tensor_scalar(gates[:, t, :], gates[:, t, :], rt[:, 8 + t:9 + t], None, ALU.mult)
            ins.then_inc(once("gates_sb"), 1)
            await_once(dve, "rank_ps")
            r2.link(dve.scalar_tensor_tensor(ranks, pb[1][:, 0:2 * NE].rearrange("p (t e) -> p t e", t=NT), 1.0, msk, ALU.add, ALU.mult))
            await_once(dve, "gates_sb")
            for r in range(ROUNDS + 1):
                r2.do(dve.tensor_scalar(rkx[:, :, r * NE:(r + 1) * NE], ranks, -1.0 - CAP * r, None, ALU.add))
                r2.do(dve.tensor_copy(gx[:, :, r * NE:(r + 1) * NE], gates))
            r2.link(dve.tensor_reduce(rt[:, 10:11], pb[1][:, 2 * NE:3 * NE], AXX, ALU.max))
            r2.link(dve.tensor_scalar(rt[:, 11:12], rt[:, 10:11], float(CAP), 1.0, ALU.is_gt, ALU.add))
            for r in range(2, ROUNDS):
                r2.link(dve.scalar_tensor_tensor(rt[:, 11:12], rt[:, 10:11], float(CAP * r), rt[:, 11:12], ALU.is_gt, ALU.add))
            for t in range(NT):
                ins = dve.tensor_scalar(P1[:, t, :], iota[:, 0:CAP], rkx[:, t, 0:1], None, ALU.is_equal)
            ins.then_inc(s("onehot"), 1)
            dve.tensor_copy(rounds_i[:, :], rt[:, 11:12]).then_inc(s("rounds_known"), 1)
            dve.wait_ge(s("rounds_known"), 1)
            rounds = dve.value_load(rounds_i[0:1, 0:1], min_val=1, max_val=ROUNDS)
            n_items = dve.snap(rounds * NE)
            NX = (ROUNDS + 1) * NE
            with dve.Fori(0, n_items) as i:
                in_moe.start(i * 2)
                dve.wait_ge(s("gather_ps"), i + 1)
                for t in range(NT):
                    ins = dve.tensor_scalar(Pg[:, t, :], iota, rkx_f[:, ds(i + t * NX, 1)], gx_f[:, ds(i + t * NX, 1)], ALU.is_equal, ALU.mult)
                ins.then_inc(s("onehot_g"), 1)
                for t in range(NT):
                    ins = dve.tensor_scalar(P1[:, t, :], iota[:, 0:CAP], rkx_f[:, ds(i + (t * NX + 1), 1)], None, ALU.is_equal)
                ins.then_inc(s("onehot"), 1)
                dve.wait_ge(s("gate_up_ps"), i + 1)
                dve.tensor_scalar(gm, pb[0][:, :], 7.0, None, ALU.min).then_inc(s("g_clamped"), 1)
                in_moe.link(dve.tensor_scalar(uc, pb[1][:, :], 7.0, -7.0, ALU.min, ALU.max))
                dve.wait_ge(s("g_clamped"), i + 1)
                in_moe.link(dve.scalar_tensor_tensor(uc, uc, 1.0, gm, ALU.add, ALU.mult))
                dve.wait_ge(s("sig"), i + 1)
                dve.tensor_tensor(gm, uc, sg, ALU.mult).then_inc(s("act"), 1)
                dve.wait_ge(s("CT_ps"), i + 1)
                dve.tensor_copy(CT, pb[2][:, 0:2 * P].rearrange("p (t c) -> p t c", t=NT)).then_inc(s("CT_sb"), 1)
                dve.wait_ge(s("actT_ps"), i + 1)
                dve.tensor_copy(actT, pb[3][:, :].rearrange("p (c h t) -> p c h t", c=4, h=2)).then_inc(s("actT_sb"), 1)
                in_moe.ended(2)
            dve.wait_ge(s("combined"), n_items + 1)
            for u in range(4):
                xs = x[:, u // 2, (u % 2) * NB:(u % 2 + 1) * NB]
                dve.tensor_tensor(xs, xs, pb[4 + u][:, :], ALU.add).then_inc(s("x_moe"), 1)
            dve.wait_ge(s("x_moe"), 4)
            normed(xn3, 5)
            copies16(10, lambda k: (hT[:, k, :], vec[:, V_PLE + k:V_PLE + k + 1]))
            r3 = Steps(dve, "dve_ple_steps")

            def gate_low(u):
                dve.wait_ge(s("ple_ps"), 2 * u + 1)
                dve.tensor_scalar(pl[u], pb[u // 2 + 2 * (u % 2)][:, :], -40.0, None, ALU.max).then_inc(s("ple_low"), 1)

            def last_norm(t):
                dve.wait_ge(s("x_ple"), 2 * (t + 1))
                dve.wait_ge(s("rstd"), 7 + t)
                dve.scalar_tensor_tensor(x[:, t, :], x[:, t, :], rstd[:, t:t + 1], grow_l, ALU.mult, ALU.mult).then_inc(s("y_final"), 1)

            dve.wait_ge(s("ple_in"), 16 * 2)
            gate_low(0)
            for u in range(4):
                t, g = divmod(u, 2)
                if u < 3:
                    gate_low(u + 1)
                dve.wait_ge(s("ple_exp"), u + 1)
                dve.wait_ge(s("ple_ps"), 2 * u + 2)
                r3.link(dve.tensor_tensor(pl[u], pl[u], pb[4 + t + 2 * g][:, :], ALU.mult))
                xs = x[:, t, g * NB:(g + 1) * NB]
                dve.tensor_tensor(xs, xs, pl[u], ALU.add).then_inc(s("x_ple"), 1)
                if u == 2:
                    last_norm(0)
            last_norm(1)

        @block.gpsimd
        def _(pool):
            with pool.Fori(0, DEPTH) as l:
                def rows_of(h):
                    ab_u = ab[:, :, :, :].rearrange("p c t h -> p (c t) h")
                    pool.tensor_tensor(gb, ab_u[:, 4:8, ds(h, 1)].broadcast_to([P, 4, P]), ones[:, :].unsqueeze(1).broadcast_to([P, 4, P]),
                                       ALU.mult).then_inc(s("gd_gb"), 1)
                    pool.tensor_copy(bb, ab_u[:, 0:4, ds(h, 1)].broadcast_to([P, 4, P])).then_inc(s("gd_gb"), 1)

                def within(n, par):
                    pool.wait_ge(s("gd_ex"), n + 1)
                    E4 = Es[par].rearrange("p (d t) c -> p d t c", d=2)
                    pool.tensor_tensor(E4, E4, tri.unsqueeze(2).broadcast_to([P, 2, NT, P]), ALU.mult).then_inc(s("gd_em"), 1)

                def attention_qk(h):
                    pool.tensor_tensor(qk_h[:, 0:2, :], qb[:, :, ds(h * P, P)], ones[:, :].unsqueeze(1).broadcast_to([P, NT, P]),
                                       ALU.mult).then_inc(s("at_qk"), 1)
                    pool.tensor_copy(qk_h[:, 2:4, :], kb[:, :, ds(h * P, P)]).then_inc(s("at_qk"), 1)

                def head_step(h, par, n, prep=True):
                    pool.wait_ge(s("gd_lt"), n + 1)
                    for v in range(LEVELS):
                        if v == 1:
                            pool.wait_ge(s("gd_u"), n * LEVELS + 1)
                        elif v > 2:
                            pool.wait_ge(s("gd_v_ps"), n * LEVELS + v - 1)
                        pool.tensor_tensor(Lv[v % 2].rearrange("p (d t) c -> p d t c", d=2),
                                           LTs[par].rearrange("p (d t) c -> p d t c", d=2),
                                           lvl[:, v].unsqueeze(2).broadcast_to([P, 2, NT, P]), ALU.mult).then_inc(s("gd_lvl"), 1)
                        if prep:
                            if v == 1:
                                rows_of(h + 1)
                            elif v == 4:
                                within(n + 1, 1 - par)
                                pool.wait_ge(s("at_qkT_ps"), n + 1)
                                attention_qk(h + 1)

                pool.wait_ge(s("gcum_sb"), l + 1)
                rows_of(0)
                within(l * H, 0)
                pool.wait_ge(s("roped"), 2 * (l + 1))
                attention_qk(0)
                with pool.Fori(0, H // 2 - 1) as j:
                    for par in range(2):
                        head_step(2 * j + par, par, l * H + 2 * j + par)
                for par in range(2):
                    head_step(H - 2 + par, par, l * H + H - 2 + par, prep=(par == 0))
                pool.wait_ge(s("at_y"), (l + 1) * H)


_INS = ["x", "positions", "norm_w", "w_in", "conv_w", "a_log", "dt_bias", "gdn_norm_w", "diff_lambda", "diff_subln_w",
        "w_pa", "w_pb", "w_out", "final_norm_w", "p_2", "g_mix_2", "w_in_2", "w_pool_2", "pool_scale_2", "rel_bias_2",
        "w_out_2", "g_ffn_2", "w_router_2", "b_router_2", "w_gate_up_2", "b_gate_up_2", "w_down_2", "b_down_2",
        "g_ple_2", "w_ple_gate_2", "w_ple_proj_2", "g_final_2"]


def kernel(**inputs):
    import concourse.bacc as bacc
    from concourse.bass_utils import run_bass_kernel_spmd

    nc = bacc.Bacc("TRN2", target_bir_lowering=False, num_devices=1)
    arrays = {name: np.ascontiguousarray(inputs[name]) for name in _INS}
    arrays.update(shape_constants())
    aps = {name: nc.dram_tensor(name + "_dram", v.shape, mybir.dt.from_np(v.dtype), kind="ExternalInput").ap()
           for name, v in arrays.items()}
    out = nc.dram_tensor("out_dram", (1, S, D), F32, kind="ExternalOutput").ap()
    block_kernel(nc, aps, out)
    r = run_bass_kernel_spmd(nc, [{name + "_dram": v for name, v in arrays.items()}], core_ids=[0])
    return np.asarray(r.results[0]["out_dram"])
```
